# Optimizing a Trainium2 kernel written in Bass

```python
import math
import jax, jax.numpy as jnp
from jax import lax
import numpy as np

D_MODEL = 1024
BATCH = 1
SEQ = 512
DEPTH = 2

N_MEM = 256
N_MIXERS = 2
N_A = (DEPTH + 1) // 2
N_B = DEPTH // 2
MIX_WIDTH = D_MODEL
MEM_HEADS = 4
MEM_HEAD_DIM = MIX_WIDTH // 4 // MEM_HEADS
MEM_WIDTH = MEM_HEADS * MEM_HEAD_DIM
MIXER_WIDTH = MIX_WIDTH - MEM_WIDTH

GLA_HEADS = 4
GLA_DV = MIXER_WIDTH // GLA_HEADS
GLA_DK = GLA_DV // 2
GLA_HK = GLA_HEADS * GLA_DK
GLA_GATE_RANK = 16
GLA_GATE_TAU = 16.0
GLA_CHUNK = 64
GLA_IN = 2 * GLA_HK + MIXER_WIDTH + GLA_GATE_RANK + MEM_WIDTH + MIX_WIDTH

DIL_GROUPS = ((128, 1), (512, 4), (2048, 16))
DIL_HEADS = 6
DIL_HEAD_DIM = MIXER_WIDTH // DIL_HEADS
DIL_IN = len(DIL_GROUPS) * 3 * MIXER_WIDTH + MEM_WIDTH + MIX_WIDTH

ROPE_THETA = 500000.0
ROPE_DIM = DIL_HEAD_DIM // 4
NORM_EPS = 1e-6


def rmsnorm(x, w):
    xf = x.astype(jnp.float32)
    y = xf * lax.rsqrt(jnp.mean(xf * xf, axis=-1, keepdims=True) + NORM_EPS)
    return (y * w.astype(jnp.float32)).astype(x.dtype)

def partial_rope(x, pos):
    half = ROPE_DIM // 2
    inv = ROPE_THETA ** (-jnp.arange(half, dtype=jnp.float32) / half)
    ang = pos.astype(jnp.float32)[:, None] * inv[None, :]
    cos = jnp.cos(ang)[None, :, None, :]
    sin = jnp.sin(ang)[None, :, None, :]
    xr = x[..., :ROPE_DIM].astype(jnp.float32)
    x1, x2 = xr[..., :half], xr[..., half:]
    rot = jnp.concatenate([x1 * cos - x2 * sin, x1 * sin + x2 * cos], axis=-1).astype(x.dtype)
    return jnp.concatenate([rot, x[..., ROPE_DIM:]], axis=-1)

def memory_attention(q, mem_n, w_memkv):
    B, T, _ = q.shape
    kv = mem_n @ w_memkv
    k, v = jnp.split(kv, 2, axis=-1)
    q = q.reshape(B, T, MEM_HEADS, MEM_HEAD_DIM)
    k = k.reshape(B, N_MEM, MEM_HEADS, MEM_HEAD_DIM)
    v = v.reshape(B, N_MEM, MEM_HEADS, MEM_HEAD_DIM)
    s = jnp.einsum('bthd,bnhd->bhtn', q, k).astype(jnp.float32) * (MEM_HEAD_DIM ** -0.5)
    p = jax.nn.softmax(s, axis=-1).astype(v.dtype)
    o = jnp.einsum('bhtn,bnhd->bthd', p, v)
    return o.reshape(B, T, MEM_WIDTH)

def gla_chunked(q, k, v, log_a):
    B, T, H, Dk = q.shape
    Dv = v.shape[-1]
    C = GLA_CHUNK
    N = T // C
    f32 = jnp.float32
    q = (q.astype(f32) * (Dk ** -0.5)).reshape(B, N, C, H, Dk)
    k = k.astype(f32).reshape(B, N, C, H, Dk)
    v = v.astype(f32).reshape(B, N, C, H, Dv)
    b = jnp.cumsum(log_a.astype(f32).reshape(B, N, C, H, Dk), axis=2)
    b_last = b[:, :, -1:]
    q_in = q * jnp.exp(b)
    k_in = k * jnp.exp(-b)
    k_out = k * jnp.exp(b_last - b)
    A = jnp.einsum('bnihd,bnjhd->bnhij', q_in, k_in)
    causal = jnp.tril(jnp.ones((C, C), dtype=bool))
    A = jnp.where(causal, A, 0.0)
    o_intra = jnp.einsum('bnhij,bnjhe->bnihe', A, v)
    dS = jnp.einsum('bnjhd,bnjhe->nbhde', k_out, v)
    decay = jnp.exp(b_last[:, :, 0]).transpose(1, 0, 2, 3)

    def step(S, inp):
        dS_c, dec_c = inp
        return dec_c[..., None] * S + dS_c, S

    S0 = jnp.zeros((B, H, Dk, Dv), f32)
    _, S_prev = lax.scan(step, S0, (dS, decay))
    o_inter = jnp.einsum('bnihd,nbhde->bnihe', q_in, S_prev)
    return (o_intra + o_inter).reshape(B, T, H, Dv)

def gla_mixer(h, w_in, w_gate_up, b_gate, gla_norm_w):
    B, T, _ = h.shape
    proj = h @ w_in
    cuts = np.cumsum([GLA_HK, GLA_HK, MIXER_WIDTH, GLA_GATE_RANK, MEM_WIDTH]).tolist()
    q, k, v, g_low, q_mem, gate = jnp.split(proj, cuts, axis=-1)
    log_a = jax.nn.log_sigmoid((g_low @ w_gate_up + b_gate).astype(jnp.float32)) / GLA_GATE_TAU
    o = gla_chunked(q.reshape(B, T, GLA_HEADS, GLA_DK),
                    k.reshape(B, T, GLA_HEADS, GLA_DK),
                    v.reshape(B, T, GLA_HEADS, GLA_DV),
                    log_a.reshape(B, T, GLA_HEADS, GLA_DK))
    o = rmsnorm(o, gla_norm_w).astype(h.dtype).reshape(B, T, MIXER_WIDTH)
    return o, q_mem, gate

def dilated_group(q, k, v, window, dilation):
    B, T, H, Dh = q.shape
    r = dilation
    n = window // dilation
    L = T // r
    nb = -(-L // n)
    Lp = nb * n

    def phase_blocks(x):
        x = x.reshape(B, L, r, H, Dh).transpose(0, 2, 3, 1, 4)
        x = jnp.pad(x, ((0, 0), (0, 0), (0, 0), (0, Lp - L), (0, 0)))
        return x.reshape(B, r, H, nb, n, Dh)

    def with_prev(x):
        prev = jnp.pad(x, ((0, 0), (0, 0), (0, 0), (1, 0), (0, 0), (0, 0)))[:, :, :, :-1]
        return jnp.concatenate([prev, x], axis=4)

    qb = phase_blocks(q)
    kw = with_prev(phase_blocks(k))
    vw = with_prev(phase_blocks(v))
    s = jnp.einsum('bphjqd,bphjkd->bphjqk', qb, kw).astype(jnp.float32) * (Dh ** -0.5)
    qi = jnp.arange(n)[:, None] + n
    ki = jnp.arange(2 * n)[None, :]
    dist = qi - ki
    key_abs = jnp.arange(nb)[:, None, None] * n + ki[None] - n
    mask = (dist >= 0)[None] & (dist <= n)[None] & (key_abs >= 0)
    s = jnp.where(mask, s, -jnp.inf)
    m = jnp.max(s, axis=-1, keepdims=True)
    p = jnp.exp(s - m)
    den = jnp.sum(p, axis=-1, keepdims=True)
    o = jnp.einsum('bphjqk,bphjkd->bphjqd', (p / den).astype(v.dtype), vw)
    lse = (m + jnp.log(den))[..., 0]
    o = o.reshape(B, r, H, Lp, Dh)[:, :, :, :L].transpose(0, 3, 1, 2, 4).reshape(B, T, H, Dh)
    lse = lse.reshape(B, r, H, Lp)[..., :L].transpose(0, 3, 1, 2).reshape(B, T, H)
    return o, lse

def dilated_mixer(h, w_in):
    B, T, _ = h.shape
    pos = jnp.arange(T)
    outs, lses = [], []
    for g, (window, dil) in enumerate(DIL_GROUPS):
        base = g * 3 * MIXER_WIDTH
        qkv = (h @ w_in[:, base:base + 3 * MIXER_WIDTH]).reshape(B, T, 3, DIL_HEADS, DIL_HEAD_DIM)
        q = partial_rope(qkv[:, :, 0], pos)
        k = partial_rope(qkv[:, :, 1], pos)
        o, lse = dilated_group(q, k, qkv[:, :, 2], window, dil)
        outs.append(o)
        lses.append(lse)
    wts = jax.nn.softmax(jnp.stack(lses, axis=0), axis=0)
    o = jnp.einsum('gbth,gbthd->bthd', wts, jnp.stack(outs, axis=0).astype(jnp.float32))
    o = o.astype(h.dtype).reshape(B, T, MIXER_WIDTH)
    rest = h @ w_in[:, len(DIL_GROUPS) * 3 * MIXER_WIDTH:]
    q_mem, gate = jnp.split(rest, [MEM_WIDTH], axis=-1)
    return o, q_mem, gate

def first_inputs(seed: int = 0) -> dict:
    key = jax.random.key(seed)
    ks = jax.random.split(key, 16)
    f32 = jnp.float32
    nrm = lambda k, shape, scale: jax.random.normal(k, shape, f32) * scale
    return {
        "x": nrm(ks[0], (BATCH, SEQ, D_MODEL), 1.0),
        "mem": nrm(ks[1], (BATCH, N_MEM, D_MODEL), 1.0),
        "mem_norm_w": 1.0 + nrm(ks[2], (D_MODEL,), 0.02),
        "norm_w": 1.0 + nrm(ks[3], (DEPTH, D_MODEL), 0.02),
        "w_memkv": nrm(ks[4], (DEPTH, D_MODEL, 2 * MEM_WIDTH), D_MODEL ** -0.5),
        "w_out": nrm(ks[5], (DEPTH, MIX_WIDTH, D_MODEL), MIX_WIDTH ** -0.5),
        "w_in_a": nrm(ks[6], (N_A, D_MODEL, GLA_IN), D_MODEL ** -0.5),
        "w_gate_up": nrm(ks[7], (N_A, GLA_GATE_RANK, GLA_HK), GLA_GATE_RANK ** -0.5),
        "b_gate": nrm(ks[8], (N_A, GLA_HK), 0.1),
        "gla_norm_w": 1.0 + nrm(ks[9], (N_A, GLA_DV), 0.02),
        "w_in_b": nrm(ks[10], (N_B, D_MODEL, DIL_IN), D_MODEL ** -0.5),
        "final_norm_w": 1.0 + nrm(ks[11], (D_MODEL,), 0.02),
    }

def first_block(x, mem, mem_norm_w, norm_w, w_memkv, w_out, w_in_a, w_gate_up, b_gate,
              gla_norm_w, w_in_b, final_norm_w):
    mem_n = rmsnorm(mem, mem_norm_w)
    for i in range(DEPTH):
        h = rmsnorm(x, norm_w[i])
        j = i // N_MIXERS
        if i % N_MIXERS == 0:
            mix, q_mem, gate = gla_mixer(h, w_in_a[j], w_gate_up[j], b_gate[j], gla_norm_w[j])
        else:
            mix, q_mem, gate = dilated_mixer(h, w_in_b[j])
        mem_o = memory_attention(q_mem, mem_n, w_memkv[i])
        branch = jnp.concatenate([mix, mem_o], axis=-1) * jax.nn.silu(gate)
        x = x + branch @ w_out[i]
    return rmsnorm(x, final_norm_w)


GRID_W = 64
CTX_LEN = 256
MIX_WIDTH_2 = D_MODEL
NA_HEADS = 6
NA_HEAD_DIM = 64
NA_WIDTH = NA_HEADS * NA_HEAD_DIM
NA_WIN_H = 8
NA_WIN_W = 16
NA_QBLOCK = 16
NA_STRIP = NA_QBLOCK + NA_WIN_W
DIFF_HEADS = 4
DIFF_QK_DIM = 48
DIFF_V_DIM = 2 * DIFF_QK_DIM
DIFF_WIDTH = DIFF_HEADS * DIFF_V_DIM
DIFF_QBLOCK = 128
ROPE_BASE = 10000.0
CONV_WIDTH = MIX_WIDTH_2 - NA_WIDTH - DIFF_WIDTH
CONV_TAPS = 31
COL_SPLITS = (NA_WIDTH, NA_WIDTH, DIFF_WIDTH, DIFF_WIDTH,
              NA_WIDTH, NA_WIDTH, DIFF_WIDTH, DIFF_WIDTH,
              CONV_WIDTH, CONV_WIDTH, CONV_WIDTH)
IN_COLS = 4 * NA_WIDTH + 4 * DIFF_WIDTH + 3 * CONV_WIDTH
EPS = 1e-6
NEG_INF = -1e30


def _rms(x, g):
    xf = x.astype(jnp.float32)
    y = xf * lax.rsqrt(jnp.mean(xf * xf, axis=-1, keepdims=True) + EPS)
    return (y * g.astype(jnp.float32)).astype(x.dtype)

def _layer_norm(x, g, b):
    xf = x.astype(jnp.float32)
    mu = jnp.mean(xf, axis=-1, keepdims=True)
    var = jnp.mean(jnp.square(xf - mu), axis=-1, keepdims=True)
    y = (xf - mu) * lax.rsqrt(var + EPS) * g.astype(jnp.float32) + b.astype(jnp.float32)
    return y.astype(x.dtype)

def _heads(z, n_heads):
    return z.reshape(z.shape[0], z.shape[1], n_heads, z.shape[-1] // n_heads)

def _split_cols(z, n):
    idx = np.cumsum(COL_SPLITS)[:n - 1].tolist()
    return jnp.split(z, idx, axis=-1)

def _rope_1d(x, pos):
    d = x.shape[-1]
    inv = ROPE_BASE ** (-jnp.arange(0, d, 2, dtype=jnp.float32) / d)
    ang = pos.astype(jnp.float32)[:, None] * inv[None, :]
    cos, sin = jnp.cos(ang)[:, None, :], jnp.sin(ang)[:, None, :]
    xf = x.astype(jnp.float32)
    x1, x2 = xf[..., :d // 2], xf[..., d // 2:]
    return jnp.concatenate([x1 * cos - x2 * sin, x2 * cos + x1 * sin], axis=-1).astype(x.dtype)

def _rope_2d(x, rows, cols):
    half = x.shape[-1] // 2
    return jnp.concatenate([_rope_1d(x[..., :half], rows), _rope_1d(x[..., half:], cols)], axis=-1)

def _na_tables():
    ncb = GRID_W // NA_QBLOCK
    qcols = np.arange(GRID_W).reshape(ncb, NA_QBLOCK)
    kstart = np.clip(np.arange(ncb) * NA_QBLOCK - NA_WIN_W // 2, 0, GRID_W - NA_STRIP)
    kcols = kstart[:, None] + np.arange(NA_STRIP)
    cstart = np.clip(qcols - NA_WIN_W // 2, 0, GRID_W - NA_WIN_W)
    kc = kcols[:, None, :]
    valid = (kc >= cstart[:, :, None]) & (kc < cstart[:, :, None] + NA_WIN_W)
    dc_idx = np.clip(kc - qcols[:, :, None] + NA_WIN_W - 1, 0, 2 * NA_WIN_W - 2)
    return kcols, valid, dc_idx

def _neighbourhood_attention(q, k, v, kc, vc, rpb):
    B, T, H, dh = q.shape
    n_rows = T // GRID_W
    wr = min(NA_WIN_H, n_rows)
    ncb = GRID_W // NA_QBLOCK
    nk = wr * NA_STRIP
    kcols, valid, dc_idx = _na_tables()
    mask = np.broadcast_to(valid[:, :, None, :], (ncb, NA_QBLOCK, wr, NA_STRIP)).reshape(ncb, NA_QBLOCK, nk)
    qg = (q * NA_HEAD_DIM ** -0.5).reshape(B, n_rows, GRID_W, H, dh)
    kg = k.reshape(B, n_rows, GRID_W, H, dh)
    vg = v.reshape(B, n_rows, GRID_W, H, dh)

    def row(r):
        rs = jnp.clip(r - wr // 2, 0, n_rows - wr)

        def strips(t):
            t = lax.dynamic_slice_in_dim(t, rs, wr, axis=1)[:, :, kcols]
            return t.transpose(0, 2, 1, 3, 4, 5).reshape(B, ncb, nk, H, dh)

        ks_, vs_ = strips(kg), strips(vg)
        qr = lax.dynamic_index_in_dim(qg, r, axis=1, keepdims=False).reshape(B, ncb, NA_QBLOCK, H, dh)
        dr_idx = rs + jnp.arange(wr) - r + (NA_WIN_H - 1)
        bias = rpb[:, dr_idx][:, :, dc_idx].transpose(0, 2, 3, 1, 4).reshape(H, ncb, NA_QBLOCK, nk)
        s_loc = jnp.einsum('bnqhd,bnkhd->bhnqk', qr, ks_).astype(jnp.float32) + bias.astype(jnp.float32)
        s_loc = jnp.where(mask, s_loc, NEG_INF)
        s_ctx = jnp.einsum('bnqhd,bkhd->bhnqk', qr, kc).astype(jnp.float32)
        p = jax.nn.softmax(jnp.concatenate([s_loc, s_ctx], axis=-1), axis=-1).astype(v.dtype)
        o = (jnp.einsum('bhnqk,bnkhd->bnqhd', p[..., :nk], vs_)
             + jnp.einsum('bhnqk,bkhd->bnqhd', p[..., nk:], vc))
        return o.reshape(B, GRID_W, H, dh)

    out = lax.map(row, jnp.arange(n_rows))
    return out.transpose(1, 0, 2, 3, 4).reshape(B, T, H * dh)

def _dense_attend(q, k, v):
    s = jnp.einsum('bqhd,bkhd->bhqk', q, k).astype(jnp.float32) * (q.shape[-1] ** -0.5)
    p = jax.nn.softmax(s, axis=-1).astype(v.dtype)
    return jnp.einsum('bhqk,bkhd->bqhd', p, v)

def _diff_attend(q1, q2, k1, k2, v, lam):
    B, Tq, H, d = q1.shape
    nb = Tq // DIFF_QBLOCK
    scale = d ** -0.5

    def to_blocks(t):
        return t.reshape(B, nb, DIFF_QBLOCK, H, d).swapaxes(0, 1)

    def blk(qs):
        a, b = qs
        s1 = jnp.einsum('bqhd,bkhd->bhqk', a, k1).astype(jnp.float32) * scale
        s2 = jnp.einsum('bqhd,bkhd->bhqk', b, k2).astype(jnp.float32) * scale
        w = jax.nn.softmax(s1, axis=-1) - lam * jax.nn.softmax(s2, axis=-1)
        return jnp.einsum('bhqk,bkhe->bqhe', w.astype(v.dtype), v)

    o = lax.map(blk, (to_blocks(q1), to_blocks(q2)))
    return o.swapaxes(0, 1).reshape(B, Tq, H, v.shape[-1])

def _diff_merge(o, subln_g, lam_init):
    return (_rms(o, subln_g) * (1.0 - lam_init)).reshape(o.shape[0], o.shape[1], -1)

def _conformer_conv(a, b, conv_w, conv_b, ln_g, ln_b):
    u = a * jax.nn.sigmoid(b)
    pad = CONV_TAPS // 2
    y = lax.conv_general_dilated(u, conv_w[:, None, :].astype(u.dtype), (1,), [(pad, pad)],
                                 dimension_numbers=('NWC', 'WIO', 'NWC'),
                                 feature_group_count=CONV_WIDTH) + conv_b
    return jax.nn.silu(_layer_norm(y, ln_g, ln_b))

def _layer(x, xc, c, c_ctx, w_mod, b_mod, g_pre, g_post, w_in, w_out, rpb,
           lq1, lk1, lq2, lk2, subln_g, conv_w, conv_b, ln_g, ln_b, layer_idx, update_ctx):
    B, T, _ = x.shape
    t = jnp.arange(T)
    rows, cols = t // GRID_W, t % GRID_W
    d = DIFF_QK_DIM

    shift, scale, gate = jnp.split((jax.nn.silu(c) @ w_mod + b_mod)[:, None, :], 3, axis=-1)
    n_mod = 3 if update_ctx else 2
    mod_c = jnp.split(jax.nn.silu(c_ctx) @ w_mod[:, :n_mod * D_MODEL] + b_mod[:n_mod * D_MODEL], n_mod)

    h = _rms(x, g_pre) * (1.0 + scale) + shift
    hc = _rms(xc, g_pre) * (1.0 + mod_c[1]) + mod_c[0]

    na_k, na_v, df_k, df_v, na_q, na_g, df_q, df_g, cv_a, cv_b, cv_g = _split_cols(h @ w_in, len(COL_SPLITS))
    n_cols = len(COL_SPLITS) if update_ctx else 4
    zc = _split_cols(hc @ w_in[:, :sum(COL_SPLITS[:n_cols])], n_cols)
    nak_c, nav_c, dfk_c, dfv_c = zc[:4]

    nak_c, nav_c = _heads(nak_c, NA_HEADS), _heads(nav_c, NA_HEADS)
    a_out = _neighbourhood_attention(_heads(na_q, NA_HEADS), _heads(na_k, NA_HEADS), _heads(na_v, NA_HEADS),
                                     nak_c, nav_c, rpb)

    lam_init = 0.8 - 0.6 * math.exp(-0.3 * layer_idx)
    lam = (jnp.exp(jnp.sum(lq1 * lk1).astype(jnp.float32))
           - jnp.exp(jnp.sum(lq2 * lk2).astype(jnp.float32)) + lam_init)
    rope = lambda z: _rope_2d(z, rows, cols)
    q, k = _heads(df_q, DIFF_HEADS), _heads(df_k, DIFF_HEADS)
    kc, vc = _heads(dfk_c, DIFF_HEADS), _heads(dfv_c, DIFF_HEADS)
    k1 = jnp.concatenate([rope(k[..., :d]), kc[..., :d]], axis=1)
    k2 = jnp.concatenate([rope(k[..., d:]), kc[..., d:]], axis=1)
    vd = jnp.concatenate([_heads(df_v, DIFF_HEADS), vc], axis=1)
    b_out = _diff_merge(_diff_attend(rope(q[..., :d]), rope(q[..., d:]), k1, k2, vd, lam), subln_g, lam_init)

    c_out = _conformer_conv(cv_a, cv_b, conv_w, conv_b, ln_g, ln_b)

    y = jnp.concatenate([a_out * jax.nn.silu(na_g), b_out * jax.nn.silu(df_g),
                         c_out * jax.nn.silu(cv_g)], axis=-1) @ w_out
    x_new = x + gate * _rms(y, g_post)

    if update_ctx:
        naq_c, nag_c, dfq_c, dfg_c, cva_c, cvb_c, cvg_c = zc[4:]
        a_c = _dense_attend(_heads(naq_c, NA_HEADS), nak_c, nav_c).reshape(B, -1, NA_WIDTH)
        qc = _heads(dfq_c, DIFF_HEADS)
        b_c = _diff_merge(_diff_attend(qc[..., :d], qc[..., d:], kc[..., :d], kc[..., d:], vc, lam),
                          subln_g, lam_init)
        c_c = _conformer_conv(cva_c, cvb_c, conv_w, conv_b, ln_g, ln_b)
        yc = jnp.concatenate([a_c * jax.nn.silu(nag_c), b_c * jax.nn.silu(dfg_c),
                              c_c * jax.nn.silu(cvg_c)], axis=-1) @ w_out
        xc = xc + mod_c[2] * _rms(yc, g_post)
    return x_new, xc

def second_inputs(seed: int = 0) -> dict:
    key = jax.random.key(seed)
    ks = jax.random.split(key, 20)
    f32 = jnp.float32

    def nrm(k, shape, s):
        return s * jax.random.normal(k, shape, f32)

    return {
        'x': nrm(ks[0], (BATCH, SEQ, D_MODEL), 1.0),
        'c': nrm(ks[1], (BATCH, D_MODEL), 1.0),
        'ctx': nrm(ks[2], (BATCH, CTX_LEN, D_MODEL), 1.0),
        'c_ctx': nrm(ks[3], (D_MODEL,), 1.0),
        'w_mod': nrm(ks[4], (DEPTH, D_MODEL, 3 * D_MODEL), 0.5 * D_MODEL ** -0.5),
        'b_mod': nrm(ks[5], (DEPTH, 3 * D_MODEL), 0.02),
        'g_pre': 1.0 + nrm(ks[6], (DEPTH, D_MODEL), 0.1),
        'g_post': 1.0 + nrm(ks[7], (DEPTH, D_MODEL), 0.1),
        'w_in': nrm(ks[8], (DEPTH, D_MODEL, IN_COLS), D_MODEL ** -0.5),
        'w_out': nrm(ks[9], (DEPTH, MIX_WIDTH_2, D_MODEL), MIX_WIDTH_2 ** -0.5),
        'na_rpb': nrm(ks[10], (DEPTH, NA_HEADS, 2 * NA_WIN_H - 1, 2 * NA_WIN_W - 1), 0.1),
        'diff_lq1': nrm(ks[11], (DEPTH, DIFF_QK_DIM), 0.1),
        'diff_lk1': nrm(ks[12], (DEPTH, DIFF_QK_DIM), 0.1),
        'diff_lq2': nrm(ks[13], (DEPTH, DIFF_QK_DIM), 0.1),
        'diff_lk2': nrm(ks[14], (DEPTH, DIFF_QK_DIM), 0.1),
        'diff_subln_g': 1.0 + nrm(ks[15], (DEPTH, DIFF_V_DIM), 0.1),
        'conv_w': nrm(ks[16], (DEPTH, CONV_TAPS, CONV_WIDTH), CONV_TAPS ** -0.5),
        'conv_b': nrm(ks[17], (DEPTH, CONV_WIDTH), 0.02),
        'conv_ln_g': 1.0 + nrm(ks[18], (DEPTH, CONV_WIDTH), 0.1),
        'conv_ln_b': nrm(ks[19], (DEPTH, CONV_WIDTH), 0.02),
    }

def second_block(x, c, ctx, c_ctx, w_mod, b_mod, g_pre, g_post, w_in, w_out, na_rpb,
              diff_lq1, diff_lk1, diff_lq2, diff_lk2, diff_subln_g,
              conv_w, conv_b, conv_ln_g, conv_ln_b):
    xc = ctx
    for l in range(DEPTH):
        x, xc = _layer(x, xc, c, c_ctx, w_mod[l], b_mod[l], g_pre[l], g_post[l], w_in[l], w_out[l],
                       na_rpb[l], diff_lq1[l], diff_lk1[l], diff_lq2[l], diff_lk2[l], diff_subln_g[l],
                       conv_w[l], conv_b[l], conv_ln_g[l], conv_ln_b[l],
                       layer_idx=l, update_ctx=(l < DEPTH - 1))
    return x


def setup_inputs(seed=0):
    out = dict(first_inputs(seed))
    for name, value in second_inputs(seed + 1).items():
        if name != "x":
            out[name + "_2"] = value
    return out


def reference(
    x, mem, mem_norm_w, norm_w, w_memkv, w_out, w_in_a, w_gate_up, b_gate, gla_norm_w, w_in_b,
    final_norm_w, c_2, ctx_2, c_ctx_2, w_mod_2, b_mod_2, g_pre_2, g_post_2, w_in_2, w_out_2,
    na_rpb_2, diff_lq1_2, diff_lk1_2, diff_lq2_2, diff_lk2_2, diff_subln_g_2, conv_w_2,
    conv_b_2, conv_ln_g_2, conv_ln_b_2,
):
    x = first_block(
        x, mem, mem_norm_w, norm_w, w_memkv, w_out, w_in_a, w_gate_up, b_gate, gla_norm_w,
        w_in_b, final_norm_w,
    )
    return second_block(
        x, c_2, ctx_2, c_ctx_2, w_mod_2, b_mod_2, g_pre_2, g_post_2, w_in_2, w_out_2, na_rpb_2,
        diff_lq1_2, diff_lk1_2, diff_lq2_2, diff_lk2_2, diff_subln_g_2, conv_w_2, conv_b_2,
        conv_ln_g_2, conv_ln_b_2,
    )


_drawn_inputs = setup_inputs


def setup_inputs(seed=0):
    import zlib

    import numpy as np

    out = dict(_drawn_inputs(seed))
    spreads = {}
    factors = {'mem_norm_w': 8.0,
     'norm_w': 2.84,
     'b_gate': 2.716,
     'gla_norm_w': 5.555,
     'na_rpb_2': 8.0,
     'diff_lk2_2': 8.0,
     'conv_b_2': 6.689,
     'conv_ln_b_2': 8.0}
    for name, (base, spread) in spreads.items():
        noise = np.random.default_rng([zlib.crc32(name.encode()), seed]).standard_normal(out[name].shape)
        drawn = base * np.exp(spread * noise) if base else spread * noise
        out[name] = __import__('jax').numpy.asarray(drawn.astype(out[name].dtype))
    for name, factor in factors.items():
        out[name] = (out[name] * factor).astype(out[name].dtype)
    return out
```

```python
from contextlib import ExitStack
import math

import numpy as np

import concourse.bass as bass
from concourse import mybir

ALU = mybir.AluOpType
ACT = mybir.ActivationFunctionType
F32 = mybir.dt.float32
I32 = mybir.dt.int32
AX_X = mybir.AxisListType.X

P = 128
D = 1024
KT = D // P
T = 512
TT = T // P
NMEM = 256
CT = NMEM // P
EPS = 1e-6
BANK = 512
BANKS = 8
WCOLS = 512
WSLOTS = 3

MH, MD = 4, 64
GH, GK, GV = 4, 96, 192
GCHUNK = 64
GRANK = 16
GTAU = 16.0
BH, BD = 6, 128
BG = 3
DIL = 4
NH, ND = 6, 64
GRID_W, GRID_H = 64, 8
NQB = 4
STRIP = 32
DH, DD, DV = 4, 48, 96
DPAD = 64
CW = 256
CF = CW // P
TAPS = 31
HALO = TAPS // 2
NEG = -1e30

C_NK, C_NV, C_DK, C_DV, C_NQ, C_NG, C_DQ, C_DG, C_CA, C_CB, C_CG = (
    0, 384, 768, 1152, 1536, 1920, 2304, 2688, 3072, 3328, 3584)
A_Q, A_K, A_V, A_G, A_M, A_GATE = 0, 384, 768, 1536, 1552, 1808

V_MEM, V_NORM, V_GPRE, V_GLA, V_SUB, V_CB, V_LG, V_LB, V_C = 0, 8, 24, 40, 43, 49, 53, 57, 61
V_ROWS = 77
CW_ROWS = 2 * TAPS
STRIP_START = (0, 8, 24, 32)
BIAS_KIND = (0, 1, 1, 2)
BIAS_OFF = (0, -8, -16)
RPB = NH * 15 * 31
RPB_PAD = 16


def constants():
    f = np.float32
    out = {}
    out["ident"] = np.eye(P, dtype=f)
    j, i = np.arange(P)[:, None], np.arange(P)[None, :]
    out["gla_mask"] = ((j // GCHUNK == i // GCHUNK) & (j <= i)).astype(np.int32)
    t = np.arange(T)
    out["gla_reset"] = np.broadcast_to((t % GCHUNK != 0).astype(f), (GK, T)).copy()
    q, k = np.arange(P)[:, None], np.arange(P)[None, :]
    prev = np.where(k >= q, 0.0, NEG)
    own = np.where(k <= q, 0.0, NEG)
    phase = np.where((k <= q) & ((q - k) % 4 == 0), 0.0, NEG)
    out["dil_mask"] = np.concatenate([prev, own, phase], axis=1).astype(f)
    half = BD // 4 // 2
    inv = (f(500000.0) ** (-np.arange(half, dtype=f) / f(half))).astype(f)
    ang = (t.astype(f)[:, None] * inv[None, :]).astype(f).astype(np.float64)
    cos = np.concatenate([np.cos(ang), np.cos(ang)], axis=1).T
    sin = np.concatenate([-np.sin(ang), np.sin(ang)], axis=1).T
    perm = (np.arange(P)[None, :] * DIL + np.arange(DIL)[:, None]).ravel()
    out["dil_rope"] = np.stack([cos, sin, cos[:, perm], sin[:, perm]], axis=1).astype(f)
    d = DD // 2
    inv = (f(10000.0) ** (-np.arange(0, d, 2, dtype=f) / f(d))).astype(f)
    tab = np.zeros((2, T, 2, 2, d // 2))
    for a, pos in enumerate((t // GRID_W, t % GRID_W)):
        ang = (pos.astype(f)[:, None] * inv[None, :]).astype(f).astype(np.float64)
        tab[0, :, a, :, :] = np.cos(ang)[:, None, :]
        tab[1, :, a, 0, :] = -np.sin(ang)
        tab[1, :, a, 1, :] = np.sin(ang)
    out["diff_rope"] = tab.reshape(2, TT, P, DD).transpose(2, 0, 1, 3).astype(f).copy()
    neg = np.zeros((P, 3, GRID_H, STRIP))
    for kind, block in enumerate((0, 1, 3)):
        cq = block * 16 + np.arange(P) % 16
        start = np.clip(cq - 8, 0, GRID_W - 16)[:, None]
        ck = STRIP_START[block] + np.arange(STRIP)[None, :]
        neg[:, kind] = np.where((ck >= start) & (ck < start + 16), 0.0, NEG)[:, None, :]
    out["na_mask"] = neg.reshape(P, 3, GRID_H * STRIP).astype(f)
    return out


def schedule():
    s = []
    add = lambda readers, *key: s.append((key, readers))
    add("v", "vecT")
    for j in range(6):
        add("v", "mod", 0, j)
    add("v", "modT", 0)
    add("avav", "memT")
    add("aa", "memkv", 0)
    add("aa", "memkv", 1)
    add("avavavav", "hT", "A")
    add("avavavav", "Av")
    add("a", "Aglow")
    add("avv", "Aproj", 0)
    add("avv", "Aproj", 1)
    add("va", "AA", 0)
    add("avv", "Aproj", 2)
    add("vvvv", "AdS", 0)
    add("va", "AA", 1)
    add("avv", "Aproj", 3)
    add("aa", "Ao", 0)
    add("vvvv", "AdS", 1)
    add("va", "AA", 2)
    for i in (0, 1):
        add("a", "gate", "A", i)
    add("aa", "Ao", 1)
    add("vvvv", "AdS", 2)
    add("va", "AA", 3)
    for i in (2, 3):
        add("a", "gate", "A", i)
    add("aa", "Ao", 2)
    add("vvvv", "AdS", 3)
    for i in (4, 5):
        add("a", "gate", "A", i)
    add("aa", "Ao", 3)
    for i in (6, 7):
        add("a", "gate", "A", i)
    add("av", "qm", "A")
    add("a" * 8, "mS", "A")
    add("v" * 6, "AoT")
    add("av" * 4, "mT", "A")
    add("vv", "mPV", "A")
    add("v" * 8, "wout", "A")
    for j in range(6):
        add("v", "mod", 1, j)
    add("v", "modT", 1)
    add("avavavav", "hT", "B")
    for i in range(8):
        add("a", "gate", "B", i)
    add("av", "qm", "B")
    add("a" * 8, "mS", "B")
    add("aav" * 3, "Bproj", 0)
    add("av" * 4, "mT", "B")
    add("vv", "mPV", "B")
    add("aav" * 3, "Bproj", 1)
    for h in range(BH):
        add("aaavvvv", "BS", h)
        if h + 2 < BH:
            add("aav" * 3, "Bproj", h + 2)
        add("avav", "BT", h)
        add("va", "BPV", h)
    add("v" * 8, "wout", "B")
    for l in range(2):
        both = l == 0
        for key, who in ((("hcT", l), "avav"), (("hT", f"C{l}"), "avavavav"))[::1 if both else -1]:
            add(who, *key)
        add("aaavvv", "nk", l)
        add("aaaavv", "nv", l)
        add("aaavvv" if both else "aaa", "nq", l)
        add("avav" + "avav" * both, "cv", l)
        fill = [[("a" + "a" * both, "gate", f"C{l}", i)] for i in range(KT)]
        fill.append([("avavav", "dv", l)])
        for t in range(TT + CT):
            fill.append([("v" if t < TT else "a", "dP", l, "k", t), ("a", "dX", l, "k", t)])
        for h in range(NH):
            add("aaaa", "nS", l, h)
            for step in fill.pop(0):
                add(*step)
            add("avav", "nT", l, h)
            for step in fill.pop(0):
                add(*step)
            add("v", "nPV", l, h)
        for steps in fill:
            for step in steps:
                add(*step)
        if both:
            for h in range(NH + 2):
                if h < NH:
                    add("a", "cS", l, h)
                if 0 <= h - 1 < NH:
                    add("a", "cT", l, h - 1)
                if h >= 2:
                    add("v", "cPV", l, h - 2)
        for t in range(TT + CT * both):
            add("v" if t < TT else "a", "dP", l, "q", t)
            add("a", "dX", l, "q", t)
        items = diff_items(l)
        for n in range(len(items) + 2):
            if n < len(items):
                add("aaaa" if items[n][0] < TT else "aa", "dS", l, *items[n])
            if 1 <= n <= len(items):
                t, h = items[n - 1]
                add("av" if t < TT else "a", "dT", l, t, h)
            if n >= 2:
                add("a", "dPV", l, *items[n - 2])
        add("vvv", "doT", l, 0)
        if both:
            add("vvv", "doT", l, 1)
        for st in range(1 + both):
            add("v" * (2 if st == 0 else 1), "cvT", l, st)
            add("aa", "cvZ", l, st)
        for t in range(TT + CT * both):
            add("vv", "yo", l, t)
    return s


def diff_items(l):
    return [(t, h) for t in range(TT + (CT if l == 0 else 0)) for h in range(DH)]


def hybrid_stack_kernel(nc, ins, consts, out):
    steps = schedule()
    base, readers, order_of = {}, [], {}
    for n, (key, who) in enumerate(steps):
        base[key] = len(readers)
        order_of[key] = n
        readers += list(who)
    ordinal, seen = [], {"a": 0, "v": 0}
    for who in readers:
        seen[who] += 1
        ordinal.append(seen[who])
    njobs = {key: len(who) for key, who in steps}

    mem_scale = MD ** -0.5
    dil_scale = BD ** -0.5
    diff_scale = DD ** -0.5
    lam_init = [0.8 - 0.6 * math.exp(-0.3 * l) for l in range(2)]

    with ExitStack() as ctx:
        def sb(name, shape, dt=F32):
            return ctx.enter_context(nc.sbuf_tensor(name, shape, dt))

        def sem(name):
            return ctx.enter_context(nc.semaphore(name))

        def dram(name, shape):
            return nc.dram_tensor(name, shape, F32, kind="Internal").ap()

        arena = sb("arena", [P, 29696])

        def at(off, *dims, parts=P):
            n = math.prod(dims)
            v = arena[0:parts, off:off + n]
            if len(dims) == 1:
                return v
            names = "abcde"[:len(dims)]
            sizes = {c: d for c, d in zip(names[1:], dims[1:])}
            return v.rearrange(f"p ({' '.join(names)}) -> p {' '.join(names)}", **sizes)

        hT = sb("hT", [P, KT, T])
        branch = sb("branch", [P, KT, T])
        wring = sb("wring", [P, WSLOTS, KT * WCOLS])
        ident = sb("ident", [P, P])
        vec = sb("vec", [P, V_ROWS + 2 * CW_ROWS])
        modv = sb("modv", [P, 2, 2, KT, 2])
        dil_mask = sb("dil_mask", [P, 3 * P])
        na_mask = sb("na_mask", [P, 3, GRID_H * STRIP])
        diff_rope = sb("diff_rope", [P, 2, TT, DD])
        siluc = sb("siluc", [P, KT, 2])
        subw = sb("subw", [P, 2, 3])
        lam = sb("lam", [P, 2])
        stat = sb("stat", [P, 544])
        cols = [0]

        def stats(*dims):
            n = math.prod(dims)
            v = stat[:, cols[0]:cols[0] + n]
            cols[0] += n
            if len(dims) == 1:
                return v
            names = "abcde"[:len(dims)]
            sizes = {c: d for c, d in zip(names[1:], dims[1:])}
            return v.rearrange(f"p ({' '.join(names)}) -> p {' '.join(names)}", **sizes)

        minus_half = stats(4)
        conv_w = vec[:, V_ROWS:].rearrange("p (f r) -> p f r", f=CF)

        x = at(0, TT, D)
        memk = at(4096, 2, 2, NMEM)
        memv = at(5120, 2, CT, MH * MD)
        xn = at(6144, TT, D)
        modrow = at(10240, 3 * D, parts=2)
        gpost = at(13312, D, parts=2)
        vrows = at(14336, P, parts=V_ROWS)
        crows = at(14464, CW, parts=CW_ROWS)
        memraw = at(14720, CT, D)
        memn = at(18816, CT, D)
        memT = at(16768, KT, NMEM)
        glow = at(18816, T, parts=GRANK)
        gv = at(19328, TT, GH * GV)
        wgu = at(22400, GH * GK, parts=GRANK)
        bgate = at(22784, 16, parts=GK)
        gmask = at(22800, P).bitcast(I32)
        greset = at(22928, T, parts=GK)
        gq = at(23440, GH, T, parts=GK)
        gk = at(25488, GH, T, parts=GK)
        gt = at(6144, 2, 4, T, parts=GK)
        gkin = at(10240, 2, T, parts=GK)
        gkout = at(11264, 2, T, parts=GK)
        gkot = at(12288, 2, TT, GK)
        gA = at(13056, 2, TT, P)
        gS = at(14080, T // GCHUNK, GV, parts=GK)
        go = at(15616, TT, GH * GV)
        gdec = sb("gdec", [GK, GH, T // GCHUNK])
        mprob = at(6144, 8, 2, NMEM)
        mprobT = at(10240, MH, CT, T)
        qmem = {"A": at(14336, 2, T), "B": at(25088, 2, T)}
        bqk = at(14336, 2, BG, 2, T)
        bvT = at(20480, 2, BG, T)
        bv = at(23552, BG, TT, BD)
        bswap = at(25088, 2, T, parts=32)
        bo12 = at(26112, T)
        bsum = at(26624, T)
        dil_rope = at(27136, 4, T, parts=32)
        bprob = at(6144, 2048)
        bprobT = at(8192, 15, P)
        hcT = at(4096, KT, NMEM)
        cbranch = at(6144, KT, NMEM)
        xc = at(8192, CT, D)
        cxn = at(10240, TT, D)
        cxcn = at(14336, CT, D)
        fw = at(16384, D)
        nkT = at(10240, 3, T + NMEM)
        nqT = at(12544, 3, T)
        nqcT = at(14080, 3, NMEM)
        vstrip = at(14848, NQB, 2, NH * ND)
        vctx = at(17920, CT, NH * ND)
        bias = at(18688, 2, 3, GRID_H * STRIP)
        dkT = at(20224, DH, T + NMEM)
        dv = at(23296, TT + CT, DH * DV)
        dstage = at(25600, 2, 2 * DH, DPAD)
        dswap = at(26624, 2 * DH, DD)
        csig = at(25600, 2, T)
        u = at(27008, CF, T + 2 * HALO)
        uc = at(28092, CF, NMEM + 2 * HALO)
        y = at(28664, CF, T)
        yc = at(4096, CF, NMEM)
        nprob = at(0, NQB, BANK)
        nprobT = at(2048, NQB, 4, P)
        vnat = at(2048, TT, NH * ND)
        cprob = at(0, 4, CT, NMEM)
        cprobT = at(2048, 4, CT, NMEM)
        dqT = [at(10240, DH, T), at(12288, DH, NMEM)]
        dprob = at(13312, 2, 2, T + NMEM)
        dwT = at(16384, 2, TT + CT, P)
        otok = [at(17920, TT, DH * DV), at(19456, CT, DH * DV)]
        czn = [at(13312, TT, CW), at(15360, CT, CW)]
        csilu = [at(14336, CF, T), at(15872, CF, NMEM)]
        gmul = at(20224, 2, D)
        ytmp = at(22272, D)
        yjunk = at(23296, D)

        gate_dram = dram("gate_dram", [2, 2, D])
        st0_dram = dram("st0_dram", [BH, 2, T])
        st12_dram = dram("st12_dram", [BH, 4, T])
        x_dram = dram("x_dram", [2, T, D])
        nv_dram = dram("nv_dram", [2, T, NH * ND])
        rpb_dram = [dram(f"rpb_dram{l}", [RPB_PAD + RPB + 2 * RPB_PAD]) for l in range(2)]
        ebias_dram = [dram(f"ebias_dram{l}", [3, NH, 16, 15 * STRIP]) for l in range(2)]

        banks = [ctx.enter_context(nc.psum_tensor(f"bank{i}", [P, BANK], F32)) for i in range(BANKS)]

        psum_full = sem("psum_full")
        evac = {"a": sem("evac_scalar"), "v": sem("evac_vector")}
        w_full = [sem(f"w_full{i}") for i in range(WSLOTS)]
        vecs_in, gla_in, const_in, mem_in, x_in = (sem(n) for n in (
            "vecs_in", "gla_in", "const_in", "mem_in", "x_in"))
        dve_chain, act_chain, pool_chain = sem("dve_chain"), sem("act_chain"), sem("pool_chain")
        silu_c, sq_done, rstd_ready, xn_ready = (sem(n) for n in ("silu_c", "sq_done", "rstd_ready", "xn_ready"))
        bmod_in, gate_row, gate_saved = sem("bmod_in"), sem("gate_row"), sem("gate_saved")
        gla_abs, gla_soft, gla_cum, gla_exps, gla_qin, gla_keys, gla_sq, gla_rstd, gla_zero = (sem(n) for n in (
            "gla_abs", "gla_soft", "gla_cum", "gla_exps", "gla_qin", "gla_keys", "gla_sq", "gla_rstd", "gla_zero"))
        mem_negmax, mem_probs = sem("mem_negmax"), sem("mem_probs")
        rope_in, rope_done, dil_negmax, dil_probs, st_saved, st_in, dil_diff, dil_exp, dil_weighted, dil_out = (
            sem(n) for n in ("rope_in", "rope_done", "dil_negmax", "dil_probs", "st_saved", "st_in", "dil_diff",
                             "dil_exp", "dil_weighted", "dil_out"))
        fw_in, xc_in, x_final, x_saved, x_back, pads_zero, lam_in, lam_dots, lam_exps, lam_ready = (sem(n) for n in (
            "fw_in", "xc_in", "x_final", "x_saved", "x_back", "pads_zero", "lam_in", "lam_dots", "lam_exps",
            "lam_ready"))
        rpb_saved, ebias_saved, bias_ready = (sem(n) for n in ("rpb_saved", "ebias_saved", "bias_ready"))
        bias_in = [sem("bias_in_even"), sem("bias_in_odd")]
        nv_saved, strips_in, na_negmax, na_probs, ctx_negmax, ctx_probs = (sem(n) for n in (
            "nv_saved", "strips_in", "na_negmax", "na_probs", "ctx_negmax", "ctx_probs"))
        diff_staged, diff_negmax, diff_w, o_sq, o_rstd, o_normed = (sem(n) for n in (
            "diff_staged", "diff_negmax", "diff_w", "o_sq", "o_rstd", "o_normed"))
        conv_done, ln_var, ln_rstd, ln_done = (sem(n) for n in ("conv_done", "ln_var", "ln_rstd", "ln_done"))
        gmul_in, y_sq, y_rstd, x_new, out_saved = (sem(n) for n in ("gmul_in", "y_sq", "y_rstd", "x_new", "out_saved"))

        def bank(key, i):
            return banks[(base[key] + i) % BANKS]

        def claim(pe, key, i):
            n = base[key] + i
            if n >= BANKS:
                pe.wait_ge(evac[readers[n - BANKS]], ordinal[n - BANKS])
            return bank(key, i)

        def full(eng, key, i):
            eng.wait_ge(psum_full, base[key] + i + 1)
            return bank(key, i)

        def read_by_pe(eng, key):
            eng.wait_ge(psum_full, base[key] + njobs[key])

        def evacuated(eng, key, i=-1):
            n = base[key] + i % njobs[key]
            eng.wait_ge(evac[readers[n]], ordinal[n])

        def cols_of(w, c0, n):
            return w.rearrange("(k p) c -> p k c", p=P)[:, :, c0:c0 + n]

        wa, wb, wout, wmem = ins["w_in_a"][0], ins["w_in_b"][0], ins["w_out"], ins["w_memkv"]
        chunks = [(("mod", 0, j), cols_of(ins["w_mod_2"][0], j * WCOLS, WCOLS), WCOLS, ("mod", 0, j)) for j in range(6)]
        chunks += [(("memkv", l), cols_of(wmem[l], 0, 512), 512, ("memkv", l)) for l in range(2)]
        chunks += [
            (("Av", 0), cols_of(wa, A_V, 384), 384, ("Av",)),
            (("Av", 1), cols_of(wa, A_V + 384, 384 + GRANK), 384 + GRANK, ("Aglow",)),
            (("Aq",), cols_of(wa, A_Q, 384), 384, ("Aproj", 3)),
            (("Ak",), cols_of(wa, A_K, 384), 384, ("Aproj", 3)),
            (("gate", "A", 0), cols_of(wa, A_GATE, 512), 512, ("gate", "A", 3)),
            (("gate", "A", 1), cols_of(wa, A_GATE + 512, 512), 512, ("gate", "A", 7)),
            (("qm", "A"), cols_of(wa, A_M, 256), 256, ("qm", "A")),
        ]
        chunks += [(("wout", "A", n), cols_of(wout[0], n * 512, 512), 512, ("wout", "A")) for n in range(2)]
        chunks += [(("mod", 1, j), cols_of(ins["w_mod_2"][1], j * WCOLS, WCOLS), WCOLS, ("mod", 1, j)) for j in range(6)]
        rest = BG * 3 * BH * BD
        chunks += [(("gate", "B", n), cols_of(wb, rest + 256 + n * 512, 512), 512, ("gate", "B", 4 * n + 3))
                   for n in range(2)]
        chunks += [(("qm", "B"), cols_of(wb, rest, 256), 256, ("qm", "B"))]
        for h in range(BH):
            for g in range(BG):
                src = wb[:, g * 2304:(g + 1) * 2304].rearrange("(k p) (s c) -> p k s c", p=P, s=3)
                chunks.append((("Bproj", h, g), src[:, :, :, h * BD:(h + 1) * BD], 384, ("Bproj", h)))
        chunks += [(("wout", "B", n), cols_of(wout[1], n * 512, 512), 512, ("wout", "B")) for n in range(2)]
        for l in range(2):
            w2, wo2 = ins["w_in_2"][l], ins["w_out_2"][l]
            last_t = TT + CT - 1
            for name, c0, n, last in (
                    ("nk", C_NK, 384, ("nk", l)), ("nv", C_NV, 384, ("nv", l)), ("nq", C_NQ, 384, ("nq", l)),
                    ("cv", C_CA, 512, ("cv", l)), ("g0", C_NG, 384, ("gate", f"C{l}", 2)),
                    ("g1", C_DG, 384, ("gate", f"C{l}", 5)), ("g2", C_CG, 256, ("gate", f"C{l}", 7)),
                    ("dv", C_DV, 384, ("dv", l)), ("dk", C_DK, 384, ("dP", l, "k", last_t)),
                    ("dq", C_DQ, 384, ("dP", l, "q", last_t if l == 0 else TT - 1))):
                chunks.append(((name, l), cols_of(w2, c0, n), n, last))
            chunks += [(("yo", l, n), cols_of(wo2, n * 512, 512), 512, ("yo", l, last_t if l == 0 else TT - 1))
                       for n in range(2)]
        chunk_at = {name: n for n, (name, *_) in enumerate(chunks)}

        def chunk(pe, name):
            n = chunk_at[name]
            pe.wait_ge(w_full[n % WSLOTS], 16 * sum(loads(m) for m in range(n % WSLOTS, n + 1, WSLOTS)))
            return slot(n)

        def loads(n):
            return 3 if chunks[n][0][0] == "Bproj" else 1

        def slot(n):
            c = chunks[n][2]
            return wring[:, n % WSLOTS, 0:KT * c].rearrange("p (k c) -> p k c", c=c)

        def slot4(n):
            return wring[:, n % WSLOTS, 0:KT * 384].rearrange("p (k s c) -> p k s c", s=3, c=BD)

        def gate_chunk(ph, i):
            if ph in "AB":
                return ("gate", ph, i // 4), (i % 4) * P
            return (f"g{i // 3}", int(ph[1])), (i % 3) * P

        norms = {}
        norm_at, n_tiles = {}, 0
        for ph, src, dst, nt in (("m", memraw, memn, CT), ("A", x, xn, TT), ("B", x, xn, TT), ("c0", xc, cxcn, CT),
                                 ("F", x, cxn, TT), ("C0", x, cxn, TT), ("C1", x, cxn, TT), ("c1", xc, cxcn, CT)):
            norms[ph] = (src, dst, nt, stats(nt), stats(nt))
            norm_at[ph] = n_tiles
            n_tiles += nt

        gla_ss, gla_rs = stats(GH, TT), stats(GH, TT)
        m_max, m_neg, m_sum, m_rec = (stats(2, 8, 2) for _ in range(4))
        b_stat = stats(2, BG, 2, 2, TT)
        b_neg = stats(2, BG, TT)
        b_top, b_w, b_rec = stats(2, TT), stats(BG, 2, TT), stats(2, TT)
        n_ctx, n_max, n_neg, n_s, n_rec = stats(NQB), stats(NQB), stats(NQB), stats(2, NQB), stats(2, NQB)
        c_max, c_neg, c_s, c_rec = (stats(2, CT) for _ in range(4))
        d_max, d_neg, d_s, d_rec = (stats(2, 4) for _ in range(4))
        o_ss, o_rs = stats(TT + CT, DH), stats(TT + CT, DH)
        ln_st, ln_mv, ln_rs = stats(6), stats(2, 2), stats(2)
        y_ss, y_rs = stats(2, 2), stats(2, 2)
        lam_st = stats(2, 2)
        lam_v = sb("lam_v", [P, 2, 4, DD])
        lam_junk = sb("lam_junk", [P, DD])
        assert cols[0] <= 544, cols[0]

        norm_pe, n_tiles = {}, 0
        for ph in norms:
            if ph != "F":
                n_tiles += norms[ph][2]
            norm_pe[ph] = n_tiles
        stages = [key for key, _ in steps if key[0] == "dP"]
        roped = [key for key in stages if key[3] < TT]

        def stage_at(key):
            return stages.index(key)

        def stage_key(n):
            return ("dX", *stages[n][1:])

        def roped_at(key):
            return roped.index(key)

        all_diff = [(l, t, h) for l in range(2) for t, h in diff_items(l)]

        def diff_at(l, t, h):
            return all_diff.index((l, t, h))

        def diff_step(kind, n):
            return (kind, *all_diff[n])

        def diff_tile(l, t):
            return l * (TT + CT) + t

        def key_part(t, part):
            return ((0, T), (T, NMEM))[part if t < TT else 1]

        def ln_pair(l, st, i):
            return 3 * l + 2 * st + i

        def conv_inputs(l, st, f):
            return 4 * l + 2 * st + f

        def conv_input_at(m):
            l, r = divmod(m, 4)
            return ("cv", l), 2 * r + 1

        def bprob_tile(g, n):
            if g == 0:
                return bprob[:, P:2 * P] if n == 0 else bprob[:, 2 * n * P:(2 * n + 2) * P]
            return bprob[:, (4 + 4 * g + n) * P:(5 + 4 * g + n) * P]

        def dil_tile(g, n):
            if g == 0:
                return 3 + n // 2, (n % 2) * 2 * P, P if n == 0 else 0
            return 4 + g, n * P, P * g

        def self_bias(pool, l, h):
            if (l, h) == (0, 0):
                pool.wait_ge(const_in, 48)
            pool.wait_ge(bias_in[h % 2], 16 * GRID_H * ((l * NH + h) // 2 + 1))
            v = bias[:, h % 2]
            nc.gpsimd.tensor_tensor(v, v, na_mask[:, :, :], ALU.add).then_inc(bias_ready, 1)

        PT_BANKS = ((0, 4), (4, 3), (7, 4), (11, 4))
        PT_TILES = (1, 2, 3, 4, 5, 6, 7, 8, 9, 10, 11, 12, 13, 14, 15)
        DS_BANK = {0: (0, 0), 1: (1, 0), 2: (0, 1), 3: (1, 1), 4: (3, 0), 5: (2, 0), 6: (3, 1)}
        DS_LAST = (2, 3, 5, 6)
        VECS_IN = 16 * 26

        block = ctx.enter_context(nc.Block())

        def sync_items():
            items = []
            for n in range(len(chunks)):
                items.append((order_of[chunks[n - WSLOTS][3]] if n >= WSLOTS else -1, "chunk", n))
            for l in range(2):
                items.append((order_of[("Aglow",)], "ebias", l))
                for h in range(NH):
                    free = ("BS", BH - 1) if l == 0 else ("doT", 0, 1)
                    items.append((order_of[free if h < 2 else ("nS", l, h - 2)], "bias", (l, h)))
                last_na = ("cPV", l, NH - 1) if l == 0 else ("nPV", l, NH - 1)
                items.append((order_of[last_na], "x_back", (l, last_na)))
                last_ds = ("dS", l, *diff_items(l)[-1])
                items.append((order_of[last_ds], "gmul", (l, last_ds)))
            return sorted(items, key=lambda i: i[0])

        @block.sync
        def _(sp):
            for _, what, arg in sync_items():
                if what == "chunk":
                    name, src, c, last = chunks[arg]
                    if arg >= WSLOTS:
                        read_by_pe(sp, chunks[arg - WSLOTS][3])
                    for i in range(loads(arg)):
                        dst, part = (slot(arg), src) if loads(arg) == 1 else (slot4(arg)[:, :, i], src[:, :, i])
                        sp.dma_start(dst, part).then_inc(w_full[arg % WSLOTS], 16)
                    if arg == 0:
                        sp.dma_start(memraw, ins["mem"][0].rearrange("(t p) d -> p t d", p=P)).then_inc(mem_in, 16)
                    if arg == 1:
                        sp.dma_start(x, ins["x"][0].rearrange("(t p) d -> p t d", p=P)).then_inc(x_in, 16)
                elif what == "ebias":
                    sp.wait_ge(rpb_saved, 48 * (arg + 1))
                    for kind in range(3):
                        for qq in range(16):
                            off = RPB_PAD + BIAS_OFF[kind] + 15 - qq
                            src = bass.AP(rpb_dram[arg].tensor, off, [[465, NH], [31, 15], [1, STRIP]])
                            sp.dma_start(ebias_dram[arg][kind, :, qq, :].rearrange("h (r c) -> h r c", c=STRIP),
                                         src).then_inc(ebias_saved, 16)
                elif what == "bias":
                    l, h = arg
                    if h < 2:
                        read_by_pe(sp, ("BS", BH - 1) if l == 0 else ("doT", 0, 1))
                    else:
                        sp.wait_ge(na_negmax, l * NH + h - 1)
                    sp.wait_ge(ebias_saved, 16 * 48 * 2)
                    for rq in range(GRID_H):
                        src = bass.AP(ebias_dram[l].tensor, h * 16 * 480 + (7 - rq) * STRIP,
                                      [[480, 16], [NH * 16 * 480, 3], [1, GRID_H * STRIP]])
                        sp.dma_start(bias[rq * 16:rq * 16 + 16, h % 2], src).then_inc(bias_in[h % 2], 16)
                elif what == "x_back":
                    l, last_na = arg
                    read_by_pe(sp, ("nPV", l, NH - 1))
                    read_by_pe(sp, last_na)
                    sp.wait_ge(x_saved, 16 * (l + 1))
                    sp.dma_start(x, x_dram[l].rearrange("(t p) d -> p t d", p=P)).then_inc(x_back, 16)
                elif what == "gmul":
                    l, last_ds = arg
                    read_by_pe(sp, last_ds)
                    sp.wait_ge(gate_saved, 16 * (l + 1))
                    for c in range(2):
                        sp.dma_start(gmul[:, c], gate_dram[l, c].partition_broadcast(P)).then_inc(gmul_in, 16)
            for t in range(TT):
                sp.wait_ge(x_new, TT + CT + t + 1)
                sp.dma_start(out[0].rearrange("(t p) d -> p t d", p=P)[:, t], x[:, t]).then_inc(out_saved, 16)
            sp.wait_ge(out_saved, 16 * TT)

        @block.gpsimd
        def _(pool):
            count = {"chain": 0}

            def chained(ins):
                count["chain"] += 1
                ins.then_inc(pool_chain, 1)
                pool.wait_ge(pool_chain, count["chain"])

            def root(rs, ss, n, done):
                chained(nc.gpsimd.tensor_scalar(rs, ss, 1.0 / n, EPS, ALU.mult, ALU.add))
                width = rs.shape[1]
                nc.gpsimd.tensor_tensor(rs, rs, minus_half[:, 0:width], ALU.pow).then_inc(done, 1)

            def norm_roots(ph, t):
                _, _, _, ss, rs = norms[ph]
                pool.wait_ge(sq_done, norm_at[ph] + t + 1)
                root(rs[:, t:t + 1], ss[:, t:t + 1], D, rstd_ready)

            chained(nc.gpsimd.memset(minus_half, -0.5))
            zeros = lam_junk[0:1, 0:2 * RPB_PAD]
            nc.gpsimd.memset(lam_junk[:, :], 0.0).then_inc(pads_zero, 1)
            nc.gpsimd.wait_ge(pads_zero, 1)
            for l in range(2):
                pool.dma_start(rpb_dram[l][0:RPB_PAD].rearrange("(a n) -> a n", a=1),
                               zeros[:, 0:RPB_PAD]).then_inc(rpb_saved, 16)
                pool.dma_start(rpb_dram[l][RPB_PAD + RPB:].rearrange("(a n) -> a n", a=1), zeros).then_inc(rpb_saved, 16)
                pool.dma_start(rpb_dram[l][RPB_PAD:RPB_PAD + RPB],
                               ins["na_rpb_2"][l].rearrange("h r c -> (h r c)")).then_inc(rpb_saved, 16)

            def load_mod(l):
                for what, dst in ((ins["b_mod_2"], modrow), (ins["g_post_2"], gpost)):
                    pool.dma_start(dst, what[l].partition_broadcast(2)).then_inc(bmod_in, 16)

            load_mod(0)
            for ph in "mA":
                for t in range(norms[ph][2]):
                    norm_roots(ph, t)

            for key, _ in steps:
                kind = key[0]
                if kind == "modT":
                    l = key[1]
                    pool.wait_ge(gate_row, l + 1)
                    pool.dma_start(gate_dram[l], modrow[:, 2 * D:]).then_inc(gate_saved, 16)
                    if l == 0:
                        pool.wait_ge(gate_saved, 16)
                        nc.gpsimd.memset(gA, 0.0).then_inc(gla_zero, 1)
                        nc.gpsimd.memset(gS[:, 0], 0.0).then_inc(gla_zero, 1)
                elif kind == "Aproj":
                    h = key[1]
                    b = h % 2
                    evacuated(pool, key, 1)
                    pool.wait_ge(gla_exps, 3 * h + 3)
                    if h >= 2:
                        read_by_pe(pool, ("AA", h - 2))
                    nc.gpsimd.tensor_tensor(gkin[:, b], gk[:, h], gt[:, b, 1], ALU.mult).then_inc(gla_keys, 1)
                    nc.gpsimd.tensor_tensor(gkout[:, b], gk[:, h], gt[:, b, 3], ALU.mult).then_inc(gla_keys, 1)
                elif kind == "Ao":
                    h = key[1]
                    for i in range(2):
                        pool.wait_ge(gla_sq, 2 * h + i + 1)
                        root(gla_rs[:, h, 2 * i:2 * i + 2], gla_ss[:, h, 2 * i:2 * i + 2], GV, gla_rstd)
                elif kind == "wout":
                    ph = key[1]
                    if ph == "A":
                        read_by_pe(pool, ("mPV", "A"))
                        load_mod(1)
                        pool.dma_start(dil_rope, consts["dil_rope"]).then_inc(rope_in, 16)
                        for t in range(TT):
                            norm_roots("B", t)
                    else:
                        read_by_pe(pool, ("BPV", BH - 1))
                        pool.dma_start(xc, ins["ctx_2"][0].rearrange("(t p) d -> p t d", p=P)).then_inc(xc_in, 16)
                        pool.dma_start(fw, ins["final_norm_w"].partition_broadcast(P)).then_inc(fw_in, 16)
                        for t in range(CT):
                            norm_roots("c0", t)
                        for t in range(TT):
                            norm_roots("F", t)
                        for t in range(TT):
                            norm_roots("C0", t)
                        pool.wait_ge(x_final, TT)
                        pool.dma_start(x_dram[0].rearrange("(t p) d -> p t d", p=P), x).then_inc(x_saved, 16)
                elif kind == "BS":
                    h = key[1]
                    b = h % 2
                    pool.wait_ge(dil_probs, h + 1)
                    stat_of = lambda g, order: b_stat[:, b, g, order].rearrange("p c n -> p (c n)")
                    natural = lambda d: d.rearrange("c (b i) -> i (c b)", b=TT)
                    strided = lambda d: d.rearrange("c (i b) -> i c b", b=DIL)
                    pairs = [(st0_dram[h], 0, natural, strided)]
                    pairs += [(st12_dram[h, 2 * g - 2:2 * g], g, strided, natural) for g in (1, 2)]
                    for d, g, save, _ in pairs:
                        pool.dma_start(save(d), b_stat[:, b, g, 1] if g else stat_of(g, 0),
                                       allow_slow_non_contiguous=True).then_inc(st_saved, 16)
                    pool.wait_ge(st_saved, 48 * (h + 1))
                    for d, g, _, load in pairs:
                        pool.dma_start(stat_of(g, 0) if g else b_stat[:, b, g, 1], load(d),
                                       allow_slow_non_contiguous=True).then_inc(st_in, 16)
                elif kind == "nv":
                    l = key[1]
                    evacuated(pool, key, 3)
                    pool.dma_start(nv_dram[l].rearrange("(t p) c -> p t c", p=P), vnat).then_inc(nv_saved, 16)
                    pool.wait_ge(nv_saved, 16 * (l + 1))
                    grid = nv_dram[l].rearrange("(r c) d -> r c d", c=GRID_W)
                    for n in range(NQB):
                        for k in range(2):
                            for r in range(4):
                                pool.dma_start(vstrip[r * STRIP:(r + 1) * STRIP, n, k, :],
                                               grid[4 * k + r, STRIP_START[n]:STRIP_START[n] + STRIP, :]).then_inc(strips_in, 16)
                    self_bias(pool, l, 0)
                elif kind == "nS" and key[2] + 1 < NH:
                    self_bias(pool, key[1], key[2] + 1)
                elif kind == "dPV":
                    l, t, h = key[1:]
                    if h == DH - 1:
                        n = diff_tile(l, t)
                        pool.wait_ge(o_sq, n + 1)
                        root(o_rs[:, t, :], o_ss[:, t, :], DV, o_rstd)
                elif kind == "cvT":
                    l, st = key[1:]
                    for i in range((TT, CT)[st] // 2):
                        n = ln_pair(l, st, i)
                        pool.wait_ge(ln_var, n + 1)
                        chained(nc.gpsimd.tensor_scalar(ln_rs, ln_mv[:, :, 1], 1.0, EPS, ALU.mult, ALU.add))
                        nc.gpsimd.tensor_tensor(ln_rs, ln_rs, minus_half[:, 0:2], ALU.pow).then_inc(ln_rstd, 1)
                elif kind == "yo":
                    l, t = key[1:]
                    n = l * (TT + CT) + t
                    b = n % 2
                    pool.wait_ge(y_sq, 2 * n + 2)
                    if n >= 2:
                        pool.wait_ge(x_new, n - 1)
                    chained(nc.gpsimd.tensor_tensor(y_rs[:, b, 0:1], y_ss[:, b, 0:1], y_ss[:, b, 1:2], ALU.add))
                    root(y_rs[:, b, 1:2], y_rs[:, b, 0:1], D, y_rstd)
                    if l == 0:
                        norm_roots("C1" if t < TT else "c1", t % TT)
                    if l == 0 and t == TT - 1:
                        pool.wait_ge(x_new, TT)
                        pool.dma_start(x_dram[1].rearrange("(t p) d -> p t d", p=P), x).then_inc(x_saved, 16)

        @block.scalar
        def _(act):
            count = {"chain": 0}

            def chained(ins):
                count["chain"] += 1
                ins.then_inc(act_chain, 1)
                act.wait_ge(act_chain, count["chain"])

            def free(ins):
                ins.then_inc(evac["a"], 1)

            def move(out, in_, scale=1.0):
                return nc.scalar.activation(out, in_, ACT.Copy, scale=scale)

            def square(ph, t):
                src, dst, _, ss, _ = norms[ph]
                nc.scalar.activation(dst[:, t], src[:, t], ACT.Square, accum_out=ss[:, t:t + 1]).then_inc(sq_done, 1)

            def rows(r, src, n, c=P):
                act.dma_start(vrows[r:r + n, 0:c], src).then_inc(vecs_in, 16)

            def piece(r, c, src):
                act.dma_start(vrows[r:r + 1, c:c + src.shape[1]], src).then_inc(vecs_in, 16)

            tiled = lambda v: v.rearrange("(r c) -> r c", c=P)
            act.dma_start(ident[:, :], consts["ident"]).then_inc(vecs_in, 16)
            rows(V_C, tiled(ins["c_2"][0]), KT)
            rows(V_C + KT, tiled(ins["c_ctx_2"]), KT)
            rows(V_MEM, tiled(ins["mem_norm_w"]), KT)
            rows(V_NORM, ins["norm_w"].rearrange("l (r c) -> (l r) c", c=P), 2 * KT)
            rows(V_GPRE, ins["g_pre_2"].rearrange("l (r c) -> (l r) c", c=P), 2 * KT)
            gla_w = ins["gla_norm_w"]
            piece(V_GLA, 0, gla_w[:, 0:128])
            piece(V_GLA + 1, 0, gla_w[:, 128:192])
            piece(V_GLA + 1, 64, gla_w[:, 0:64])
            piece(V_GLA + 2, 0, gla_w[:, 64:192])
            n_vec = 10
            for l in range(2):
                sw = ins["diff_subln_g_2"][l:l + 1]
                for r in range(3):
                    f = r * P
                    while f < (r + 1) * P:
                        e = f % DV
                        n = min(DV - e, (r + 1) * P - f)
                        piece(V_SUB + 3 * l + r, f - r * P, sw[:, e:e + n])
                        f += n
                        n_vec += 1
            for r, name in ((V_CB, "conv_b_2"), (V_LG, "conv_ln_g_2"), (V_LB, "conv_ln_b_2")):
                rows(r, ins[name].rearrange("l (r c) -> (l r) c", c=P), 2 * CF)
            act.dma_start(crows, ins["conv_w_2"].rearrange("l k c -> (l k) c")).then_inc(vecs_in, 16)
            n_vec += 4
            assert n_vec * 16 == VECS_IN, n_vec
            act.dma_start(wgu, ins["w_gate_up"][0]).then_inc(gla_in, 16)
            act.dma_start(bgate[:, 0:GH], ins["b_gate"][0].rearrange("(h p) -> p h", p=GK),
                          allow_slow_non_contiguous=True).then_inc(gla_in, 16)
            act.dma_start(gmask, consts["gla_mask"]).then_inc(gla_in, 16)
            act.dma_start(greset, consts["gla_reset"]).then_inc(gla_in, 16)
            act.dma_start(dil_mask[:, :], consts["dil_mask"]).then_inc(const_in, 16)
            act.dma_start(na_mask[:, :, :], consts["na_mask"]).then_inc(const_in, 16)
            act.dma_start(diff_rope[:, :, :, :], consts["diff_rope"]).then_inc(const_in, 16)
            for q, name in enumerate(("diff_lq1_2", "diff_lk1_2", "diff_lq2_2", "diff_lk2_2")):
                act.dma_start(lam_v[:, :, q, :], ins[name].partition_broadcast(P)).then_inc(lam_in, 16)

            for key, _ in steps:
                kind = key[0]
                if kind == "vecT":
                    evacuated(act, key)
                    nc.scalar.activation(siluc[:, :, :].rearrange("p k c -> p c k"),
                                         vec[:, V_C:V_C + 2 * KT].rearrange("p (c k) -> p c k", c=2),
                                         ACT.Silu).then_inc(silu_c, 1)
                    act.wait_ge(lam_dots, 1)
                    nc.scalar.activation(lam_st, lam_st, ACT.Exp).then_inc(lam_exps, 1)
                    act.wait_ge(mem_in, 16)
                    for t in range(CT):
                        square("m", t)
                    act.wait_ge(x_in, 16)
                    for t in range(TT):
                        square("A", t)
                elif kind == "memT":
                    for i in (0, 2):
                        b = full(act, key, i)
                        move(memT[:, 2 * i], b[:, 0:NMEM], vec[:, V_MEM + 2 * i:V_MEM + 2 * i + 1])
                        free(move(memT[:, 2 * i + 1], b[:, NMEM:], vec[:, V_MEM + 2 * i + 1:V_MEM + 2 * i + 2]))
                elif kind == "memkv":
                    for i, dst in enumerate((memk, memv)):
                        free(move(dst[:, key[1]], full(act, key, i)[:, :].rearrange("p (a b) -> p a b", a=2)))
                elif kind == "hT":
                    for k in range(0, KT, 2):
                        b = full(act, key, k)
                        if key[1] in "AB":
                            c = V_NORM + KT * "AB".index(key[1]) + k
                            free(move(hT[:, k], b[:, :], vec[:, c:c + 1]))
                        else:
                            l = int(key[1][1])
                            free(nc.scalar.activation(hT[:, k], b[:, :], ACT.Identity, bias=modv[:, l, 1, k, 0:1],
                                                      scale=modv[:, l, 0, k, 0:1]))
                elif kind == "hcT":
                    l = key[1]
                    for i in (0, 2):
                        b = full(act, key, i)
                        for k in (2 * i, 2 * i + 1):
                            ins_ = nc.scalar.activation(hcT[:, k], b[:, (k % 2) * NMEM:(k % 2 + 1) * NMEM], ACT.Identity,
                                                        bias=modv[:, l, 1, k, 1:2], scale=modv[:, l, 0, k, 1:2])
                        free(ins_)
                elif kind == "Av":
                    for i in range(0, 8, 2):
                        half, t = divmod(i, TT)
                        free(move(gv[:, t, half * 384:half * 384 + 384], full(act, key, i)[:, 0:384]))
                elif kind == "Aglow":
                    free(move(glow, full(act, key, 0)[0:GRANK, :]))
                elif kind == "Aproj":
                    h = key[1]
                    b = h % 2
                    t1, t2, t3, t4 = (gt[:, b, i] for i in range(4))
                    free(move(gq[:, h], full(act, key, 0)[0:GK, :], GK ** -0.5))
                    z = full(act, key, 2)[0:GK, :]
                    if h == 0:
                        act.wait_ge(gla_in, 64)
                    if h >= 2:
                        act.wait_ge(gla_qin, h - 1)
                    nc.scalar.activation(t1, z, ACT.Abs, bias=bgate[:, h:h + 1]).then_inc(gla_abs, 1)
                    act.wait_ge(gla_abs, h + 1)
                    chained(nc.scalar.activation(t1, t1, ACT.Exp, scale=-1.0))
                    nc.scalar.activation(t1, t1, ACT.Ln, bias=1.0).then_inc(gla_soft, 1)
                    act.wait_ge(gla_cum, h + 1)
                    nc.scalar.activation(t1, t3, ACT.Exp, scale=1.0 / GTAU).then_inc(gla_exps, 1)
                    nc.scalar.activation(t2, t3, ACT.Exp, scale=-1.0 / GTAU).then_inc(gla_exps, 1)
                    nc.scalar.activation(t4, t4, ACT.Exp, scale=1.0 / GTAU).then_inc(gla_exps, 1)
                elif kind == "AA":
                    h = key[1]
                    if h >= 2:
                        read_by_pe(act, ("AdS", h - 2))
                    free(move(gkot[:, h % 2], full(act, key, 1)[:, 0:TT * GK].rearrange("p (t d) -> p t d", d=GK)))
                elif kind == "Ao":
                    h = key[1]
                    for i in range(2):
                        b = full(act, key, i)
                        for j in range(2):
                            t = 2 * i + j
                            ins_ = nc.scalar.activation(go[:, t, h * GV:(h + 1) * GV], b[:, j * GV:(j + 1) * GV],
                                                        ACT.Square, accum_out=gla_ss[:, h, t:t + 1])
                        ins_.then_inc(gla_sq, 1)
                        act.wait_ge(gla_rstd, 2 * h + i + 1)
                        for j in range(2):
                            t = 2 * i + j
                            ins_ = move(go[:, t, h * GV:(h + 1) * GV], b[:, j * GV:(j + 1) * GV], gla_rs[:, h, t:t + 1])
                        free(ins_)
                elif kind == "gate":
                    ph, i = key[1:]
                    free(nc.scalar.activation(branch[:, i], full(act, key, 0)[:, :], ACT.Silu))
                    if njobs[key] == 2:
                        free(nc.scalar.activation(cbranch[:, i], full(act, key, 1)[:, 0:NMEM], ACT.Silu))
                elif kind == "qm":
                    free(move(qmem[key[1]][:, 0], full(act, key, 0)[:, :]))
                elif kind == "mS":
                    ph = "AB".index(key[1])
                    for i in range(8):
                        b = bank(key, i)
                        act.wait_ge(mem_negmax, 8 * ph + i + 1)
                        for j in range(2):
                            ins_ = nc.scalar.activation(mprob[:, i, j], b[:, j * NMEM:(j + 1) * NMEM], ACT.Exp,
                                                        bias=m_neg[:, ph, i, j:j + 1], scale=mem_scale,
                                                        accum_out=m_sum[:, ph, i, j:j + 1])
                        free(ins_)
                elif kind == "mT":
                    if key[1] == "B":
                        act.wait_ge(gate_saved, 32)
                    for i in range(0, 8, 2):
                        free(move(mprobT[:, i % 2::2, :, (i // 2) * P:(i // 2 + 1) * P],
                                  full(act, key, i)[:, :].rearrange("p (h k q) -> p h k q", h=2, k=CT)))
                elif kind == "wout":
                    ph = key[1]
                    if ph == "A":
                        for t in range(TT):
                            evacuated(act, key, 2 * t + 1)
                            square("B", t)
                    else:
                        act.wait_ge(xc_in, 16)
                        read_by_pe(act, ("BPV", BH - 1))
                        for t in range(CT):
                            square("c0", t)
                        for t in range(TT):
                            evacuated(act, key, 2 * t + 1)
                            square("F", t)
                        for t in range(TT):
                            act.wait_ge(x_final, t + 1)
                            square("C0", t)
                elif kind == "Bproj":
                    h = key[1]
                    if h >= 2:
                        read_by_pe(act, ("BS", h - 2))
                    for g in range(BG):
                        for s in range(2):
                            b, dst = full(act, key, 3 * g + s), bqk[:, h % 2, g, s]
                            if g == 0:
                                free(move(dst, b[:, :]))
                            else:
                                free(move(dst.rearrange("p (b i) -> p b i", b=DIL), b[:, :].rearrange("p (i b) -> p b i", b=DIL)))
                elif kind == "BS":
                    h = key[1]
                    if h:
                        read_by_pe(act, ("BPV", h - 1))
                    for g in range(BG):
                        free(move(bv[:, g], full(act, key, g)[:, :].rearrange("p (b d) -> p b d", d=BD)))
                    act.wait_ge(dil_negmax, h + 1)
                    for g in range(BG):
                        for n in range(TT):
                            v = bprob_tile(g, n)
                            ins_ = nc.scalar.activation(v, v, ACT.Exp, bias=b_neg[:, h % 2, g, n:n + 1],
                                                        accum_out=b_stat[:, h % 2, g, int(g > 0), 1, n:n + 1])
                    ins_.then_inc(dil_probs, 1)
                elif kind == "BT":
                    h = key[1]
                    act.wait_ge(dil_diff, h + 1)
                    nc.scalar.activation(b_w, b_w, ACT.Exp).then_inc(dil_exp, 1)
                    if h:
                        read_by_pe(act, ("BPV", h - 1))
                    for i in (0, 2):
                        n0, n = PT_BANKS[i]
                        free(move(bprobT[:, n0:n0 + n], full(act, key, i)[:, 0:n * P].rearrange("p (n q) -> p n q", q=P)))
                elif kind == "BPV":
                    h = key[1]
                    if h:
                        act.wait_ge(dil_out, h)
                    free(move(bo12.rearrange("p (i b) -> p b i", b=DIL), full(act, key, 1)[:, :].rearrange("p (b i) -> p b i", b=DIL)))
                elif kind == "nk":
                    for j in range(3):
                        free(move(nkT[:, j, 0:T], full(act, key, j)[:, :]))
                elif kind == "nv":
                    act.wait_ge(x_saved, 16 * (key[1] + 1))
                    for t in range(TT):
                        free(move(vnat[:, t], full(act, key, t)[:, 0:NH * ND]))
                elif kind == "nq":
                    for j in range(3):
                        free(move(nqT[:, j].rearrange("p (n r c) -> p n r c", n=NQB, r=GRID_H),
                                  full(act, key, j)[:, :].rearrange("p (r n c) -> p n r c", r=GRID_H, n=NQB), ND ** -0.5))
                elif kind == "cv":
                    l = key[1]
                    for st, n in ((0, T), (1, NMEM))[0:1 if njobs[key] == 4 else 2]:
                        for f in range(CF):
                            i = 4 * st + 2 * f
                            m = conv_inputs(l, st, f)
                            if m >= 2:
                                evacuated(act, *conv_input_at(m - 2))
                            free(nc.scalar.activation(csig[:, f, 0:n], full(act, key, i)[:, 0:n], ACT.Sigmoid))
                elif kind == "dP":
                    l, what, t = key[1:]
                    if t >= TT:
                        n = stage_at(key)
                        if n >= 2:
                            read_by_pe(act, stage_key(n - 2))
                        free(move(dstage[:, n % 2, :, 0:DD], full(act, key, 0)[:, 0:384].rearrange("p (h d) -> p h d", d=DD)))
                elif kind == "dX":
                    l, what, t = key[1:]
                    dst = dkT[:, :, t * P:(t + 1) * P] if what == "k" else dqT[t // TT][:, :, (t % TT) * P:(t % TT + 1) * P]
                    free(move(dst, full(act, key, 0)[:, :].rearrange("p (h q) -> p h q", q=P)))
                elif kind == "dv":
                    for t in range(0, TT + CT, 2):
                        free(move(dv[:, t], full(act, key, t)[:, 0:384]))
                elif kind == "nS":
                    l, h = key[1:]
                    act.wait_ge(na_negmax, l * NH + h + 1)
                    for n in range(NQB):
                        nc.scalar.activation(nprob[:, n, 0:256], nprob[:, n, 0:256], ACT.Exp, bias=n_neg[:, n:n + 1],
                                             accum_out=n_s[:, 0, n:n + 1])
                        free(nc.scalar.activation(nprob[:, n, 256:512], bank(key, n)[:, 256:512], ACT.Exp,
                                                  bias=n_neg[:, n:n + 1], accum_out=n_s[:, 1, n:n + 1]))
                elif kind == "nT":
                    l, h = key[1:]
                    if h:
                        read_by_pe(act, ("nPV", l, h - 1))
                    else:
                        act.wait_ge(nv_saved, 16 * (l + 1))
                    for n in (0, 2):
                        free(move(nprobT[:, n], full(act, key, n)[:, :].rearrange("p (k q) -> p k q", q=P)))
                elif kind == "cS":
                    l, h = key[1:]
                    if h >= 4:
                        read_by_pe(act, ("cT", l, h - 4))
                    act.wait_ge(ctx_negmax, h + 1)
                    for t in range(CT):
                        ins_ = nc.scalar.activation(cprob[:, h % 4, t], bank(key, 0)[:, t * NMEM:(t + 1) * NMEM], ACT.Exp,
                                                    bias=c_neg[:, h % 2, t:t + 1], accum_out=c_s[:, h % 2, t:t + 1])
                    free(ins_)
                elif kind == "cT":
                    l, h = key[1:]
                    if h >= 4:
                        read_by_pe(act, ("cPV", l, h - 4))
                    free(move(cprobT[:, h % 4].rearrange("p k (t q) -> p t k q", t=CT),
                              full(act, key, 0)[:, :].rearrange("p (t k q) -> p t k q", t=CT, k=CT)))
                elif kind == "dS":
                    l, t, h = key[1:]
                    n = diff_at(l, t, h)
                    if n >= 2:
                        read_by_pe(act, diff_step("dT", n - 2))
                    act.wait_ge(diff_negmax, n + 1)
                    for i in range(njobs[key]):
                        sub, part = i % 2, i // 2
                        lo, w = key_part(t, part)
                        free(nc.scalar.activation(dprob[:, n % 2, sub, lo:lo + w], bank(key, i)[:, 0:w], ACT.Exp,
                                                  bias=d_neg[:, n % 2, sub:sub + 1], scale=diff_scale,
                                                  accum_out=d_s[:, n % 2, i:i + 1]))
                elif kind == "dT":
                    l, t, h = key[1:]
                    n = diff_at(l, t, h)
                    if n >= 2:
                        read_by_pe(act, diff_step("dPV", n - 2))
                    w = 4 if t < TT else 2
                    k0 = 0 if t < TT else TT
                    free(move(dwT[:, n % 2, k0:k0 + w], full(act, key, 0)[:, 0:w * P].rearrange("p (k q) -> p k q", q=P)))
                elif kind == "dPV":
                    l, t, h = key[1:]
                    free(move(otok[t // TT][:, t % TT, h * DV:(h + 1) * DV], full(act, key, 0)[:, 0:DV]))
                elif kind == "cvZ":
                    l, st = key[1:]
                    n = (T, NMEM)[st]
                    for f in range(CF):
                        c = 2 * l + f
                        free(nc.scalar.activation(csilu[st][:, f], full(act, key, f)[:, 0:n], ACT.Silu,
                                                  bias=vec[:, V_LB + c:V_LB + c + 1], scale=vec[:, V_LG + c:V_LG + c + 1]))
                elif kind == "yo":
                    l, t = key[1:]
                    n = l * (TT + CT) + t
                    if n >= 2:
                        act.wait_ge(y_rstd, n - 1)
                    for i in range(2):
                        b = full(act, key, i)
                        if n:
                            act.wait_ge(y_sq, 2 * n - 2 + i + 1)
                        nc.scalar.activation(yjunk[:, i * BANK:(i + 1) * BANK], b[:, :], ACT.Square,
                                             accum_out=y_ss[:, n % 2, i:i + 1]).then_inc(y_sq, 1)
                    if l == 0:
                        act.wait_ge(x_new, t + 1)
                        square("C1" if t < TT else "c1", t % TT)

        @block.vector
        def _(dve):
            count = {"chain": 0}
            taps = {"l": 0, "lat": 0, "ctx": 0}

            def chained(ins_):
                count["chain"] += 1
                ins_.then_inc(dve_chain, 1)
                dve.wait_ge(dve_chain, count["chain"])

            def free(ins_):
                return ins_.then_inc(evac["v"], 1)

            def mul(out, a, b):
                return nc.vector.tensor_tensor(out, a, b, ALU.mult)

            def scaled(out, a, s):
                return nc.vector.tensor_scalar(out, a, s, None, ALU.mult)

            def norm_scale(ph, t):
                src, dst, _, _, rs = norms[ph]
                dve.wait_ge(rstd_ready, norm_at[ph] + t + 1)
                scaled(dst[:, t], src[:, t], rs[:, t:t + 1]).then_inc(xn_ready, 1)

            def conv_taps(l, st, n):
                name = ("lat", "ctx")[st]
                total = CF * TAPS
                src, dst, width = ((u, y, T), (uc, yc, NMEM))[st]
                for _ in range(n):
                    if taps[name] == total:
                        return
                    tap, f = divmod(taps[name], CF)
                    if tap == 0:
                        evacuated(dve, ("cv", l), 4 * st + 2 * f + 1)
                    w = conv_w[:, f, l * TAPS + tap:l * TAPS + tap + 1]
                    cut = src[:, f, tap:tap + width]
                    if tap == 0:
                        c = V_CB + 2 * l + f
                        ins_ = nc.vector.tensor_scalar(dst[:, f], cut, w, vec[:, c:c + 1], ALU.mult, ALU.add)
                    else:
                        ins_ = nc.vector.scalar_tensor_tensor(dst[:, f], cut, w, dst[:, f], ALU.mult, ALU.add)
                    taps[name] += 1
                    if taps[name] == total:
                        ins_.then_inc(conv_done, 1)
                    else:
                        chained(ins_)

            for key, _ in steps:
                kind = key[0]
                if kind == "vecT":
                    free(nc.vector.tensor_copy(vec[:, :], full(dve, key, 0)[:, 0:V_ROWS + 2 * CW_ROWS]))
                    evacuated(dve, key)
                    for l in range(2):
                        chained(scaled(subw[:, l], vec[:, V_SUB + 3 * l:V_SUB + 3 * l + 3], 1.0 - lam_init[l]))
                    dve.wait_ge(lam_in, 64)
                    dve.wait_ge(rpb_saved, 96)
                    for l in range(2):
                        for q in range(2):
                            ins_ = nc.vector.tensor_tensor_reduce(
                                out=lam_junk[:, :], in0=lam_v[:, l, 2 * q], in1=lam_v[:, l, 2 * q + 1], scale=1.0,
                                scalar=0.0, op0=ALU.mult, op1=ALU.add, accum_out=lam_st[:, l, q:q + 1])
                            if (l, q) != (1, 1):
                                chained(ins_)
                    ins_.then_inc(lam_dots, 1)
                    dve.wait_ge(lam_exps, 1)
                    for l in range(2):
                        chained(nc.vector.tensor_tensor(lam[:, l:l + 1], lam_st[:, l, 0:1], lam_st[:, l, 1:2], ALU.subtract))
                        chained(nc.vector.tensor_scalar(lam[:, l:l + 1], lam[:, l:l + 1], lam_init[l], None, ALU.add))
                elif kind == "mod":
                    l, j = key[1:]
                    cut = modrow[:, j * WCOLS:(j + 1) * WCOLS]
                    dve.wait_ge(bmod_in, 32 * (l + 1))
                    free(nc.vector.tensor_tensor(cut, full(dve, key, 0)[0:2, :], cut, ALU.add))
                    if l == 0 and j in (3, 5):
                        ph = "m" if j == 3 else "A"
                        for t in range(norms[ph][2]):
                            norm_scale(ph, t)
                elif kind == "modT":
                    l = key[1]
                    b = full(dve, key, 0)[:, 0:4 * KT].rearrange("p (s k c) -> p s k c", s=2, c=2)
                    nc.vector.tensor_copy(modv[:, l, 1], b[:, 0])
                    gp = vec[:, V_GPRE + l * KT:V_GPRE + (l + 1) * KT].unsqueeze(2).to_broadcast([P, KT, 2])
                    free(nc.vector.scalar_tensor_tensor(modv[:, l, 0], b[:, 1], 1.0, gp, ALU.add, ALU.mult))
                    mul(modrow[:, 2 * D:], modrow[:, 2 * D:], gpost).then_inc(gate_row, 1)
                elif kind == "memT":
                    for i in (1, 3):
                        b = full(dve, key, i)
                        c = V_MEM + 2 * i
                        scaled(memT[:, 2 * i], b[:, 0:NMEM], vec[:, c:c + 1])
                        free(scaled(memT[:, 2 * i + 1], b[:, NMEM:], vec[:, c + 1:c + 2]))
                elif kind == "hT":
                    for k in range(1, KT, 2):
                        b = full(dve, key, k)
                        if key[1] in "AB":
                            c = V_NORM + KT * "AB".index(key[1]) + k
                            free(scaled(hT[:, k], b[:, :], vec[:, c:c + 1]))
                        else:
                            l = int(key[1][1])
                            free(nc.vector.tensor_scalar(hT[:, k], b[:, :], modv[:, l, 0, k, 0:1], modv[:, l, 1, k, 0:1],
                                                         ALU.mult, ALU.add))
                elif kind == "hcT":
                    l = key[1]
                    for i in (1, 3):
                        b = full(dve, key, i)
                        for k in (2 * i, 2 * i + 1):
                            ins_ = nc.vector.tensor_scalar(hcT[:, k], b[:, (k % 2) * NMEM:(k % 2 + 1) * NMEM],
                                                           modv[:, l, 0, k, 1:2], modv[:, l, 1, k, 1:2], ALU.mult, ALU.add)
                        free(ins_)
                elif kind == "Av":
                    for i in range(1, 8, 2):
                        half, t = divmod(i, TT)
                        free(nc.vector.tensor_copy(gv[:, t, half * 384:half * 384 + 384], full(dve, key, i)[:, 0:384]))
                elif kind == "Aproj":
                    h = key[1]
                    b = h % 2
                    t1, t2, t3, t4 = (gt[:, b, i] for i in range(4))
                    free(nc.vector.tensor_copy(gk[:, h], full(dve, key, 1)[0:GK, :]))
                    if h == 0:
                        dve.wait_ge(gla_in, 64)
                    if h >= 2:
                        dve.wait_ge(gla_keys, 2 * (h - 1))
                    dve.wait_ge(gla_abs, h + 1)
                    free(nc.vector.tensor_scalar(t2, full(dve, key, 2)[0:GK, :], bgate[:, h:h + 1], 0.0, ALU.add, ALU.min))
                    evacuated(dve, key, 2)
                    dve.wait_ge(gla_soft, h + 1)
                    chained(nc.vector.tensor_tensor(t2, t2, t1, ALU.subtract))
                    chained(nc.vector.tensor_tensor_scan(t3, greset, t2, 0.0, ALU.mult, ALU.add))
                    by_chunk = lambda v: v.rearrange("p (n c) -> p n c", c=GCHUNK)
                    last = by_chunk(t3)[:, :, GCHUNK - 1:GCHUNK].to_broadcast([GK, T // GCHUNK, GCHUNK])
                    nc.vector.tensor_tensor(by_chunk(t4), last, by_chunk(t3), ALU.subtract).then_inc(gla_cum, 1)
                    dve.wait_ge(gla_exps, 3 * h + 3)
                    nc.vector.tensor_copy(gdec[:, h], by_chunk(t1)[:, :, GCHUNK - 1])
                    evacuated(dve, key, 0)
                    mul(gq[:, h], gq[:, h], t1).then_inc(gla_qin, 1)
                elif kind == "AA":
                    h = key[1]
                    if h == 0:
                        dve.wait_ge(gla_zero, 2)
                    if h >= 2:
                        read_by_pe(dve, ("Ao", h - 2))
                    free(nc.vector.copy_predicated(gA[:, h % 2], gmask.unsqueeze(1).to_broadcast([P, TT, P]),
                                                   full(dve, key, 0)[:, :].rearrange("p (t q) -> p t q", q=P)))
                elif kind == "AdS":
                    h = key[1]
                    if h:
                        read_by_pe(dve, ("Ao", h - 1))
                    for n in range(T // GCHUNK - 1):
                        i, j = DS_BANK[n]
                        b = full(dve, key, i)[0:GK, j * GV:(j + 1) * GV]
                        if n == 0:
                            ins_ = nc.vector.tensor_copy(gS[:, 1], b)
                        else:
                            ins_ = nc.vector.scalar_tensor_tensor(gS[:, n + 1], gS[:, n], gdec[:, h, n:n + 1], b,
                                                                  ALU.mult, ALU.add)
                        if n in DS_LAST:
                            free(ins_)
                            evacuated(dve, key, i)
                        else:
                            chained(ins_)
                elif kind == "qm":
                    free(nc.vector.tensor_copy(qmem[key[1]][:, 1], full(dve, key, 1)[:, :]))
                elif kind == "mS":
                    ph = "AB".index(key[1])

                    def mem_normalise(i):
                        evacuated(dve, key, i)
                        chained(nc.vector.reciprocal(m_rec[:, ph, i], m_sum[:, ph, i]))
                        mul(mprob[:, i], mprob[:, i],
                            m_rec[:, ph, i].unsqueeze(2).to_broadcast([P, 2, NMEM])).then_inc(mem_probs, 1)

                    for i in range(8):
                        b = full(dve, key, i)
                        chained(nc.vector.reduce_max(m_max[:, ph, i], b[:, :].rearrange("p (h m) -> p h m", h=2), AX_X))
                        scaled(m_neg[:, ph, i], m_max[:, ph, i], -mem_scale).then_inc(mem_negmax, 1)
                        if i:
                            mem_normalise(i - 1)
                    mem_normalise(7)
                elif kind == "mT":
                    if key[1] == "B":
                        dve.wait_ge(gate_saved, 32)
                    for i in range(1, 8, 2):
                        free(nc.vector.tensor_copy(mprobT[:, i % 2::2, :, (i // 2) * P:(i // 2 + 1) * P],
                                                   full(dve, key, i)[:, :].rearrange("p (h k q) -> p h k q", h=2, k=CT)))
                elif kind == "mPV":
                    for j in range(2):
                        evacuated(dve, ("gate", key[1], 6 + j))
                        free(mul(branch[:, 6 + j], full(dve, key, j)[:, :], branch[:, 6 + j]))
                elif kind == "AoT":
                    for f in range(6):
                        evacuated(dve, ("gate", "A", f))
                        free(nc.vector.scalar_tensor_tensor(branch[:, f], full(dve, key, f)[:, :],
                                                            vec[:, V_GLA + f % 3:V_GLA + f % 3 + 1], branch[:, f],
                                                            ALU.mult, ALU.mult))
                elif kind == "wout":
                    ph = key[1]
                    for i in range(8):
                        t, n = divmod(i, 2)
                        cut = x[:, t, n * BANK:(n + 1) * BANK]
                        free(nc.vector.tensor_tensor(cut, full(dve, key, i)[:, :], cut, ALU.add))
                    if ph == "A":
                        for t in range(TT):
                            norm_scale("B", t)
                    else:
                        read_by_pe(dve, ("BPV", BH - 1))
                        for pad in (u[:, :, 0:HALO], u[:, :, HALO + T:], uc[:, :, 0:HALO], uc[:, :, HALO + NMEM:],
                                    dstage[:, :, :, DD:]):
                            nc.vector.memset(pad, 0.0)
                        for t in range(CT):
                            norm_scale("c0", t)
                        dve.wait_ge(fw_in, 16)
                        for t in range(TT):
                            dve.wait_ge(rstd_ready, norm_at["F"] + t + 1)
                            nc.vector.scalar_tensor_tensor(x[:, t], x[:, t], norms["F"][4][:, t:t + 1], fw,
                                                           ALU.mult, ALU.mult).then_inc(x_final, 1)
                        for t in range(TT):
                            norm_scale("C0", t)
                elif kind == "Bproj":
                    h = key[1]
                    if h >= 2:
                        read_by_pe(dve, ("BS", h - 2))
                    if h == 0:
                        dve.wait_ge(rope_in, 16)
                    for g in range(BG):
                        b, dst = full(dve, key, 3 * g + 2), bvT[:, h % 2, g]
                        if g == 0:
                            free(nc.vector.tensor_copy(dst, b[:, :]))
                        else:
                            free(nc.vector.tensor_copy(dst.rearrange("p (b i) -> p b i", b=DIL),
                                                       b[:, :].rearrange("p (i b) -> p b i", b=DIL)))
                        evacuated(dve, key, 3 * g + 1)
                        rot = bqk[0:32, h % 2, g]
                        tab = lambda c: dil_rope[:, 2 * (g > 0) + c].unsqueeze(1).to_broadcast([32, 2, T])
                        chained(nc.vector.stream_shuffle(bswap, rot, [(i + 16) % 32 for i in range(32)]))
                        chained(mul(bswap, bswap, tab(1)))
                        chained(mul(rot, rot, tab(0)))
                        nc.vector.tensor_tensor(rot, rot, bswap, ALU.add).then_inc(rope_done, 1)
                        dve.wait_ge(rope_done, BG * h + g + 1)
                elif kind == "BS":
                    h = key[1]
                    p = h % 2
                    if h == 0:
                        dve.wait_ge(const_in, 48)
                    else:
                        read_by_pe(dve, ("BT", h - 1))
                    if h >= 2:
                        dve.wait_ge(st_saved, 48 * (h - 1))
                    for g in range(BG):
                        for n in range(TT):
                            i, lo, m_lo = dil_tile(g, n)
                            v = bprob_tile(g, n)
                            w = v.shape[1]
                            ins_ = nc.vector.tensor_tensor_reduce(
                                out=v, in0=full(dve, key, i)[:, lo:lo + w], in1=dil_mask[:, m_lo:m_lo + w],
                                scale=dil_scale, scalar=-3e38, op0=ALU.add, op1=ALU.max,
                                accum_out=b_stat[:, p, g, int(g > 0), 0, n:n + 1])
                            if n == 3 or (g == 0 and n == 1):
                                free(ins_)
                    evacuated(dve, key, 6)
                    scaled(b_neg[:, p, 0], b_stat[:, p, 0, 0, 0], -1.0)
                    scaled(b_neg[:, p, 1:3], b_stat[:, p, 1:3, 1, 0], -1.0).then_inc(dil_negmax, 1)
                elif kind == "BT":
                    h = key[1]
                    p = h % 2
                    dve.wait_ge(dil_probs, h + 1)
                    dve.wait_ge(st_in, 48 * (h + 1))
                    top, bot = b_stat[:, p, :, :, 0], b_stat[:, p, :, :, 1]
                    chained(nc.vector.tensor_tensor(b_top, top[:, 0], top[:, 1], ALU.max))
                    chained(nc.vector.tensor_tensor(b_top, b_top, top[:, 2], ALU.max))
                    nc.vector.tensor_tensor(b_w, top, b_top.unsqueeze(1).to_broadcast([P, BG, 2, TT]),
                                            ALU.subtract).then_inc(dil_diff, 1)
                    dve.wait_ge(dil_exp, h + 1)
                    chained(mul(bot, bot, b_w))
                    chained(nc.vector.tensor_tensor(b_rec, bot[:, 0], bot[:, 1], ALU.add))
                    chained(nc.vector.tensor_tensor(b_rec, b_rec, bot[:, 2], ALU.add))
                    chained(nc.vector.reciprocal(b_rec, b_rec))
                    chained(mul(b_w, b_w, b_rec.unsqueeze(1).to_broadcast([P, BG, 2, TT])))
                    scaled(bprob[:, P:2 * P], bprob[:, P:2 * P], b_w[:, 0, 0, 0:1])
                    v = bprob[:, 2 * P:8 * P].rearrange("p (n k) -> p n k", n=3)
                    mul(v, v, b_w[:, 0, 0, 1:4].unsqueeze(2).to_broadcast([P, 3, 2 * P]))
                    v = bprob[:, 8 * P:].rearrange("p (g n k) -> p g n k", g=2, n=TT)
                    mul(v, v, b_w[:, 1:3, 1].unsqueeze(3).to_broadcast([P, 2, TT, P])).then_inc(dil_weighted, 1)
                    if h:
                        read_by_pe(dve, ("BPV", h - 1))
                    for i in (1, 3):
                        n0, n = PT_BANKS[i]
                        free(nc.vector.tensor_copy(bprobT[:, n0:n0 + n],
                                                   full(dve, key, i)[:, 0:n * P].rearrange("p (n q) -> p n q", q=P)))
                elif kind == "BPV":
                    h = key[1]
                    evacuated(dve, key, 1)
                    if h:
                        dve.wait_ge(dil_out, h)
                    free(nc.vector.tensor_tensor(bsum, full(dve, key, 0)[:, :], bo12, ALU.add))
                    evacuated(dve, key, 0)
                    evacuated(dve, ("gate", "B", h))
                    mul(branch[:, h], branch[:, h], bsum).then_inc(dil_out, 1)
                elif kind == "nk":
                    taps.update(lat=0, ctx=0)
                    for j in range(3):
                        free(nc.vector.tensor_copy(nkT[:, j, T:], full(dve, key, 3 + j)[:, 0:NMEM]))
                elif kind == "nv":
                    for t in range(CT):
                        free(nc.vector.tensor_copy(vctx[:, t], full(dve, key, TT + t)[:, 0:NH * ND]))
                elif kind == "nq":
                    for j in range(3, njobs[key]):
                        free(scaled(nqcT[:, j - 3], full(dve, key, j)[:, 0:NMEM], ND ** -0.5))
                elif kind == "cv":
                    l = key[1]
                    for st in range(njobs[key] // 4):
                        n, dst = ((T, u), (NMEM, uc))[st]
                        for f in range(CF):
                            i = 4 * st + 2 * f
                            evacuated(dve, key, i)
                            free(mul(dst[:, f, HALO:HALO + n], full(dve, key, i + 1)[:, 0:n], csig[:, f, 0:n]))
                elif kind == "gate" and key[1][0] == "C":
                    conv_taps(int(key[1][1]), 0, 6)
                elif kind == "dP":
                    l, what, t = key[1:]
                    if t < TT:
                        n = stage_at(key)
                        if n >= 2:
                            read_by_pe(dve, stage_key(n - 2))
                        b = full(dve, key, 0)[:, 0:384]
                        st = dstage[:, n % 2, :, 0:DD]
                        cos = diff_rope[:, 0, t].unsqueeze(1).to_broadcast([P, 2 * DH, DD])
                        chained(mul(st, b.rearrange("p (h d) -> p h d", d=DD), cos))
                        pairs = b.rearrange("p (h a r d) -> p h a r d", h=2 * DH, a=2, r=2)
                        swap = dswap.rearrange("p h (a r d) -> p h a r d", a=2, r=2)
                        sin = diff_rope[:, 1, t].rearrange("p (a r d) -> p a r d", a=2, r=2)
                        for r in range(2):
                            ins_ = mul(swap[:, :, :, r], pairs[:, :, :, 1 - r],
                                       sin[:, :, r].unsqueeze(1).to_broadcast([P, 2 * DH, 2, DD // 4]))
                        free(ins_)
                        evacuated(dve, key)
                        nc.vector.tensor_tensor(st, st, dswap, ALU.add).then_inc(diff_staged, 1)
                        dve.wait_ge(diff_staged, roped_at(key) + 1)
                elif kind == "dv":
                    for t in range(1, TT + CT, 2):
                        free(nc.vector.tensor_copy(dv[:, t], full(dve, key, t)[:, 0:384]))
                elif kind == "nS":
                    l, h = key[1:]
                    dve.wait_ge(bias_ready, l * NH + h + 1)
                    if h:
                        read_by_pe(dve, ("nT", l, h - 1))
                    else:
                        dve.wait_ge(x_saved, 16 * (l + 1))
                    for n in range(NQB):
                        b = full(dve, key, n)
                        chained(nc.vector.reduce_max(n_ctx[:, n:n + 1], b[:, 256:512], AX_X))
                        ins_ = nc.vector.tensor_tensor_reduce(
                            out=nprob[:, n, 0:256], in0=b[:, 0:256], in1=bias[:, h % 2, BIAS_KIND[n]], scale=1.0,
                            scalar=n_ctx[:, n:n + 1], op0=ALU.add, op1=ALU.max, accum_out=n_max[:, n:n + 1])
                    chained(ins_)
                    scaled(n_neg, n_max, -1.0).then_inc(na_negmax, 1)
                    conv_taps(l, 0, 5)
                elif kind == "nT":
                    l, h = key[1:]
                    evacuated(dve, ("nS", l, h))
                    chained(nc.vector.tensor_tensor(n_rec[:, 0], n_s[:, 0], n_s[:, 1], ALU.add))
                    chained(nc.vector.reciprocal(n_rec[:, 1], n_rec[:, 0]))
                    for n in range(NQB):
                        ins_ = scaled(nprob[:, n], nprob[:, n], n_rec[:, 1, n:n + 1])
                    ins_.then_inc(na_probs, 1)
                    if h:
                        read_by_pe(dve, ("nPV", l, h - 1))
                    else:
                        dve.wait_ge(nv_saved, 16 * (l + 1))
                    for n in (1, 3):
                        free(nc.vector.tensor_copy(nprobT[:, n], full(dve, key, n)[:, :].rearrange("p (k q) -> p k q", q=P)))
                elif kind == "nPV":
                    l, h = key[1:]
                    lo = 64 * (h % 2)
                    evacuated(dve, ("gate", f"C{l}", h // 2), 0)
                    v = branch[lo:lo + 64, h // 2].rearrange("p (r n c) -> p n r c", r=GRID_H, n=NQB)
                    b = full(dve, key, 0)[lo:lo + 64, :].rearrange("p (n r c) -> p n r c", n=NQB, r=GRID_H)
                    free(mul(v, b, v))
                elif kind == "cS":
                    l, h = key[1:]
                    b = full(dve, key, 0)
                    if h >= 2:
                        evacuated(dve, ("cS", l, h - 2))
                    chained(nc.vector.reduce_max(c_max[:, h % 2], b[:, :].rearrange("p (t k) -> p t k", t=CT), AX_X))
                    scaled(c_neg[:, h % 2], c_max[:, h % 2], -1.0).then_inc(ctx_negmax, 1)
                elif kind == "cT":
                    l, h = key[1:]
                    evacuated(dve, ("cS", l, h))
                    chained(nc.vector.reciprocal(c_rec[:, h % 2], c_s[:, h % 2]))
                    v = cprob[:, h % 4]
                    mul(v, v, c_rec[:, h % 2].unsqueeze(2).to_broadcast([P, CT, NMEM])).then_inc(ctx_probs, 1)
                elif kind == "cPV":
                    l, h = key[1:]
                    lo = 64 * (h % 2)
                    evacuated(dve, ("gate", f"C{l}", h // 2), 1)
                    v = cbranch[lo:lo + 64, h // 2]
                    free(mul(v, full(dve, key, 0)[lo:lo + 64, 0:NMEM], v))
                elif kind == "dS":
                    l, t, h = key[1:]
                    n = diff_at(l, t, h)
                    p = n % 2
                    for i in range(njobs[key]):
                        _, w = key_part(t, i // 2)
                        ins_ = nc.vector.reduce_max(d_max[:, p, i:i + 1], full(dve, key, i)[:, 0:w], AX_X)
                    chained(ins_)
                    if t < TT:
                        chained(nc.vector.tensor_tensor(d_max[:, p, 0:2], d_max[:, p, 0:2], d_max[:, p, 2:4], ALU.max))
                    scaled(d_neg[:, p, 0:2], d_max[:, p, 0:2], -diff_scale).then_inc(diff_negmax, 1)
                    conv_taps(l, 0, 4)
                    if l == 0 and taps["lat"] == CF * TAPS:
                        read_by_pe(dve, ("dP", l, "q", TT + CT - 1))
                        conv_taps(l, 1, 6)
                elif kind == "dT":
                    l, t, h = key[1:]
                    n = diff_at(l, t, h)
                    p = n % 2
                    evacuated(dve, ("dS", l, t, h))
                    rec, s = d_rec[:, p], d_s[:, p]
                    if t < TT:
                        chained(nc.vector.tensor_tensor(s[:, 0:2], s[:, 0:2], s[:, 2:4], ALU.add))
                    chained(nc.vector.reciprocal(rec[:, 0:2], s[:, 0:2]))
                    chained(mul(rec[:, 2:3], rec[:, 1:2], lam[:, l:l + 1]))
                    k0 = 0 if t < TT else T
                    p1, p2 = dprob[:, p, 0, k0:], dprob[:, p, 1, k0:]
                    chained(scaled(p2, p2, rec[:, 2:3]))
                    nc.vector.scalar_tensor_tensor(p1, p1, rec[:, 0:1], p2, ALU.mult, ALU.subtract).then_inc(diff_w, 1)
                    if t < TT:
                        if n >= 2:
                            read_by_pe(dve, diff_step("dPV", n - 2))
                        free(nc.vector.tensor_copy(dwT[:, p, TT:], full(dve, key, 1)[:, 0:2 * P].rearrange("p (k q) -> p k q", q=P)))
                elif kind == "dPV":
                    l, t, h = key[1:]
                    if h == DH - 1:
                        n = diff_tile(l, t)
                        o = otok[t // TT][:, t % TT]
                        evacuated(dve, key)
                        sq = dswap.rearrange("p h d -> p (h d)")
                        chained(mul(sq, o, o))
                        nc.vector.tensor_reduce(o_ss[:, t], sq.rearrange("p (h d) -> p h d", d=DV), AX_X,
                                                ALU.add).then_inc(o_sq, 1)
                        dve.wait_ge(o_rstd, n + 1)
                        v = o.rearrange("p (h d) -> p h d", d=DV)
                        mul(v, v, o_rs[:, t].unsqueeze(2).to_broadcast([P, DH, DV])).then_inc(o_normed, 1)
                elif kind == "doT":
                    l, st = key[1:]
                    n, dst = ((T, branch), (NMEM, cbranch))[st]
                    for f in range(3):
                        evacuated(dve, ("gate", f"C{l}", 3 + f), st)
                        free(nc.vector.scalar_tensor_tensor(dst[:, 3 + f], full(dve, key, f)[:, 0:n], subw[:, l, f:f + 1],
                                                            dst[:, 3 + f], ALU.mult, ALU.mult))
                elif kind == "cvT":
                    l, st = key[1:]
                    conv_taps(l, st, CF * TAPS)
                    for i in range((TT, CT)[st] // 2):
                        b = full(dve, key, i)
                        n = ln_pair(l, st, i)
                        for j in range(2):
                            chained(nc.vector.bn_stats(ln_st, b[:, j * CW:(j + 1) * CW]))
                            ins_ = nc.vector.bn_aggr(ln_mv[:, j], ln_st)
                            if j == 0:
                                chained(ins_)
                        ins_.then_inc(ln_var, 1)
                        dve.wait_ge(ln_rstd, n + 1)
                        for j in range(2):
                            ins_ = nc.vector.tensor_scalar(czn[st][:, 2 * i + j], b[:, j * CW:(j + 1) * CW],
                                                           ln_mv[:, j, 0:1], ln_rs[:, j:j + 1], ALU.subtract, ALU.mult)
                        free(ins_)
                        evacuated(dve, key, i)
                elif kind == "cvZ":
                    l, st = key[1:]
                    dst = (branch, cbranch)[st]
                    for f in range(CF):
                        evacuated(dve, key, f)
                        evacuated(dve, ("gate", f"C{l}", 6 + f), st)
                        mul(dst[:, 6 + f], dst[:, 6 + f], csilu[st][:, f]).then_inc(ln_done, 1)
                elif kind == "yo":
                    l, t = key[1:]
                    n = l * (TT + CT) + t
                    c = t // TT
                    row = x[:, t] if t < TT else xc[:, t - TT]
                    dve.wait_ge(y_rstd, n + 1)
                    dve.wait_ge(gmul_in, 32 * (l + 1))
                    if t < TT:
                        dve.wait_ge(x_back, 16 * (l + 1))
                    if n:
                        dve.wait_ge(x_new, n)
                    for i in range(2):
                        cut = slice(i * BANK, (i + 1) * BANK)
                        free(nc.vector.scalar_tensor_tensor(ytmp[:, cut], full(dve, key, i)[:, :], y_rs[:, n % 2, 1:2],
                                                            gmul[:, c, cut], ALU.mult, ALU.mult))
                    evacuated(dve, key)
                    nc.vector.tensor_tensor(row, row, ytmp, ALU.add).then_inc(x_new, 1)
                    if l == 0:
                        norm_scale("C1" if t < TT else "c1", t % TT)

        @block.tensor
        def _(pe):
            def done(ins_):
                ins_.then_inc(psum_full, 1)

            def product(out, pairs):
                pairs = list(pairs)
                for i, (lhsT, rhs) in enumerate(pairs):
                    ins_ = nc.tensor.matmul(out, lhsT, rhs, start=i == 0, stop=i == len(pairs) - 1)
                return ins_

            def features(out, w, c0, m, rhs):
                return product(out, ((w[:, k, c0:c0 + m], rhs[:, k]) for k in range(KT)))

            def tokens(out, lhs, t, w, c0, n):
                return product(out, ((lhs[:, k, t * P:(t + 1) * P], w[:, k, c0:c0 + n]) for k in range(KT)))

            def turn(out, in_):
                n = in_.shape[0]
                return nc.tensor.transpose(out, in_, ident[0:n, 0:n])

            def norm_in(ph):
                pe.wait_ge(xn_ready, norm_pe[ph])

            for key, _ in steps:
                kind = key[0]
                if kind == "vecT":
                    pe.wait_ge(vecs_in, VECS_IN)
                    b = claim(pe, key, 0)
                    turn(b[:, 0:V_ROWS], vrows)
                    for f in range(CF):
                        ins_ = turn(b[:, V_ROWS + f * CW_ROWS:V_ROWS + (f + 1) * CW_ROWS], crows[:, f * P:(f + 1) * P])
                    done(ins_)
                elif kind == "mod":
                    l, j = key[1:]
                    pe.wait_ge(silu_c, 1)
                    w = chunk(pe, key)
                    b = claim(pe, key, 0)
                    done(product(b[0:2, :], ((siluc[:, k], w[:, k]) for k in range(KT))))
                elif kind == "modT":
                    l = key[1]
                    evacuated(pe, ("mod", l, 5))
                    b = claim(pe, key, 0)
                    for c in range(2 * KT):
                        ins_ = turn(b[:, 2 * c:2 * c + 2], modrow[:, c * P:(c + 1) * P])
                    done(ins_)
                elif kind == "memT":
                    norm_in("m")
                    for i in range(4):
                        b = claim(pe, key, i)
                        for j in range(2):
                            k = 2 * i + j
                            for t in range(CT):
                                ins_ = turn(b[:, j * NMEM + t * P:j * NMEM + (t + 1) * P], memn[:, t, k * P:(k + 1) * P])
                        done(ins_)
                elif kind == "memkv":
                    l = key[1]
                    w = chunk(pe, key)
                    if l == 0:
                        evacuated(pe, ("memT",), 2)
                        evacuated(pe, ("memT",), 3)
                    b = claim(pe, key, 0)
                    for j in range(2):
                        ins_ = features(b[:, j * NMEM:(j + 1) * NMEM], w, j * P, P, memT)
                    done(ins_)
                    b = claim(pe, key, 1)
                    for t in range(CT):
                        ins_ = tokens(b[:, t * 256:(t + 1) * 256], memT, t, w, 256, 256)
                    done(ins_)
                elif kind == "hT":
                    norm_in(key[1])
                    src = norms[key[1]][1]
                    for k in range(KT):
                        b = claim(pe, key, k)
                        for t in range(TT):
                            ins_ = turn(b[:, t * P:(t + 1) * P], src[:, t, k * P:(k + 1) * P])
                        done(ins_)
                    evacuated(pe, key, 6)
                    evacuated(pe, key, 7)
                elif kind == "hcT":
                    norm_in(f"c{key[1]}")
                    for i in range(4):
                        b = claim(pe, key, i)
                        for j in range(2):
                            k = 2 * i + j
                            for t in range(CT):
                                ins_ = turn(b[:, j * NMEM + t * P:j * NMEM + (t + 1) * P], cxcn[:, t, k * P:(k + 1) * P])
                        done(ins_)
                    evacuated(pe, key, 2)
                    evacuated(pe, key, 3)
                elif kind == "Av":
                    for i in range(8):
                        half, t = divmod(i, TT)
                        w = chunk(pe, ("Av", half))
                        b = claim(pe, key, i)
                        done(tokens(b[:, 0:384], hT, t, w, 0, 384))
                elif kind == "Aglow":
                    w = chunk(pe, ("Av", 1))
                    done(features(claim(pe, key, 0)[0:GRANK, :], w, 384, GRANK, hT))
                elif kind == "Aproj":
                    h = key[1]
                    for i, name in enumerate(("Aq", "Ak")):
                        w = chunk(pe, (name,))
                        done(features(claim(pe, key, i)[0:GK, :], w, h * GK, GK, hT))
                    if h == 0:
                        pe.wait_ge(gla_in, 64)
                        evacuated(pe, ("Aglow",))
                    done(product(claim(pe, key, 2)[0:GK, :], [(wgu[:, h * GK:(h + 1) * GK], glow)]))
                elif kind == "AA":
                    h = key[1]
                    pe.wait_ge(gla_qin, h + 1)
                    pe.wait_ge(gla_keys, 2 * h + 2)
                    b = claim(pe, key, 0)
                    for t in range(TT):
                        cut = slice(t * P, (t + 1) * P)
                        ins_ = product(b[:, cut], [(gkin[:, h % 2, cut], gq[:, h, cut])])
                    done(ins_)
                    b = claim(pe, key, 1)
                    for t in range(TT):
                        ins_ = turn(b[:, t * GK:(t + 1) * GK], gkout[:, h % 2, t * P:(t + 1) * P])
                    done(ins_)
                elif kind == "AdS":
                    h = key[1]
                    evacuated(pe, ("AA", h), 1)
                    if h == 0:
                        evacuated(pe, ("Av",), 6)
                        evacuated(pe, ("Av",), 7)
                    for i in range(4):
                        b = claim(pe, key, i)
                        for n in range(T // GCHUNK - 1):
                            if DS_BANK[n][0] != i:
                                continue
                            t, half = divmod(n, 2)
                            lo = half * GCHUNK
                            ins_ = product(b[0:GK, DS_BANK[n][1] * GV:(DS_BANK[n][1] + 1) * GV],
                                           [(gkot[lo:lo + GCHUNK, h % 2, t], gv[lo:lo + GCHUNK, t, h * GV:(h + 1) * GV])])
                        done(ins_)
                elif kind == "Ao":
                    h = key[1]
                    evacuated(pe, ("AA", h), 0)
                    evacuated(pe, ("AdS", h), 3)
                    for i in range(2):
                        b = claim(pe, key, i)
                        for t in (2 * i, 2 * i + 1):
                            o = b[:, (t % 2) * GV:(t % 2 + 1) * GV]
                            ins_ = nc.tensor.matmul(o, gA[:, h % 2, t], gv[:, t, h * GV:(h + 1) * GV], start=True, stop=False)
                            for half in range(2):
                                lo = half * GCHUNK
                                ins_ = nc.tensor.matmul(o[lo:lo + GCHUNK], gq[:, h, t * P + lo:t * P + lo + GCHUNK],
                                                        gS[:, 2 * t + half], start=False, stop=True)
                        done(ins_)
                elif kind == "gate":
                    ph, i = key[1:]
                    name, c0 = gate_chunk(ph, i)
                    w = chunk(pe, name)
                    done(features(claim(pe, key, 0)[:, :], w, c0, P, hT))
                    if njobs[key] == 2:
                        done(features(claim(pe, key, 1)[:, 0:NMEM], w, c0, P, hcT))
                elif kind == "qm":
                    w = chunk(pe, key)
                    for j in range(2):
                        done(features(claim(pe, key, j)[:, :], w, j * P, P, hT))
                elif kind == "mS":
                    ph = key[1]
                    l = "AB".index(ph)
                    evacuated(pe, ("qm", ph), 0)
                    evacuated(pe, ("qm", ph), 1)
                    for i in range(8):
                        t, odd = divmod(i, 2)
                        lo = odd * MD
                        b = claim(pe, key, i)
                        for j in range(2):
                            ins_ = product(b[:, j * NMEM:(j + 1) * NMEM], [(qmem[ph][lo:lo + MD, j, t * P:(t + 1) * P],
                                                                            memk[lo:lo + MD, l, j])])
                        done(ins_)
                elif kind == "mT":
                    ph = key[1]
                    for i in range(8):
                        pe.wait_ge(mem_probs, 8 * "AB".index(ph) + i + 1)
                        b = claim(pe, key, i)
                        for j in range(2):
                            for k in range(CT):
                                ins_ = turn(b[:, (j * CT + k) * P:(j * CT + k + 1) * P], mprob[:, i, j, k * P:(k + 1) * P])
                        done(ins_)
                elif kind == "mPV":
                    ph = key[1]
                    l = "AB".index(ph)
                    evacuated(pe, ("mT", ph), 6)
                    evacuated(pe, ("mT", ph), 7)
                    for j in range(2):
                        b = claim(pe, key, j)
                        for h in (2 * j, 2 * j + 1):
                            lo = (h % 2) * MD
                            ins_ = product(b[lo:lo + MD, :], ((memv[:, l, k, h * MD:(h + 1) * MD], mprobT[:, h, k])
                                                              for k in range(CT)))
                        done(ins_)
                elif kind == "AoT":
                    evacuated(pe, ("Ao", GH - 1))
                    for f in range(6):
                        b = claim(pe, key, f)
                        for t in range(TT):
                            ins_ = turn(b[:, t * P:(t + 1) * P], go[:, t, f * P:(f + 1) * P])
                        done(ins_)
                elif kind == "wout":
                    ph = key[1]
                    evacuated(pe, ("mPV", ph), 1)
                    if ph == "A":
                        evacuated(pe, ("AoT",), 5)
                    else:
                        pe.wait_ge(dil_out, BH)
                    for i in range(8):
                        t, n = divmod(i, 2)
                        w = chunk(pe, ("wout", ph, n))
                        done(tokens(claim(pe, key, i)[:, :], branch, t, w, 0, WCOLS))
                elif kind == "Bproj":
                    h = key[1]
                    for g in range(BG):
                        w = chunk(pe, ("Bproj", h, g))
                        for s in range(3):
                            done(features(claim(pe, key, 3 * g + s)[:, :], w, s * BD, BD, hT))
                elif kind == "BS":
                    h = key[1]
                    p = h % 2
                    for g in range(BG):
                        evacuated(pe, ("Bproj", h), 3 * g + 2)
                        b = claim(pe, key, g)
                        for n in range(TT):
                            ins_ = turn(b[:, n * P:(n + 1) * P], bvT[:, p, g, n * P:(n + 1) * P])
                        done(ins_)
                    pe.wait_ge(rope_done, BG * (h + 1))
                    for i in range(3, 7):
                        b = claim(pe, key, i)
                        for g in range(BG):
                            for n in range(TT):
                                at_, lo, _ = dil_tile(g, n)
                                if at_ == i:
                                    w = bprob_tile(g, n).shape[1]
                                    ins_ = product(b[:, lo:lo + w], [(bqk[:, p, g, 0, n * P:(n + 1) * P],
                                                                      bqk[:, p, g, 1, (n + 1) * P - w:(n + 1) * P])])
                        done(ins_)
                elif kind == "BT":
                    h = key[1]
                    pe.wait_ge(dil_weighted, h + 1)
                    for i, (n0, n) in enumerate(PT_BANKS):
                        b = claim(pe, key, i)
                        for j in range(n):
                            lo = PT_TILES[n0 + j] * P
                            ins_ = turn(b[:, j * P:(j + 1) * P], bprob[:, lo:lo + P])
                        done(ins_)
                elif kind == "BPV":
                    h = key[1]
                    for i in range(4):
                        evacuated(pe, ("BT", h), i)
                    evacuated(pe, ("BS", h), 2)
                    b = claim(pe, key, 0)
                    for n in range(TT):
                        pairs = [(bv[:, 0, n], bprobT[:, 2 * n])]
                        if n:
                            pairs.append((bv[:, 0, n - 1], bprobT[:, 2 * n - 1]))
                        ins_ = product(b[:, n * P:(n + 1) * P], pairs)
                    done(ins_)
                    b = claim(pe, key, 1)
                    for n in range(TT):
                        ins_ = product(b[:, n * P:(n + 1) * P], [(bv[:, 1, n], bprobT[:, 7 + n]), (bv[:, 2, n], bprobT[:, 11 + n])])
                    done(ins_)
                elif kind in ("nk", "nq"):
                    w = chunk(pe, key)
                    for j in range(njobs[key]):
                        b = claim(pe, key, j)
                        if j < 3:
                            done(features(b[:, :], w, j * P, P, hT))
                        else:
                            done(features(b[:, 0:NMEM], w, (j - 3) * P, P, hcT))
                elif kind in ("nv", "dv"):
                    w = chunk(pe, key)
                    for t in range(TT + CT):
                        src, tt = (hT, t) if t < TT else (hcT, t - TT)
                        done(tokens(claim(pe, key, t)[:, 0:384], src, tt, w, 0, 384))
                elif kind == "cv":
                    w = chunk(pe, key)
                    for st in range(njobs[key] // 4):
                        n, src = ((T, hT), (NMEM, hcT))[st]
                        for f in range(CF):
                            done(features(claim(pe, key, 4 * st + 2 * f)[:, 0:n], w, CW + f * P, P, src))
                            done(features(claim(pe, key, 4 * st + 2 * f + 1)[:, 0:n], w, f * P, P, src))
                elif kind == "dP":
                    l, what, t = key[1:]
                    w = chunk(pe, ("d" + what, l))
                    src, tt = (hT, t) if t < TT else (hcT, t - TT)
                    done(tokens(claim(pe, key, 0)[:, 0:384], src, tt, w, 0, 384))
                elif kind == "dX":
                    l, what, t = key[1:]
                    key_p = ("dP", l, what, t)
                    if t < TT:
                        pe.wait_ge(diff_staged, roped_at(key_p) + 1)
                    else:
                        evacuated(pe, key_p)
                    b = claim(pe, key, 0)
                    n = stage_at(key_p)
                    for h in range(DH):
                        ins_ = turn(b[:, h * P:(h + 1) * P], dstage[:, n % 2, 2 * h:2 * h + 2].rearrange("p s d -> p (s d)"))
                    done(ins_)
                elif kind == "nS":
                    l, h = key[1:]
                    lo, j = 64 * (h % 2), h // 2
                    if h == 0:
                        evacuated(pe, ("nk", l), 2)
                        evacuated(pe, ("nk", l), 5)
                        evacuated(pe, ("nq", l), 2)
                    k = nkT[lo:lo + ND, j, 0:T].rearrange("p (r c) -> p r c", c=GRID_W)
                    for n in range(NQB):
                        b = claim(pe, key, n)
                        qn = nqT[lo:lo + ND, j, n * P:(n + 1) * P]
                        product(b[:, 0:256], [(qn, k[:, :, STRIP_START[n]:STRIP_START[n] + STRIP])])
                        done(product(b[:, 256:512], [(qn, nkT[lo:lo + ND, j, T:])]))
                elif kind == "nT":
                    l, h = key[1:]
                    pe.wait_ge(na_probs, l * NH + h + 1)
                    for n in range(NQB):
                        b = claim(pe, key, n)
                        for k in range(4):
                            ins_ = turn(b[:, k * P:(k + 1) * P], nprob[:, n, k * P:(k + 1) * P])
                        done(ins_)
                elif kind == "nPV":
                    l, h = key[1:]
                    lo = 64 * (h % 2)
                    if h == 0:
                        pe.wait_ge(strips_in, 512 * (l + 1))
                        evacuated(pe, ("nv", l), 5)
                    evacuated(pe, ("nT", l, h), 2)
                    evacuated(pe, ("nT", l, h), 3)
                    b = claim(pe, key, 0)
                    cut = slice(h * ND, (h + 1) * ND)
                    for n in range(NQB):
                        v = [vstrip[:, n, 0, cut], vstrip[:, n, 1, cut], vctx[:, 0, cut], vctx[:, 1, cut]]
                        ins_ = product(b[lo:lo + ND, n * P:(n + 1) * P], ((v[k], nprobT[:, n, k]) for k in range(4)))
                    done(ins_)
                elif kind == "cS":
                    l, h = key[1:]
                    lo, j = 64 * (h % 2), h // 2
                    if h == 0:
                        evacuated(pe, ("nq", l), 5)
                    b = claim(pe, key, 0)
                    for t in range(CT):
                        ins_ = product(b[:, t * NMEM:(t + 1) * NMEM], [(nqcT[lo:lo + ND, j, t * P:(t + 1) * P],
                                                                        nkT[lo:lo + ND, j, T:])])
                    done(ins_)
                elif kind == "cT":
                    l, h = key[1:]
                    pe.wait_ge(ctx_probs, h + 1)
                    b = claim(pe, key, 0)
                    for t in range(CT):
                        for k in range(CT):
                            ins_ = turn(b[:, (t * CT + k) * P:(t * CT + k + 1) * P], cprob[:, h % 4, t, k * P:(k + 1) * P])
                    done(ins_)
                elif kind == "cPV":
                    l, h = key[1:]
                    lo = 64 * (h % 2)
                    evacuated(pe, ("cT", l, h))
                    b = claim(pe, key, 0)
                    done(product(b[lo:lo + ND, 0:NMEM], ((vctx[:, k, h * ND:(h + 1) * ND], cprobT[:, h % 4, k]) for k in range(CT))))
                elif kind == "dS":
                    l, t, h = key[1:]
                    evacuated(pe, ("dX", l, "q", t))
                    if (t, h) == (0, 0):
                        evacuated(pe, ("dX", l, "k", TT + CT - 1))
                    for i in range(njobs[key]):
                        lo = (i % 2) * DPAD
                        k0, w = key_part(t, i // 2)
                        b = claim(pe, key, i)
                        q = dqT[t // TT][lo:lo + DD, h, (t % TT) * P:(t % TT + 1) * P]
                        done(product(b[:, 0:w], [(q, dkT[lo:lo + DD, h, k0:k0 + w])]))
                elif kind == "dT":
                    l, t, h = key[1:]
                    n = diff_at(l, t, h)
                    pe.wait_ge(diff_w, n + 1)
                    k0 = 0 if t < TT else TT
                    for i in range(njobs[key]):
                        b = claim(pe, key, i)
                        w = 4 if (t < TT and i == 0) else 2
                        for j in range(w):
                            k = k0 + 4 * i + j
                            ins_ = turn(b[:, j * P:(j + 1) * P], dprob[:, n % 2, 0, k * P:(k + 1) * P])
                        done(ins_)
                elif kind == "dPV":
                    l, t, h = key[1:]
                    n = diff_at(l, t, h)
                    if (t, h) == (0, 0):
                        evacuated(pe, ("dv", l), 4)
                        evacuated(pe, ("dv", l), 5)
                    for i in range(njobs[("dT", l, t, h)]):
                        evacuated(pe, ("dT", l, t, h), i)
                    b = claim(pe, key, 0)
                    tiles = range(TT + CT) if t < TT else range(TT, TT + CT)
                    done(product(b[:, 0:DV], ((dwT[:, n % 2, k], dv[:, k, h * DV:(h + 1) * DV]) for k in tiles)))
                elif kind == "doT":
                    l, st = key[1:]
                    nt = (TT, CT)[st]
                    pe.wait_ge(o_normed, diff_tile(l, (TT if st == 0 else TT + CT) - 1) + 1)
                    for f in range(3):
                        b = claim(pe, key, f)
                        for t in range(nt):
                            ins_ = turn(b[:, t * P:(t + 1) * P], otok[st][:, t, f * P:(f + 1) * P])
                        done(ins_)
                elif kind == "cvT":
                    l, st = key[1:]
                    pe.wait_ge(conv_done, 1 + st if l == 0 else 3)
                    src = (y, yc)[st]
                    for i in range((TT, CT)[st] // 2):
                        b = claim(pe, key, i)
                        for j in range(2):
                            t = 2 * i + j
                            for f in range(CF):
                                ins_ = turn(b[:, j * CW + f * P:j * CW + (f + 1) * P], src[:, f, t * P:(t + 1) * P])
                        done(ins_)
                elif kind == "cvZ":
                    l, st = key[1:]
                    nt = (TT, CT)[st]
                    evacuated(pe, ("cvT", l, st))
                    for f in range(CF):
                        b = claim(pe, key, f)
                        for t in range(nt):
                            ins_ = turn(b[:, t * P:(t + 1) * P], czn[st][:, t, f * P:(f + 1) * P])
                        done(ins_)
                elif kind == "yo":
                    l, t = key[1:]
                    st = t // TT
                    pe.wait_ge(ln_done, CF * (1 + st if l == 0 else 3))
                    evacuated(pe, ("doT", l, st))
                    src, tt = ((branch, t), (cbranch, t - TT))[st]
                    for n in range(2):
                        w = chunk(pe, ("yo", l, n))
                        done(tokens(claim(pe, key, n)[:, :], src, tt, w, 0, WCOLS))


_INS = ['x', 'mem', 'mem_norm_w', 'norm_w', 'w_memkv', 'w_out', 'w_in_a', 'w_gate_up', 'b_gate', 'gla_norm_w', 'w_in_b',
        'final_norm_w', 'c_2', 'ctx_2', 'c_ctx_2', 'w_mod_2', 'b_mod_2', 'g_pre_2', 'g_post_2', 'w_in_2', 'w_out_2',
        'na_rpb_2', 'diff_lq1_2', 'diff_lk1_2', 'diff_lq2_2', 'diff_lk2_2', 'diff_subln_g_2', 'conv_w_2', 'conv_b_2',
        'conv_ln_g_2', 'conv_ln_b_2']


def kernel(**inputs):
    import concourse.bacc as bacc
    from concourse.bass_utils import run_bass_kernel_spmd

    nc = bacc.Bacc("TRN2", target_bir_lowering=False, num_devices=1)
    arrays, ins, consts = {}, {}, {}
    for name in _INS:
        a = np.ascontiguousarray(inputs[name])
        arrays[f"in_{name}"] = a
        ins[name] = nc.dram_tensor(f"in_{name}", a.shape, mybir.dt.from_np(a.dtype), kind="ExternalInput").ap()
    for name, a in constants().items():
        arrays[f"const_{name}"] = a
        consts[name] = nc.dram_tensor(f"const_{name}", a.shape, mybir.dt.from_np(a.dtype), kind="ExternalInput").ap()
    out = nc.dram_tensor("out", (1, T, D), F32, kind="ExternalOutput").ap()
    hybrid_stack_kernel(nc, ins, consts, out)
    r = run_bass_kernel_spmd(nc, [arrays], core_ids=[0])
    return r.results[0]["out"]
```

```python
from contextlib import ExitStack
import math

import numpy as np

import concourse.bass as bass
from concourse import mybir

ALU = mybir.AluOpType
ACT = mybir.ActivationFunctionType
F32 = mybir.dt.float32
I32 = mybir.dt.int32
F32R = mybir.dt.float32r
AX_X = mybir.AxisListType.X

P = 128
D = 1024
KT = D // P
T = 512
TT = T // P
NMEM = 256
CT = NMEM // P
EPS = 1e-6
BANK = 512
BANKS = 8
WCOLS = 512
WSLOTS = 3
WNARROW = 384
MODC = 384
MODS = 3 * D // MODC
UNITS = 5

MH, MD = 4, 64
GH, GK, GV = 4, 96, 192
GCHUNK = 64
GRANK = 16
GTAU = 16.0
BH, BD = 6, 128
BG = 3
DIL = 4
NH, ND = 6, 64
GRID_W, GRID_H = 64, 8
NQB = 4
STRIP = 32
DH, DD, DV = 4, 48, 96
DPAD = 64
CW = 256
CF = CW // P
TAPS = 31
HALO = TAPS // 2
NEG = -1e30

C_NK, C_NV, C_DK, C_DV, C_NQ, C_NG, C_DQ, C_DG, C_CA, C_CB, C_CG = (
    0, 384, 768, 1152, 1536, 1920, 2304, 2688, 3072, 3328, 3584)
A_Q, A_K, A_V, A_G, A_M, A_GATE = 0, 384, 768, 1536, 1552, 1808

V_C, V_MEM, V_NORM, V_GPRE, V_GPOST, V_GLA, V_SUB, V_CB, V_LG, V_LB = 0, 16, 24, 40, 56, 72, 75, 81, 85, 89
V_EARLY = V_GLA
V_ROWS = 93
CW_ROWS = 2 * TAPS
STRIP_START = (0, 8, 24, 32)
BIAS_KIND = (0, 1, 1, 2)
BIAS_OFF = (0, -8, -16)
RPB = NH * 15 * 31
RPB_PAD = 16


def constants():
    f = np.float32
    out = {}
    out["ident"] = np.eye(P, dtype=f)
    j, i = np.arange(P)[:, None], np.arange(P)[None, :]
    out["gla_mask"] = ((j // GCHUNK == i // GCHUNK) & (j <= i)).astype(np.int32)
    t = np.arange(T)
    out["gla_reset"] = np.broadcast_to((t % GCHUNK != 0).astype(f), (GK, T)).copy()
    q, k = np.arange(P)[:, None], np.arange(P)[None, :]
    prev = np.where(k >= q, 0.0, NEG)
    own = np.where(k <= q, 0.0, NEG)
    phase = np.where((k <= q) & ((q - k) % 4 == 0), 0.0, NEG)
    out["dil_mask"] = np.concatenate([prev, own, phase], axis=1).astype(f)
    half = BD // 4 // 2
    inv = (f(500000.0) ** (-np.arange(half, dtype=f) / f(half))).astype(f)
    ang = (t.astype(f)[:, None] * inv[None, :]).astype(f).astype(np.float64)
    cos = np.concatenate([np.cos(ang), np.cos(ang)], axis=1).T
    sin = np.concatenate([-np.sin(ang), np.sin(ang)], axis=1).T
    perm = (np.arange(P)[None, :] * DIL + np.arange(DIL)[:, None]).ravel()
    out["dil_rope"] = np.stack([cos, sin, cos[:, perm], sin[:, perm]], axis=1).astype(f)
    d = DD // 2
    inv = (f(10000.0) ** (-np.arange(0, d, 2, dtype=f) / f(d))).astype(f)
    tab = np.zeros((2, T, 2, 2, d // 2))
    for a, pos in enumerate((t // GRID_W, t % GRID_W)):
        ang = (pos.astype(f)[:, None] * inv[None, :]).astype(f).astype(np.float64)
        tab[0, :, a, :, :] = np.cos(ang)[:, None, :]
        tab[1, :, a, 0, :] = -np.sin(ang)
        tab[1, :, a, 1, :] = np.sin(ang)
    out["diff_rope"] = tab.reshape(2, TT, P, DD).transpose(2, 0, 1, 3).astype(f).copy()
    neg = np.zeros((P, 3, GRID_H, STRIP))
    for kind, block in enumerate((0, 1, 3)):
        cq = block * 16 + np.arange(P) % 16
        start = np.clip(cq - 8, 0, GRID_W - 16)[:, None]
        ck = STRIP_START[block] + np.arange(STRIP)[None, :]
        neg[:, kind] = np.where((ck >= start) & (ck < start + 16), 0.0, NEG)[:, None, :]
    out["na_mask"] = neg.reshape(P, 3, GRID_H * STRIP).astype(f)
    return out


def schedule():
    s = []
    add = lambda readers, *key: s.append((key, readers))
    add("v", "vecT", 0)
    add("avav", "memT")
    add("aa", "memkv", 0)
    add("aa", "memkv", 1)
    add("v", "vecT", 1)
    add("avavavav", "hT", "A")
    add("avavavav", "Av")
    add("a", "Aglow")
    add("avv", "Aproj", 0)
    add("avv", "Aproj", 1)
    add("va", "AA", 0)
    add("avv", "Aproj", 2)
    add("vvvv", "AdS", 0)
    add("va", "AA", 1)
    add("avv", "Aproj", 3)
    add("aa", "Ao", 0)
    add("vvvv", "AdS", 1)
    add("va", "AA", 2)
    for i in (0, 1):
        add("a", "gate", "A", i)
    add("aa", "Ao", 1)
    add("vvvv", "AdS", 2)
    add("va", "AA", 3)
    add("a", "gate", "A", 2)
    add("aa", "Ao", 2)
    add("vvvv", "AdS", 3)
    for i in (3, 4):
        add("a", "gate", "A", i)
    add("aa", "Ao", 3)
    add("av", "qm", "A")
    add("a", "gate", "A", 5)
    add("a" * 8, "mS", "A")
    for i in (6, 7):
        add("a", "gate", "A", i)
    add("av" * 4, "mT", "A")
    add("v" * 6, "AoT")
    add("vv", "mPV", "A")
    add("v" * 8, "wout", "A")
    add("v" * 8, "hT", "B")
    for i in range(8):
        add("a", "gate", "B", i)
    add("av", "qm", "B")
    add("a" * 8, "mS", "B")
    for g in range(2):
        add("aav", "Bproj", 0, g)
    add("av" * 4, "mT", "B")
    add("aav", "Bproj", 0, 2)
    add("vv", "mPV", "B")

    def modulation(j):
        if 0 < j <= MODS:
            add("v", "mod", 0, j - 1)
        if j < MODS:
            add("", "modv", j)

    for h in range(BH):
        add("aaavvvv", "BS", h)
        if h + 1 < BH:
            add("aav", "Bproj", h + 1, 0)
            add("", "Bw", h)
            modulation(2 * h)
            add("aav", "Bproj", h + 1, 1)
            if 2 * h == MODS:
                add("v", "modT", 0)
            add("avav", "BT", h)
            add("aav", "Bproj", h + 1, 2)
        else:
            for j in range(MODS):
                if j == MODS - 2:
                    add("", "Bw", h)
                add("v", "mod", 1, j)
            add("avav", "BT", h)
        add("va", "BPV", h)
        modulation(2 * h + 1)
    add("v", "modT", 1)
    add("v" * 8, "wout", "B")
    for l in range(2):
        both = l == 0
        if both:
            add("avav", "hcT", l)
            add("", "norms", l)
            add("vvv", "nkc", l)
            add("avavavav", "hT", f"C{l}")
            add("aaa", "nk", l)
        else:
            add("aaa", "nk", l)
            add("avav", "hcT", l)
            add("vvv", "nkc", l)
        add("aaaavv", "nv", l)
        add("aaavvv" if both else "aaa", "nq", l)
        add("avav" + "avav" * both, "cv", l)
        gates = [("a" + "a" * both, "gate", f"C{l}", i) for i in range(KT)]

        def staged(what, tiles):
            units = [[("v" if t < TT else "a", "dP", l, what, t)] for t in range(tiles)] + [[]]
            for t in range(tiles):
                units[t + 1].append(("a", "dX", l, what, t))
            return units

        keys = staged("k", TT + CT)
        for h in range(NH):
            add("aaaa", "nS", l, h)
            add(*gates[h])
            add("", "nW", l, h)
            if not both:
                for step in keys.pop(0):
                    add(*step)
            add("avav", "nT", l, h)
            add("av"[h % 2], "dv", l, h)
            add("v", "nPV", l, h)
        if both:
            for h in range(NH + 2):
                if h < NH:
                    add("a", "cS", l, h)
                if 0 <= h - 1 < NH:
                    add("", "cW", l, h - 1)
                if keys:
                    for step in keys.pop(0):
                        add(*step)
                if 0 <= h - 1 < NH:
                    add("a", "cT", l, h - 1)
                if h >= 2:
                    add("v", "cPV", l, h - 2)
        for unit in keys:
            for step in unit:
                add(*step)
        queries = staged("q", TT + CT * both)
        add(*gates[6])
        for unit in queries[:-1]:
            for step in unit:
                add(*step)
        add(*gates[7])
        add(*queries[-1][0])
        items = diff_items(l)
        for n in range(len(items) + 3):
            if n < len(items):
                add("aaaa" if items[n][0] < TT else "aa", "dS", l, *items[n])
            if 2 <= n < len(items) + 2:
                t, h = items[n - 2]
                add("av" if t < TT else "a", "dT", l, t, h)
            if n >= 3:
                add("a", "dPV", l, *items[n - 3])
            for st in range(1 + both):
                at_ = 8 + 12 * st
                if n == at_:
                    add("v" * (2 if st == 0 else 1), "cvT", l, st)
                if n == at_ + 3:
                    add("aa", "cvZ", l, st)
            if both and n == TT * DH + 5:
                add("vvv", "doT", l, 0)
        add("vvv", "doT", l, 1 if both else 0)
        for t in range(TT + CT * both):
            if t == TT + CT - 1:
                add("avavavav", "hT", "C1")
            add("vv", "yo", l, t)
    out, n, split = [], 0, 0
    total = sum(split_jobs(key) for key, _ in s)
    for key, readers in s:
        if split_jobs(key) or key == ("hT", "B") or key[0] == "BS":
            while split < min(n + UNITS, total):
                out.append((("split", split), ""))
                split += 1
            n += split_jobs(key)
        out.append((key, readers))
    return out


def split_jobs(key):
    return {("gate", "B"): 1, ("qm", "B"): 2}.get(key[:2], 3 * (key[0] == "Bproj"))


def diff_items(l):
    return [(t, h) for t in range(TT + (CT if l == 0 else 0)) for h in range(DH)]


def hybrid_stack_kernel(nc, ins, consts, out):
    steps = schedule()
    base, readers, order_of = {}, [], {}
    for n, (key, who) in enumerate(steps):
        base[key] = len(readers)
        order_of[key] = n
        readers += list(who)
    ordinal, seen = [], {"a": 0, "v": 0}
    for who in readers:
        seen[who] += 1
        ordinal.append(seen[who])
    njobs = {key: len(who) for key, who in steps}

    mem_scale = MD ** -0.5
    dil_scale = BD ** -0.5
    diff_scale = DD ** -0.5
    lam_init = [0.8 - 0.6 * math.exp(-0.3 * l) for l in range(2)]

    with ExitStack() as ctx:
        def sb(name, shape, dt=F32):
            return ctx.enter_context(nc.sbuf_tensor(name, shape, dt))

        def sem(name):
            return ctx.enter_context(nc.semaphore(name))

        def dram(name, shape):
            return nc.dram_tensor(name, shape, F32, kind="Internal").ap()

        arena_cols = 29696
        with (nc.sbuf_tensor("arena", [P, arena_cols], F32) as arena, nc.sbuf_tensor("hT", [P, KT, T], F32) as hT,
              nc.sbuf_tensor("wring", [P, WSLOTS, KT * WCOLS], F32) as wring):
            pass
        arena_r = sb("arena_r", [P, arena_cols], F32R)
        hT_r = sb("hT_r", [P, KT, T], F32R)
        wring_r = sb("wring_r", [P, WSLOTS, KT * WCOLS], F32R)

        def at(off, *dims, parts=P):
            n = math.prod(dims)
            v = arena[0:parts, off:off + n]
            if len(dims) == 1:
                return v
            names = "abcde"[:len(dims)]
            sizes = {c: d for c, d in zip(names[1:], dims[1:])}
            return v.rearrange(f"p ({' '.join(names)}) -> p {' '.join(names)}", **sizes)

        branch = sb("branch", [P, KT, T])
        ident = sb("ident", [P, P])
        vec = sb("vec", [P, V_ROWS + 2 * CW_ROWS])
        modv = sb("modv", [P, 2, 2, KT, 2])
        dil_mask = sb("dil_mask", [P, 3 * P])
        na_mask = sb("na_mask", [P, 3, GRID_H * STRIP])
        diff_rope = sb("diff_rope", [P, 2, TT, DD])
        siluc = sb("siluc", [P, KT, 2])
        subw = sb("subw", [P, 2, 3])
        lam = sb("lam", [P, 2])
        stat = sb("stat", [P, 600])
        cols = [0]

        def stats(*dims):
            n = math.prod(dims)
            v = stat[:, cols[0]:cols[0] + n]
            cols[0] += n
            if len(dims) == 1:
                return v
            names = "abcde"[:len(dims)]
            sizes = {c: d for c, d in zip(names[1:], dims[1:])}
            return v.rearrange(f"p ({' '.join(names)}) -> p {' '.join(names)}", **sizes)

        minus_half = stats(4)
        pick = stats(2, 2)
        gatev = stats(2, KT)
        conv_w = vec[:, V_ROWS:].rearrange("p (f r) -> p f r", f=CF)

        hT_hi = hT_r[:, :, :]
        hT_lo = arena_r[:, 0:KT * T].rearrange("p (k t) -> p k t", k=KT)
        x = at(0, TT, D)
        memk = at(4096, 2, 2, NMEM)
        memv = at(5120, 2, CT, MH * MD)
        xn = at(6144, TT, D)
        modrow = at(10240, 3 * D, parts=2)
        modacc = at(13312, 2, MODC)
        vrows = at(14336, P, parts=V_EARLY)
        vrows2 = at(27552, P, parts=V_ROWS - V_EARLY)
        crows = at(27680, CW, parts=CW_ROWS)
        memraw = at(14720, CT, D)
        memn = at(18816, CT, D)
        memT = at(16768, KT, NMEM)
        glow = at(18816, T, parts=GRANK)
        gv = at(19328, TT, GH * GV)
        wgu = at(22400, GH * GK, parts=GRANK)
        bgate = at(22784, 16, parts=GK)
        gmask = at(22800, P).bitcast(I32)
        greset = at(22928, T, parts=GK)
        gq = at(23440, GH, T, parts=GK)
        gk = at(25488, GH, T, parts=GK)
        gt = at(6144, 2, 4, T, parts=GK)
        gkin = at(10240, 2, T, parts=GK)
        gkout = at(11264, 2, T, parts=GK)
        gkot = at(12288, 2, TT, GK)
        gA = at(13056, 2, TT, P)
        gS = at(14080, T // GCHUNK, GV, parts=GK)
        go = at(15616, TT, GH * GV)
        gdec = sb("gdec", [GK, GH, T // GCHUNK])
        mprob = at(6144, 8, 2, NMEM)
        mprobT = at(10240, MH, CT, T)
        qmem = {"A": at(14336, 2, T), "B": at(25088, 2, T)}
        bqk = at(14336, 2, BG, 2, T)
        bvT = at(20480, 2, BG, T)
        bv = at(23552, BG, TT, BD)
        bswap = at(25088, 2, T, parts=32)
        bo12 = at(26112, T)
        bsum = at(26624, T)
        dil_rope = at(27136, 4, T, parts=32)
        bprob = at(6144, 2048)
        bprobT = at(8192, 15, P)
        hcT = at(4096, KT, NMEM)
        cbranch = at(6144, KT, NMEM)
        xc = at(8192, CT, D)
        cxn = at(10240, TT, D)
        cxcn = at(14336, CT, D)
        fw = at(16384, D)
        nkT = at(10240, 3, T)
        nqT = at(11776, 3, T)
        nqcT = at(13312, 3, NMEM)
        nkcT = at(14336, 3, NMEM)
        vstrip = at(15104, NQB, 2, NH * ND)
        vctx = at(18176, CT, NH * ND)
        bias = at(18944, 2, 3, GRID_H * STRIP)
        dkT = at(20480, DH, T + NMEM)
        dv = at(23552, TT + CT, DH * DV)
        dstage = at(25856, 2, 2 * DH, DPAD)
        dswap = dil_mask[:, :].rearrange("p (h d) -> p h d", d=DD)
        csig = at(25856, 2, T)
        u = at(27008, CF, T + 2 * HALO)
        uc = at(28092, CF, NMEM + 2 * HALO)
        y = at(28664, CF, T)
        yc = at(4096, CF, NMEM)
        nprob = at(0, NQB, BANK)
        nprobT = at(2048, NQB, 4, P)
        vnat = at(2048, TT, NH * ND)
        cprob = at(0, 4, CT, NMEM)
        cprobT = at(2048, 4, CT, NMEM)
        dqT = [at(10240, DH, T), at(12288, DH, NMEM)]
        hflat = hT[:, :, :].rearrange("p k t -> p (k t)")
        dprob = [hflat[:, i * 1536:(i + 1) * 1536].rearrange("p (s k) -> p s k", s=2) for i in range(2)]
        dprob.append(at(13312, 2, T + NMEM))
        dwT = at(14848, 2, TT + CT, P)
        otok = [at(17920, TT, DH * DV), at(19456, CT, DH * DV)]
        czn = [at(16384, TT, CW), at(17408, CT, CW)]
        csilu = [hflat[:, 3072:4096].rearrange("p (f t) -> p f t", f=CF), at(25856, CF, NMEM)]
        gmul = at(20480, 2, D)
        ytmp = at(22528, D)
        yjunk = at(23552, D)

        gate_dram = dram("gate_dram", [2, 2, D])
        x0_dram = dram("x0_dram", [T, D])
        st0_dram = dram("st0_dram", [BH, 2, T])
        st12_dram = dram("st12_dram", [BH, 4, T])
        x_dram = dram("x_dram", [2, T, D])
        nv_dram = dram("nv_dram", [2, T, NH * ND])
        rpb_dram = [dram(f"rpb_dram{l}", [RPB_PAD + RPB + 2 * RPB_PAD]) for l in range(2)]
        ebias_dram = [dram(f"ebias_dram{l}", [3, NH, 16, 15 * STRIP]) for l in range(2)]

        banks = [ctx.enter_context(nc.psum_tensor(f"bank{i}", [P, BANK], F32)) for i in range(BANKS)]

        psum_full = sem("psum_full")
        evac = {"a": sem("evac_scalar"), "v": sem("evac_vector")}
        w_full = [sem(f"w_full{i}") for i in range(WSLOTS)]
        vecs_in, vecs2_in, gla_in, const_in, mem_in, x_in = (sem(n) for n in (
            "vecs_in", "vecs2_in", "gla_in", "const_in", "mem_in", "x_in"))
        dve_chain, act_chain, pool_chain = sem("dve_chain"), sem("act_chain"), sem("pool_chain")
        silu_c, sq_done, rstd_ready, xn_ready = (sem(n) for n in ("silu_c", "sq_done", "rstd_ready", "xn_ready"))
        split_hi, split_lo, hi_ready, x0_saved, x0_back = (sem(n) for n in (
            "split_hi", "split_lo", "hi_ready", "x0_saved", "x0_back"))
        bmod_in, mod_sums, gate_row, gate_saved = (sem(n) for n in ("bmod_in", "mod_sums", "gate_row", "gate_saved"))
        gla_abs, gla_soft, gla_cum, gla_exps, gla_qin, gla_keys, gla_sq, gla_rstd, gla_zero = (sem(n) for n in (
            "gla_abs", "gla_soft", "gla_cum", "gla_exps", "gla_qin", "gla_keys", "gla_sq", "gla_rstd", "gla_zero"))
        mem_negmax, mem_probs = sem("mem_negmax"), sem("mem_probs")
        rope_in, rope_done, dil_negmax, dil_probs, st_saved, st_in, dil_diff, dil_exp, dil_weighted, dil_out = (
            sem(n) for n in ("rope_in", "rope_done", "dil_negmax", "dil_probs", "st_saved", "st_in", "dil_diff",
                             "dil_exp", "dil_weighted", "dil_out"))
        fw_in, xc_in, x_final, x_saved, x_back, pads_zero, lam_in, lam_dots, lam_exps, lam_ready = (sem(n) for n in (
            "fw_in", "xc_in", "x_final", "x_saved", "x_back", "pads_zero", "lam_in", "lam_dots", "lam_exps",
            "lam_ready"))
        rpb_saved, ebias_saved, bias_ready = (sem(n) for n in ("rpb_saved", "ebias_saved", "bias_ready"))
        bias_in = [sem("bias_in_even"), sem("bias_in_odd")]
        nv_saved, strips_in, na_negmax, na_probs, ctx_negmax, ctx_probs = (sem(n) for n in (
            "nv_saved", "strips_in", "na_negmax", "na_probs", "ctx_negmax", "ctx_probs"))
        diff_staged, diff_negmax, diff_w, o_sq, o_rstd, o_normed = (sem(n) for n in (
            "diff_staged", "diff_negmax", "diff_w", "o_sq", "o_rstd", "o_normed"))
        conv_done, ln_var, ln_rstd, ln_done = (sem(n) for n in ("conv_done", "ln_var", "ln_rstd", "ln_done"))
        gmul_in, y_sq, y_rstd, x_new, out_saved = (sem(n) for n in ("gmul_in", "y_sq", "y_rstd", "x_new", "out_saved"))

        def bank(key, i):
            return banks[(base[key] + i) % BANKS]

        def claim(pe, key, i):
            n = base[key] + i
            if n >= BANKS:
                pe.wait_ge(evac[readers[n - BANKS]], ordinal[n - BANKS])
            return bank(key, i)

        def full(eng, key, i):
            eng.wait_ge(psum_full, base[key] + i + 1)
            return bank(key, i)

        def read_by_pe(eng, key):
            eng.wait_ge(psum_full, base[key] + njobs[key])

        def evacuated(eng, key, i=-1):
            n = base[key] + i % njobs[key]
            eng.wait_ge(evac[readers[n]], ordinal[n])

        def cols_of(w, c0, n):
            return w.rearrange("(k p) c -> p k c", p=P)[:, :, c0:c0 + n]

        wa, wb, wout, wmem = ins["w_in_a"][0], ins["w_in_b"][0], ins["w_out"], ins["w_memkv"]
        chunks = [(("memkv", l), cols_of(wmem[l], 0, 512), 512, ("memkv", l)) for l in range(2)]
        chunks += [
            (("Av", 0), cols_of(wa, A_V, 384), 384, ("Av",)),
            (("Av", 1), cols_of(wa, A_V + 384, 384 + GRANK), 384 + GRANK, ("Aglow",)),
            (("Aq",), cols_of(wa, A_Q, 384), 384, ("Aproj", 3)),
            (("Ak",), cols_of(wa, A_K, 384), 384, ("Aproj", 3)),
            (("gate", "A", 0), cols_of(wa, A_GATE, 512), 512, ("gate", "A", 3)),
            (("gate", "A", 1), cols_of(wa, A_GATE + 512, 512), 512, ("gate", "A", 7)),
            (("qm", "A"), cols_of(wa, A_M, 256), 256, ("qm", "A")),
        ]
        chunks += [(("wout", "A", n), cols_of(wout[0], n * 512, 512), 512, ("wout", "A")) for n in range(2)]
        rest = BG * 3 * BH * BD
        for n, c in ((0, 384), (1, 384), (2, 256)):
            chunks.append((("gate", "B", n), cols_of(wb, rest + 256 + n * WNARROW, c), c, ("gate", "B", min(3 * n + 2, 7))))
        chunks += [(("qm", "B"), cols_of(wb, rest, 256), 256, ("qm", "B"))]
        mods = [[(("mod", l, j), cols_of(ins["w_mod_2"][l], j * MODC, MODC), MODC, ("mod", l, j) if l else ("modv", j))
                 for j in range(MODS)] for l in range(2)]
        for h in range(BH):
            for g in range(BG):
                src = wb[:, g * 2304:(g + 1) * 2304].rearrange("(k p) (s c) -> p k s c", p=P, s=3)
                chunks.append((("Bproj", h, g), src[:, :, :, h * BD:(h + 1) * BD], 384, ("Bproj", h, g)))
                if h and g != 1 and 2 * (h - 1) + g // 2 < MODS:
                    chunks.append(mods[0][2 * (h - 1) + g // 2])
        chunks += mods[1]
        chunks += [(("wout", "B", n), cols_of(wout[1], n * 512, 512), 512, ("wout", "B")) for n in range(2)]
        for l in range(2):
            w2, wo2 = ins["w_in_2"][l], ins["w_out_2"][l]
            last_t = TT + CT - 1
            for name, c0, n, last in (
                    ("nk", C_NK, 384, ("nk" if l == 0 else "nkc", l)), ("nv", C_NV, 384, ("nv", l)), ("nq", C_NQ, 384, ("nq", l)),
                    ("cv", C_CA, 512, ("cv", l)), ("g0", C_NG, 384, ("gate", f"C{l}", 2)),
                    ("dk", C_DK, 384, ("dP", l, "k", last_t)), ("dv", C_DV, 384, ("dv", l, last_t)),
                    ("g1", C_DG, 384, ("gate", f"C{l}", 5)), ("g2", C_CG, 256, ("gate", f"C{l}", 7)),
                    ("dq", C_DQ, 384, ("dP", l, "q", last_t if l == 0 else TT - 1))):
                chunks.append(((name, l), cols_of(w2, c0, n), n, last))
            chunks += [(("yo", l, n), cols_of(wo2, n * 512, 512), 512, ("yo", l, last_t if l == 0 else TT - 1))
                       for n in range(2)]
        chunk_at = {name: n for n, (name, *_) in enumerate(chunks)}

        def chunk(pe, name):
            n = chunk_at[name]
            pe.wait_ge(w_full[n % WSLOTS], loaded(n))
            return slot(n)

        def loads(n):
            return 3 if chunks[n][0][0] == "Bproj" else 1

        def slot(n):
            c = chunks[n][2]
            return wring[:, n % WSLOTS, 0:KT * c].rearrange("p (k c) -> p k c", c=c)

        def loaded(n):
            return 16 * sum(loads(m) for m in range(n % WSLOTS, n + 1, WSLOTS))

        def done_before(eng, job):
            key, i = job
            eng.wait_ge(psum_full, base[key] + i + 1)

        def slot4(n):
            return wring[:, n % WSLOTS, 0:KT * 384].rearrange("p (k s c) -> p k s c", s=3, c=BD)

        def gate_chunk(ph, i):
            if ph == "A":
                return ("gate", ph, i // 4), (i % 4) * P
            if ph == "B":
                return ("gate", ph, i // 3), (i % 3) * P
            return (f"g{i // 3}", int(ph[1])), (i % 3) * P

        split_list = [(key, i) for key, _ in steps for i in range(split_jobs(key))]
        split_at = {job: n for n, job in enumerate(split_list)}
        before_mem = split_at[("Bproj", 1, 0), 0] + 3

        def split_weights(n):
            key, i = split_list[n]
            if key[0] == "gate":
                name, c0 = gate_chunk("B", key[2])
            else:
                name, c0 = key, i * P
            at_, u = chunk_at[name], n % UNITS
            if u < WSLOTS:
                hi = wring_r[:, u, KT * WNARROW:KT * WCOLS]
            else:
                lo = ((23552, 26112) if n < before_mem else (4096, 5120))[u - WSLOTS]
                hi = arena_r[:, lo:lo + KT * P]
            width = chunks[at_][2]
            rest = wring_r[:, at_ % WSLOTS, 0:KT * width].rearrange("p (k c) -> p k c", c=width)[:, :, c0:c0 + P]
            return at_, slot(at_)[:, :, c0:c0 + P], hi.rearrange("p (k c) -> p k c", c=P), rest

        norms = {}
        norm_at, n_tiles = {}, 0
        for ph, src, dst, nt in (("m", memraw, memn, CT), ("A", x, xn, TT), ("B", x, xn, TT), ("c0", xc, cxcn, CT),
                                 ("F", x, cxn, TT), ("C0", x, cxn, TT), ("C1", x, cxn, TT), ("c1", xc, cxcn, CT)):
            norms[ph] = (src, dst, nt, stats(nt), stats(nt))
            norm_at[ph] = n_tiles
            n_tiles += nt

        gla_ss, gla_rs = stats(GH, TT), stats(GH, TT)
        m_max, m_neg, m_sum, m_rec = (stats(2, 8, 2) for _ in range(4))
        b_stat = stats(2, BG, 2, 2, TT)
        b_neg = stats(2, BG, TT)
        b_top, b_w, b_rec = stats(2, TT), stats(BG, 2, TT), stats(2, TT)
        n_ctx, n_max, n_neg, n_s, n_rec = stats(NQB), stats(NQB), stats(NQB), stats(2, NQB), stats(2, NQB)
        c_max, c_neg, c_s, c_rec = (stats(2, CT) for _ in range(4))
        d_max, d_neg, d_s, d_rec = (stats(4, 4) for _ in range(4))
        o_ss, o_rs = stats(TT + CT, DH), stats(TT + CT, DH)
        ln_st, ln_mv, ln_rs = stats(6), stats(2, 2, 2), stats(2, 2)
        y_ss, y_rs = stats(2, 2), stats(2, 2)
        lam_st = stats(2, 2)
        lam_v = sb("lam_v", [P, 2, 4, DD])
        lam_junk = at(28000, DD)
        assert cols[0] <= 600, cols[0]

        norm_pe, n_tiles = {}, 0
        for ph in norms:
            if ph != "F":
                n_tiles += norms[ph][2]
            norm_pe[ph] = n_tiles
        stages = [key for key, _ in steps if key[0] == "dP"]
        roped = [key for key in stages if key[3] < TT]

        def stage_at(key):
            return stages.index(key)

        def stage_key(n):
            return ("dX", *stages[n][1:])

        def roped_at(key):
            return roped.index(key)

        all_diff = [(l, t, h) for l in range(2) for t, h in diff_items(l)]

        def diff_at(l, t, h):
            return all_diff.index((l, t, h))

        def diff_step(kind, n):
            return (kind, *all_diff[n])

        def diff_tile(l, t):
            return l * (TT + CT) + t

        def score_part(t, i):
            half, part = divmod(i, 2) if t < TT else (i, 1)
            return (half, part, 0, T) if part == 0 else (half, part, T, NMEM)

        def ln_pair(l, st, i):
            return 3 * l + 2 * st + i

        def conv_inputs(l, st, f):
            return 4 * l + 2 * st + f

        def conv_input_at(m):
            l, r = divmod(m, 4)
            return ("cv", l), 2 * r + 1

        def bprob_tile(g, n):
            if g == 0:
                return bprob[:, P:2 * P] if n == 0 else bprob[:, 2 * n * P:(2 * n + 2) * P]
            return bprob[:, (4 + 4 * g + n) * P:(5 + 4 * g + n) * P]

        def dil_tile(g, n):
            if g == 0:
                return 3 + n // 2, (n % 2) * 2 * P, P if n == 0 else 0
            return 4 + g, n * P, P * g

        def self_bias(pool, l, h):
            if (l, h) == (0, 0):
                pool.wait_ge(const_in, 48)
            pool.wait_ge(bias_in[h % 2], 16 * GRID_H * ((l * NH + h) // 2 + 1))
            v = bias[:, h % 2]
            nc.gpsimd.tensor_tensor(v, v, na_mask[:, :, :], ALU.add).then_inc(bias_ready, 1)

        PT_BANKS = ((0, 4), (4, 3), (7, 4), (11, 4))
        PT_TILES = (1, 2, 3, 4, 5, 6, 7, 8, 9, 10, 11, 12, 13, 14, 15)
        DS_BANK = {0: (0, 0), 1: (1, 0), 2: (0, 1), 3: (1, 1), 4: (3, 0), 5: (2, 0), 6: (3, 1)}
        DS_LAST = (2, 3, 5, 6)
        VECS_IN = 16 * 7
        VECS2_IN = 16 * 20

        block = ctx.enter_context(nc.Block())

        def sync_items():
            items = []
            for n in range(len(chunks)):
                items.append((order_of[chunks[n - WSLOTS][3]] if n >= WSLOTS else -1, "chunk", n))
            items.append((order_of[("Bproj", BH - 1, BG - 1)], "x0_back", None))
            for l in range(2):
                for kind in range(3):
                    items.append((order_of[("BS", 3 * l + kind - (l == 1))], "ebias", (l, kind)))
                for h in range(NH):
                    free = ("BS", BH - 1) if l == 0 else ("doT", 0, 1)
                    items.append((order_of[free if h < 2 else ("nS", l, h - 2)], "bias", (l, h)))
                last_na = ("cPV", l, NH - 1) if l == 0 else ("nPV", l, NH - 1)
                items.append((order_of[last_na], "x_back", (l, last_na)))
                last_ds = ("dS", l, *diff_items(l)[-1])
                items.append((order_of[last_ds], "gmul", (l, last_ds)))
            return sorted(items, key=lambda i: i[0])

        @block.sync
        def _(sp):
            def late_vectors():
                n_vec = 0

                def piece(r, c, src):
                    sp.dma_start(vrows2[r - V_EARLY:r - V_EARLY + src.shape[0], c:c + src.shape[1]], src).then_inc(vecs2_in, 16)
                    return 1

                gla_w = ins["gla_norm_w"]
                n_vec += piece(V_GLA, 0, gla_w[:, 0:128])
                n_vec += piece(V_GLA + 1, 0, gla_w[:, 128:192])
                n_vec += piece(V_GLA + 1, 64, gla_w[:, 0:64])
                n_vec += piece(V_GLA + 2, 0, gla_w[:, 64:192])
                for l in range(2):
                    sw = ins["diff_subln_g_2"][l:l + 1]
                    for r in range(3):
                        f = r * P
                        while f < (r + 1) * P:
                            e = f % DV
                            n = min(DV - e, (r + 1) * P - f)
                            n_vec += piece(V_SUB + 3 * l + r, f - r * P, sw[:, e:e + n])
                            f += n
                for r, name in ((V_CB, "conv_b_2"), (V_LG, "conv_ln_g_2"), (V_LB, "conv_ln_b_2")):
                    n_vec += piece(r, 0, ins[name].rearrange("l (r c) -> (l r) c", c=P))
                sp.dma_start(crows, ins["conv_w_2"].rearrange("l k c -> (l k) c")).then_inc(vecs2_in, 16)
                assert 16 * (n_vec + 1) == VECS2_IN, n_vec
                for q, name in enumerate(("diff_lq1_2", "diff_lk1_2", "diff_lq2_2", "diff_lk2_2")):
                    sp.dma_start(lam_v[:, :, q, :], ins[name].partition_broadcast(P)).then_inc(lam_in, 16)
                sp.dma_start(wgu, ins["w_gate_up"][0]).then_inc(gla_in, 16)
                sp.dma_start(bgate[:, 0:GH], ins["b_gate"][0].rearrange("(h p) -> p h", p=GK),
                             allow_slow_non_contiguous=True).then_inc(gla_in, 16)
                sp.dma_start(gmask, consts["gla_mask"]).then_inc(gla_in, 16)
                sp.dma_start(greset, consts["gla_reset"]).then_inc(gla_in, 16)
                sp.dma_start(dil_mask[:, :], consts["dil_mask"]).then_inc(const_in, 16)
                sp.dma_start(na_mask[:, :, :], consts["na_mask"]).then_inc(const_in, 16)
                sp.dma_start(diff_rope[:, :, :, :], consts["diff_rope"]).then_inc(const_in, 16)

            sp.wait_ge(vecs_in, VECS_IN)
            sp.dma_start(memraw, ins["mem"][0].rearrange("(t p) d -> p t d", p=P)).then_inc(mem_in, 16)
            for _, what, arg in sync_items():
                if what == "chunk":
                    name, src, c, last = chunks[arg]
                    if arg >= WSLOTS:
                        last = chunks[arg - WSLOTS][3]
                        if last[0] == "modv":
                            sp.wait_ge(mod_sums, last[1] + 1)
                        else:
                            read_by_pe(sp, last)
                    for i in range(loads(arg)):
                        dst, part = (slot(arg), src) if loads(arg) == 1 else (slot4(arg)[:, :, i], src[:, :, i])
                        sp.dma_start(dst, part).then_inc(w_full[arg % WSLOTS], 16)
                    if arg == 0:
                        sp.dma_start(x, ins["x"][0].rearrange("(t p) d -> p t d", p=P)).then_inc(x_in, 16)
                    if arg == 2:
                        late_vectors()
                elif what == "ebias":
                    l, kind = arg
                    sp.wait_ge(rpb_saved, 48 * (l + 1))
                    for qq in range(16):
                        off = RPB_PAD + BIAS_OFF[kind] + 15 - qq
                        src = bass.AP(rpb_dram[l].tensor, off, [[465, NH], [31, 15], [1, STRIP]])
                        sp.dma_start(ebias_dram[l][kind, :, qq, :].rearrange("h (r c) -> h r c", c=STRIP),
                                     src).then_inc(ebias_saved, 16)
                elif what == "bias":
                    l, h = arg
                    if h < 2:
                        read_by_pe(sp, ("BS", BH - 1) if l == 0 else ("doT", 0, 1))
                    else:
                        sp.wait_ge(na_negmax, l * NH + h - 1)
                    sp.wait_ge(ebias_saved, 16 * 48 * 2)
                    for rq in range(GRID_H):
                        src = bass.AP(ebias_dram[l].tensor, h * 16 * 480 + (7 - rq) * STRIP,
                                      [[480, 16], [NH * 16 * 480, 3], [1, GRID_H * STRIP]])
                        sp.dma_start(bias[rq * 16:rq * 16 + 16, h % 2], src).then_inc(bias_in[h % 2], 16)
                elif what == "x0_back":
                    read_by_pe(sp, ("Bproj", BH - 1, BG - 1))
                    sp.wait_ge(x0_saved, 16 * TT)
                    sp.dma_start(x, x0_dram.rearrange("(t p) d -> p t d", p=P)).then_inc(x0_back, 16)
                elif what == "x_back":
                    l, last_na = arg
                    read_by_pe(sp, ("nPV", l, NH - 1))
                    read_by_pe(sp, last_na)
                    sp.wait_ge(x_saved, 16 * (l + 1))
                    sp.dma_start(x, x_dram[l].rearrange("(t p) d -> p t d", p=P)).then_inc(x_back, 16)
                elif what == "gmul":
                    l, last_ds = arg
                    read_by_pe(sp, last_ds)
                    sp.wait_ge(gate_saved, 32 * (l + 1))
                    for c in range(2):
                        sp.dma_start(gmul[:, c], gate_dram[l, c].partition_broadcast(P)).then_inc(gmul_in, 16)
            for t in range(TT):
                sp.wait_ge(x_new, TT + CT + t + 1)
                sp.dma_start(out[0].rearrange("(t p) d -> p t d", p=P)[:, t], x[:, t]).then_inc(out_saved, 16)
            sp.wait_ge(out_saved, 16 * TT)

        @block.gpsimd
        def _(pool):
            count = {"chain": 0}

            def chained(ins):
                count["chain"] += 1
                ins.then_inc(pool_chain, 1)
                pool.wait_ge(pool_chain, count["chain"])

            def root(rs, ss, n, done):
                chained(nc.gpsimd.tensor_scalar(rs, ss, 1.0 / n, EPS, ALU.mult, ALU.add))
                width = rs.shape[1]
                nc.gpsimd.tensor_tensor(rs, rs, minus_half[:, 0:width], ALU.pow).then_inc(done, 1)

            def norm_roots(ph, t):
                _, _, _, ss, rs = norms[ph]
                pool.wait_ge(sq_done, norm_at[ph] + t + 1)
                root(rs[:, t:t + 1], ss[:, t:t + 1], D, rstd_ready)

            chained(nc.gpsimd.memset(minus_half, -0.5))
            zeros = lam_junk[0:1, 0:2 * RPB_PAD]
            nc.gpsimd.memset(lam_junk, 0.0).then_inc(pads_zero, 1)
            nc.gpsimd.wait_ge(pads_zero, 1)
            for l in range(2):
                pool.dma_start(rpb_dram[l][0:RPB_PAD].rearrange("(a n) -> a n", a=1),
                               zeros[:, 0:RPB_PAD]).then_inc(rpb_saved, 16)
                pool.dma_start(rpb_dram[l][RPB_PAD + RPB:].rearrange("(a n) -> a n", a=1), zeros).then_inc(rpb_saved, 16)
                pool.dma_start(rpb_dram[l][RPB_PAD:RPB_PAD + RPB],
                               ins["na_rpb_2"][l].rearrange("h r c -> (h r c)")).then_inc(rpb_saved, 16)

            def load_mod(l):
                pool.dma_start(modrow, ins["b_mod_2"][l].partition_broadcast(2)).then_inc(bmod_in, 16)

            for j in range(2):
                nc.gpsimd.memset(pick[:, j, j:j + 1], 1.0).then_inc(gla_zero, 1)
                nc.gpsimd.memset(pick[:, j, 1 - j:2 - j], 0.0).then_inc(gla_zero, 1)
            nc.gpsimd.memset(gA, 0.0).then_inc(gla_zero, 1)
            nc.gpsimd.memset(gS[:, 0], 0.0).then_inc(gla_zero, 1)
            for ph in "mA":
                for t in range(norms[ph][2]):
                    norm_roots(ph, t)

            for key, _ in steps:
                kind = key[0]
                if kind == "modT":
                    l = key[1]
                    pool.wait_ge(gate_row, l + 1)
                    for c in range(2):
                        pool.dma_start(gate_dram[l, c].rearrange("(k p) -> p k", p=P), gatev[:, c],
                                       allow_slow_non_contiguous=True).then_inc(gate_saved, 16)
                    if l == 0:
                        pool.wait_ge(gate_saved, 32)
                        load_mod(1)
                elif kind == "Aproj":
                    h = key[1]
                    b = h % 2
                    evacuated(pool, key, 1)
                    pool.wait_ge(gla_exps, 3 * h + 3)
                    if h >= 2:
                        read_by_pe(pool, ("AA", h - 2))
                    nc.gpsimd.tensor_tensor(gkin[:, b], gk[:, h], gt[:, b, 1], ALU.mult).then_inc(gla_keys, 1)
                    nc.gpsimd.tensor_tensor(gkout[:, b], gk[:, h], gt[:, b, 3], ALU.mult).then_inc(gla_keys, 1)
                elif kind == "split":
                    _, w, hi, rest = split_weights(key[1])
                    pool.wait_ge(split_hi, key[1] + 1)
                    nc.gpsimd.tensor_tensor(rest, w, hi.bitcast(F32), ALU.subtract).then_inc(split_lo, 1)
                elif key == ("mPV", "B"):
                    read_by_pe(pool, key)
                    load_mod(0)
                elif kind == "Ao":
                    h = key[1]
                    for i in range(2):
                        pool.wait_ge(gla_sq, 2 * h + i + 1)
                        root(gla_rs[:, h, 2 * i:2 * i + 2], gla_ss[:, h, 2 * i:2 * i + 2], GV, gla_rstd)
                elif kind == "wout":
                    ph = key[1]
                    if ph == "A":
                        read_by_pe(pool, ("mPV", "A"))
                        for t in range(TT):
                            evacuated(pool, key, 2 * t + 1)
                            pool.dma_start(x0_dram[t * P:(t + 1) * P], x[:, t]).then_inc(x0_saved, 16)
                        pool.dma_start(dil_rope, consts["dil_rope"]).then_inc(rope_in, 16)
                        for t in range(TT):
                            norm_roots("B", t)
                    else:
                        read_by_pe(pool, ("BPV", BH - 1))
                        pool.dma_start(xc, ins["ctx_2"][0].rearrange("(t p) d -> p t d", p=P)).then_inc(xc_in, 16)
                        pool.dma_start(fw, ins["final_norm_w"].partition_broadcast(P)).then_inc(fw_in, 16)
                        for t in range(CT):
                            norm_roots("c0", t)
                        for t in range(TT):
                            norm_roots("F", t)
                        for t in range(TT):
                            norm_roots("C0", t)
                        pool.wait_ge(x_final, TT)
                        pool.dma_start(x_dram[0].rearrange("(t p) d -> p t d", p=P), x).then_inc(x_saved, 16)
                elif kind == "BS":
                    h = key[1]
                    b = h % 2
                    pool.wait_ge(dil_probs, h + 1)
                    stat_of = lambda g, order: b_stat[:, b, g, order].rearrange("p c n -> p (c n)")
                    natural = lambda d: d.rearrange("c (b i) -> i (c b)", b=TT)
                    strided = lambda d: d.rearrange("c (i b) -> i c b", b=DIL)
                    pairs = [(st0_dram[h], 0, natural, strided)]
                    pairs += [(st12_dram[h, 2 * g - 2:2 * g], g, strided, natural) for g in (1, 2)]
                    for d, g, save, _ in pairs:
                        pool.dma_start(save(d), b_stat[:, b, g, 1] if g else stat_of(g, 0),
                                       allow_slow_non_contiguous=True).then_inc(st_saved, 16)
                    pool.wait_ge(st_saved, 48 * (h + 1))
                    for d, g, _, load in pairs:
                        pool.dma_start(stat_of(g, 0) if g else b_stat[:, b, g, 1], load(d),
                                       allow_slow_non_contiguous=True).then_inc(st_in, 16)
                elif kind == "nv":
                    l = key[1]
                    evacuated(pool, key, 3)
                    pool.dma_start(nv_dram[l].rearrange("(t p) c -> p t c", p=P), vnat).then_inc(nv_saved, 16)
                    pool.wait_ge(nv_saved, 16 * (l + 1))
                    grid = nv_dram[l].rearrange("(r c) d -> r c d", c=GRID_W)
                    for n in range(NQB):
                        for k in range(2):
                            for r in range(4):
                                pool.dma_start(vstrip[r * STRIP:(r + 1) * STRIP, n, k, :],
                                               grid[4 * k + r, STRIP_START[n]:STRIP_START[n] + STRIP, :]).then_inc(strips_in, 16)
                    self_bias(pool, l, 0)
                elif kind == "nS" and key[2] + 1 < NH:
                    self_bias(pool, key[1], key[2] + 1)
                elif kind == "dPV":
                    l, t, h = key[1:]
                    if h == DH - 1:
                        n = diff_tile(l, t)
                        pool.wait_ge(o_sq, n + 1)
                        root(o_rs[:, t, :], o_ss[:, t, :], DV, o_rstd)
                elif kind == "cvT":
                    l, st = key[1:]
                    for i in range((TT, CT)[st] // 2):
                        n = ln_pair(l, st, i)
                        pool.wait_ge(ln_var, n + 1)
                        rs = ln_rs[:, i]
                        chained(nc.gpsimd.tensor_scalar(rs, ln_mv[:, i, :, 1], 1.0, EPS, ALU.mult, ALU.add))
                        nc.gpsimd.tensor_tensor(rs, rs, minus_half[:, 0:2], ALU.pow).then_inc(ln_rstd, 1)
                elif kind == "yo":
                    l, t = key[1:]
                    n = l * (TT + CT) + t
                    b = n % 2
                    pool.wait_ge(y_sq, 2 * n + 2)
                    if n >= 2:
                        pool.wait_ge(x_new, n - 1)
                    chained(nc.gpsimd.tensor_tensor(y_rs[:, b, 0:1], y_ss[:, b, 0:1], y_ss[:, b, 1:2], ALU.add))
                    root(y_rs[:, b, 1:2], y_rs[:, b, 0:1], D, y_rstd)
                    if l == 0:
                        norm_roots("C1" if t < TT else "c1", t % TT)
                    if l == 0 and t == TT - 1:
                        pool.wait_ge(x_new, TT)
                        pool.dma_start(x_dram[1].rearrange("(t p) d -> p t d", p=P), x).then_inc(x_saved, 16)

        @block.scalar
        def _(act):
            count = {"chain": 0}

            def chained(ins):
                count["chain"] += 1
                ins.then_inc(act_chain, 1)
                act.wait_ge(act_chain, count["chain"])

            def free(ins):
                ins.then_inc(evac["a"], 1)

            def move(out, in_, scale=1.0):
                return nc.scalar.activation(out, in_, ACT.Copy, scale=scale)

            def square(ph, t):
                src, dst, _, ss, _ = norms[ph]
                nc.scalar.activation(dst[:, t], src[:, t], ACT.Square, accum_out=ss[:, t:t + 1]).then_inc(sq_done, 1)

            def rows(r, src, n):
                act.dma_start(vrows[r:r + n, :], src).then_inc(vecs_in, 16)

            act.dma_start(ident[:, :], consts["ident"]).then_inc(vecs_in, 16)
            rows(V_C, ins["c_2"][0].rearrange("(r c) -> r c", c=P), KT)
            rows(V_C + KT, ins["c_ctx_2"].rearrange("(r c) -> r c", c=P), KT)
            rows(V_MEM, ins["mem_norm_w"].rearrange("(r c) -> r c", c=P), KT)
            rows(V_NORM, ins["norm_w"].rearrange("l (r c) -> (l r) c", c=P), 2 * KT)
            rows(V_GPRE, ins["g_pre_2"].rearrange("l (r c) -> (l r) c", c=P), 2 * KT)
            rows(V_GPOST, ins["g_post_2"].rearrange("l (r c) -> (l r) c", c=P), 2 * KT)

            for key, _ in steps:
                kind = key[0]
                if kind == "vecT" and key[1] == 0:
                    evacuated(act, key)
                    nc.scalar.activation(siluc[:, :, :].rearrange("p k c -> p c k"),
                                         vec[:, V_C:V_C + 2 * KT].rearrange("p (c k) -> p c k", c=2),
                                         ACT.Silu).then_inc(silu_c, 1)
                    act.wait_ge(mem_in, 16)
                    for t in range(CT):
                        square("m", t)
                elif kind == "vecT":
                    act.wait_ge(lam_dots, 1)
                    nc.scalar.activation(lam_st, lam_st, ACT.Exp).then_inc(lam_exps, 1)
                elif kind == "split":
                    n = key[1]
                    at_, w, hi, _ = split_weights(n)
                    act.wait_ge(w_full[at_ % WSLOTS], loaded(at_))
                    if n >= UNITS:
                        done_before(act, split_list[n - UNITS])
                        if n == before_mem or n == before_mem + 1:
                            read_by_pe(act, ("mPV", "B"))
                    else:
                        read_by_pe(act, ("wout", "A"))
                    move(hi, w).then_inc(split_hi, 1)
                elif kind == "memT":
                    for i in (0, 2):
                        b = full(act, key, i)
                        move(memT[:, 2 * i], b[:, 0:NMEM], vec[:, V_MEM + 2 * i:V_MEM + 2 * i + 1])
                        free(move(memT[:, 2 * i + 1], b[:, NMEM:], vec[:, V_MEM + 2 * i + 1:V_MEM + 2 * i + 2]))
                elif kind == "memkv":
                    if key[1] == 0:
                        act.wait_ge(x_in, 16)
                        for t in range(TT):
                            square("A", t)
                    for i, dst in enumerate((memk, memv)):
                        free(move(dst[:, key[1]], full(act, key, i)[:, :].rearrange("p (a b) -> p a b", a=2)))
                elif key == ("hT", "B"):
                    for k in range(KT):
                        c = V_NORM + KT + k
                        move(hT_hi[:, k], full(act, key, k)[:, :], vec[:, c:c + 1]).then_inc(hi_ready, 1)
                elif kind == "hT":
                    for k in range(0, KT, 2):
                        b = full(act, key, k)
                        if key[1] == "A":
                            c = V_NORM + k
                            free(move(hT[:, k], b[:, :], vec[:, c:c + 1]))
                        else:
                            l = int(key[1][1])
                            free(nc.scalar.activation(hT[:, k], b[:, :], ACT.Identity, bias=modv[:, l, 1, k, 0:1],
                                                      scale=modv[:, l, 0, k, 0:1]))
                elif kind == "hcT":
                    l = key[1]
                    for i in (0, 2):
                        b = full(act, key, i)
                        for k in (2 * i, 2 * i + 1):
                            ins_ = nc.scalar.activation(hcT[:, k], b[:, (k % 2) * NMEM:(k % 2 + 1) * NMEM], ACT.Identity,
                                                        bias=modv[:, l, 1, k, 1:2], scale=modv[:, l, 0, k, 1:2])
                        free(ins_)
                elif kind == "Av":
                    for i in range(0, 8, 2):
                        half, t = divmod(i, TT)
                        free(move(gv[:, t, half * 384:half * 384 + 384], full(act, key, i)[:, 0:384]))
                elif kind == "Aglow":
                    free(move(glow, full(act, key, 0)[0:GRANK, :]))
                elif kind == "Aproj":
                    h = key[1]
                    b = h % 2
                    t1, t2, t3, t4 = (gt[:, b, i] for i in range(4))
                    free(move(gq[:, h], full(act, key, 0)[0:GK, :], GK ** -0.5))
                    z = full(act, key, 2)[0:GK, :]
                    if h == 0:
                        act.wait_ge(gla_in, 64)
                    if h >= 2:
                        act.wait_ge(gla_qin, h - 1)
                    nc.scalar.activation(t1, z, ACT.Abs, bias=bgate[:, h:h + 1]).then_inc(gla_abs, 1)
                    act.wait_ge(gla_abs, h + 1)
                    chained(nc.scalar.activation(t1, t1, ACT.Exp, scale=-1.0))
                    nc.scalar.activation(t1, t1, ACT.Ln, bias=1.0).then_inc(gla_soft, 1)
                    act.wait_ge(gla_cum, h + 1)
                    nc.scalar.activation(t1, t3, ACT.Exp, scale=1.0 / GTAU).then_inc(gla_exps, 1)
                    nc.scalar.activation(t2, t3, ACT.Exp, scale=-1.0 / GTAU).then_inc(gla_exps, 1)
                    nc.scalar.activation(t4, t4, ACT.Exp, scale=1.0 / GTAU).then_inc(gla_exps, 1)
                elif kind == "AA":
                    h = key[1]
                    if h >= 2:
                        read_by_pe(act, ("AdS", h - 2))
                    free(move(gkot[:, h % 2], full(act, key, 1)[:, 0:TT * GK].rearrange("p (t d) -> p t d", d=GK)))
                elif kind == "Ao":
                    h = key[1]
                    for i in range(2):
                        b = full(act, key, i)
                        for j in range(2):
                            t = 2 * i + j
                            ins_ = nc.scalar.activation(go[:, t, h * GV:(h + 1) * GV], b[:, j * GV:(j + 1) * GV],
                                                        ACT.Square, accum_out=gla_ss[:, h, t:t + 1])
                        ins_.then_inc(gla_sq, 1)
                        act.wait_ge(gla_rstd, 2 * h + i + 1)
                        for j in range(2):
                            t = 2 * i + j
                            ins_ = move(go[:, t, h * GV:(h + 1) * GV], b[:, j * GV:(j + 1) * GV], gla_rs[:, h, t:t + 1])
                        free(ins_)
                elif kind == "gate":
                    ph, i = key[1:]
                    free(nc.scalar.activation(branch[:, i], full(act, key, 0)[:, :], ACT.Silu))
                    if njobs[key] == 2:
                        free(nc.scalar.activation(cbranch[:, i], full(act, key, 1)[:, 0:NMEM], ACT.Silu))
                elif kind == "qm":
                    free(move(qmem[key[1]][:, 0], full(act, key, 0)[:, :]))
                elif kind == "mS":
                    ph = "AB".index(key[1])
                    for i in range(8):
                        b = bank(key, i)
                        act.wait_ge(mem_negmax, 8 * ph + i + 1)
                        for j in range(2):
                            ins_ = nc.scalar.activation(mprob[:, i, j], b[:, j * NMEM:(j + 1) * NMEM], ACT.Exp,
                                                        bias=m_neg[:, ph, i, j:j + 1], scale=mem_scale,
                                                        accum_out=m_sum[:, ph, i, j:j + 1])
                        free(ins_)
                elif kind == "mT":
                    for i in range(0, 8, 2):
                        free(move(mprobT[:, i % 2::2, :, (i // 2) * P:(i // 2 + 1) * P],
                                  full(act, key, i)[:, :].rearrange("p (h k q) -> p h k q", h=2, k=CT)))
                elif kind == "wout":
                    ph = key[1]
                    if ph == "A":
                        for t in range(TT):
                            evacuated(act, key, 2 * t + 1)
                            square("B", t)
                    else:
                        act.wait_ge(xc_in, 16)
                        act.wait_ge(gate_saved, 64)
                        read_by_pe(act, ("BPV", BH - 1))
                        for t in range(CT):
                            square("c0", t)
                        for t in range(TT):
                            evacuated(act, key, 2 * t + 1)
                            square("F", t)
                elif kind == "norms":
                    for t in range(TT):
                        act.wait_ge(x_final, t + 1)
                        square("C0", t)
                elif kind == "Bproj":
                    h, g = key[1:]
                    if h >= 2:
                        read_by_pe(act, ("BS", h - 2))
                    for i in range(2):
                        b, dst = full(act, key, i), bqk[:, h % 2, g, i]
                        if g == 0:
                            free(move(dst, b[:, :]))
                        else:
                            free(move(dst.rearrange("p (b i) -> p b i", b=DIL), b[:, :].rearrange("p (i b) -> p b i", b=DIL)))
                elif kind == "BS":
                    h = key[1]
                    if h:
                        read_by_pe(act, ("BPV", h - 1))
                    for g in range(BG):
                        free(move(bv[:, g], full(act, key, g)[:, :].rearrange("p (b d) -> p b d", d=BD)))
                    act.wait_ge(dil_negmax, h + 1)
                    for g in range(BG):
                        for n in range(TT):
                            v = bprob_tile(g, n)
                            ins_ = nc.scalar.activation(v, v, ACT.Exp, bias=b_neg[:, h % 2, g, n:n + 1],
                                                        accum_out=b_stat[:, h % 2, g, int(g > 0), 1, n:n + 1])
                    ins_.then_inc(dil_probs, 1)
                elif kind == "Bw":
                    h = key[1]
                    act.wait_ge(dil_diff, h + 1)
                    nc.scalar.activation(b_w, b_w, ACT.Exp).then_inc(dil_exp, 1)
                elif kind == "BT":
                    h = key[1]
                    if h:
                        read_by_pe(act, ("BPV", h - 1))
                    for i in (0, 2):
                        n0, n = PT_BANKS[i]
                        free(move(bprobT[:, n0:n0 + n], full(act, key, i)[:, 0:n * P].rearrange("p (n q) -> p n q", q=P)))
                elif kind == "BPV":
                    h = key[1]
                    if h:
                        act.wait_ge(dil_out, h)
                    free(move(bo12.rearrange("p (i b) -> p b i", b=DIL), full(act, key, 1)[:, :].rearrange("p (b i) -> p b i", b=DIL)))
                elif kind == "nk":
                    for j in range(3):
                        free(move(nkT[:, j], full(act, key, j)[:, :]))
                elif kind == "nv":
                    act.wait_ge(x_saved, 16 * (key[1] + 1))
                    for t in range(TT):
                        free(move(vnat[:, t], full(act, key, t)[:, 0:NH * ND]))
                elif kind == "nq":
                    for j in range(3):
                        free(move(nqT[:, j].rearrange("p (n r c) -> p n r c", n=NQB, r=GRID_H),
                                  full(act, key, j)[:, :].rearrange("p (r n c) -> p n r c", r=GRID_H, n=NQB), ND ** -0.5))
                elif kind == "cv":
                    l = key[1]
                    for st, n in ((0, T), (1, NMEM))[0:1 if njobs[key] == 4 else 2]:
                        for f in range(CF):
                            i = 4 * st + 2 * f
                            m = conv_inputs(l, st, f)
                            if m >= 2:
                                evacuated(act, *conv_input_at(m - 2))
                            free(nc.scalar.activation(csig[:, f, 0:n], full(act, key, i)[:, 0:n], ACT.Sigmoid))
                elif kind == "dP":
                    l, what, t = key[1:]
                    if t >= TT:
                        n = stage_at(key)
                        if n >= 2:
                            read_by_pe(act, stage_key(n - 2))
                        free(move(dstage[:, n % 2, :, 0:DD], full(act, key, 0)[:, 0:384].rearrange("p (h d) -> p h d", d=DD)))
                elif kind == "dX":
                    l, what, t = key[1:]
                    dst = dkT[:, :, t * P:(t + 1) * P] if what == "k" else dqT[t // TT][:, :, (t % TT) * P:(t % TT + 1) * P]
                    free(move(dst, full(act, key, 0)[:, :].rearrange("p (h q) -> p h q", q=P)))
                elif kind == "dv" and key[2] % 2 == 0:
                    free(move(dv[:, key[2]], full(act, key, 0)[:, 0:384]))
                elif kind == "nS":
                    l, h = key[1:]
                    act.wait_ge(na_negmax, l * NH + h + 1)
                    for n in range(NQB):
                        nc.scalar.activation(nprob[:, n, 0:256], nprob[:, n, 0:256], ACT.Exp, bias=n_neg[:, n:n + 1],
                                             accum_out=n_s[:, 0, n:n + 1])
                        free(nc.scalar.activation(nprob[:, n, 256:512], bank(key, n)[:, 256:512], ACT.Exp,
                                                  bias=n_neg[:, n:n + 1], accum_out=n_s[:, 1, n:n + 1]))
                elif kind == "nT":
                    l, h = key[1:]
                    if h:
                        read_by_pe(act, ("nPV", l, h - 1))
                    else:
                        act.wait_ge(nv_saved, 16 * (l + 1))
                    for n in (0, 2):
                        free(move(nprobT[:, n], full(act, key, n)[:, :].rearrange("p (k q) -> p k q", q=P)))
                elif kind == "cS":
                    l, h = key[1:]
                    if h >= 4:
                        read_by_pe(act, ("cT", l, h - 4))
                    act.wait_ge(ctx_negmax, h + 1)
                    for t in range(CT):
                        ins_ = nc.scalar.activation(cprob[:, h % 4, t], bank(key, 0)[:, t * NMEM:(t + 1) * NMEM], ACT.Exp,
                                                    bias=c_neg[:, h % 2, t:t + 1], accum_out=c_s[:, h % 2, t:t + 1])
                    free(ins_)
                elif kind == "cT":
                    l, h = key[1:]
                    if h >= 4:
                        read_by_pe(act, ("cPV", l, h - 4))
                    free(move(cprobT[:, h % 4].rearrange("p k (t q) -> p t k q", t=CT),
                              full(act, key, 0)[:, :].rearrange("p (t k q) -> p t k q", t=CT, k=CT)))
                elif kind == "dS":
                    l, t, h = key[1:]
                    n = diff_at(l, t, h)
                    if (t, h) == (0, 0):
                        read_by_pe(act, ("gate", f"C{l}", KT - 1))
                    elif n >= 3:
                        read_by_pe(act, diff_step("dT", n - 3))
                    for i in range(njobs[key]):
                        half, part, k0, w = score_part(t, i)
                        act.wait_ge(diff_negmax, 2 * n + half + 1)
                        free(nc.scalar.activation(dprob[n % 3][:, half, k0:k0 + w], bank(key, i)[:, 0:w], ACT.Exp,
                                                  bias=d_neg[:, n % 4, half:half + 1], scale=diff_scale,
                                                  accum_out=d_s[:, n % 4, 2 * part + half:2 * part + half + 1]))
                elif kind == "dT":
                    l, t, h = key[1:]
                    n = diff_at(l, t, h)
                    if n >= 2:
                        read_by_pe(act, diff_step("dPV", n - 2))
                    w = 4 if t < TT else 2
                    k0 = 0 if t < TT else TT
                    free(move(dwT[:, n % 2, k0:k0 + w], full(act, key, 0)[:, 0:w * P].rearrange("p (k q) -> p k q", q=P)))
                elif kind == "dPV":
                    l, t, h = key[1:]
                    n = diff_at(l, t, h)
                    free(move(otok[t // TT][:, t % TT, h * DV:(h + 1) * DV], full(act, key, 0)[:, 0:DV], d_rec[:, n % 4, 0:1]))
                elif kind == "cvZ":
                    l, st = key[1:]
                    n = (T, NMEM)[st]
                    for f in range(CF):
                        c = 2 * l + f
                        free(nc.scalar.activation(csilu[st][:, f], full(act, key, f)[:, 0:n], ACT.Silu,
                                                  bias=vec[:, V_LB + c:V_LB + c + 1], scale=vec[:, V_LG + c:V_LG + c + 1]))
                elif kind == "yo":
                    l, t = key[1:]
                    n = l * (TT + CT) + t
                    if n >= 2:
                        act.wait_ge(y_rstd, n - 1)
                    for i in range(2):
                        b = full(act, key, i)
                        if n:
                            act.wait_ge(y_sq, 2 * n - 2 + i + 1)
                        nc.scalar.activation(yjunk[:, i * BANK:(i + 1) * BANK], b[:, :], ACT.Square,
                                             accum_out=y_ss[:, n % 2, i:i + 1]).then_inc(y_sq, 1)
                    if l == 0:
                        act.wait_ge(x_new, t + 1)
                        square("C1" if t < TT else "c1", t % TT)

        @block.vector
        def _(dve):
            count = {"chain": 0}
            taps = {"lat": 0, "ctx": 0}

            def chained(ins_):
                count["chain"] += 1
                ins_.then_inc(dve_chain, 1)
                dve.wait_ge(dve_chain, count["chain"])

            def free(ins_):
                return ins_.then_inc(evac["v"], 1)

            def mul(out, a, b):
                return nc.vector.tensor_tensor(out, a, b, ALU.mult)

            def scaled(out, a, s):
                return nc.vector.tensor_scalar(out, a, s, None, ALU.mult)

            def norm_scale(ph, t):
                src, dst, _, _, rs = norms[ph]
                dve.wait_ge(rstd_ready, norm_at[ph] + t + 1)
                scaled(dst[:, t], src[:, t], rs[:, t:t + 1]).then_inc(xn_ready, 1)

            def conv_taps(l, st, n):
                name = ("lat", "ctx")[st]
                total = CF * TAPS
                src, dst, width = ((u, y, T), (uc, yc, NMEM))[st]
                for _ in range(n):
                    if taps[name] == total:
                        return
                    tap, f = divmod(taps[name], CF)
                    if tap == 0:
                        evacuated(dve, ("cv", l), 4 * st + 2 * f + 1)
                    w = conv_w[:, f, l * TAPS + tap:l * TAPS + tap + 1]
                    cut = src[:, f, tap:tap + width]
                    if tap == 0:
                        c = V_CB + 2 * l + f
                        ins_ = nc.vector.tensor_scalar(dst[:, f], cut, w, vec[:, c:c + 1], ALU.mult, ALU.add)
                    else:
                        ins_ = nc.vector.scalar_tensor_tensor(dst[:, f], cut, w, dst[:, f], ALU.mult, ALU.add)
                    taps[name] += 1
                    if taps[name] == total:
                        ins_.then_inc(conv_done, 1)
                    else:
                        chained(ins_)

            def o_normalise(l, t):
                dve.wait_ge(o_rstd, diff_tile(l, t) + 1)
                v = otok[t // TT][:, t % TT].rearrange("p (h d) -> p h d", d=DV)
                mul(v, v, o_rs[:, t].unsqueeze(2).to_broadcast([P, DH, DV])).then_inc(o_normed, 1)

            def diff_combine(n):
                l, t, h = all_diff[n]
                evacuated(dve, ("dS", l, t, h))
                rec, s = d_rec[:, n % 4], d_s[:, n % 4]
                if t < TT:
                    chained(nc.vector.tensor_tensor(s[:, 2:4], s[:, 0:2], s[:, 2:4], ALU.add))
                chained(nc.vector.reciprocal(rec[:, 0:2], s[:, 2:4]))
                chained(nc.vector.scalar_tensor_tensor(rec[:, 2:3], s[:, 2:3], lam[:, l:l + 1], rec[:, 1:2], ALU.mult, ALU.mult))
                k0 = 0 if t < TT else T
                p1, p2 = dprob[n % 3][:, 0, k0:], dprob[n % 3][:, 1, k0:]
                nc.vector.scalar_tensor_tensor(p1, p2, rec[:, 2:3], p1, ALU.mult, ALU.add).then_inc(diff_w, 1)

            for key, _ in steps:
                kind = key[0]
                if kind == "vecT" and key[1] == 0:
                    free(nc.vector.tensor_copy(vec[:, 0:V_EARLY], full(dve, key, 0)[:, 0:V_EARLY]))
                    evacuated(dve, key)
                    for t in range(CT):
                        norm_scale("m", t)
                elif kind == "vecT":
                    free(nc.vector.tensor_copy(vec[:, V_EARLY:], full(dve, key, 0)[:, 0:V_ROWS - V_EARLY + 2 * CW_ROWS]))
                    evacuated(dve, key)
                    for l in range(2):
                        chained(scaled(subw[:, l], vec[:, V_SUB + 3 * l:V_SUB + 3 * l + 3], 1.0 - lam_init[l]))
                    dve.wait_ge(lam_in, 64)
                    dve.wait_ge(rpb_saved, 96)
                    for l in range(2):
                        for q in range(2):
                            ins_ = nc.vector.tensor_tensor_reduce(
                                out=lam_junk, in0=lam_v[:, l, 2 * q], in1=lam_v[:, l, 2 * q + 1], scale=1.0,
                                scalar=0.0, op0=ALU.mult, op1=ALU.add, accum_out=lam_st[:, l, q:q + 1])
                            if (l, q) != (1, 1):
                                chained(ins_)
                    ins_.then_inc(lam_dots, 1)
                    dve.wait_ge(lam_exps, 1)
                    for l in range(2):
                        chained(nc.vector.tensor_tensor(lam[:, l:l + 1], lam_st[:, l, 1:2], lam_st[:, l, 0:1], ALU.subtract))
                        chained(nc.vector.tensor_scalar(lam[:, l:l + 1], lam[:, l:l + 1], lam_init[l], None, ALU.subtract))
                elif kind == "mod":
                    l, j = key[1:]
                    cut = modrow[:, j * MODC:(j + 1) * MODC]
                    dve.wait_ge(bmod_in, 16 * (l + 1))
                    free(nc.vector.tensor_tensor(cut, full(dve, key, 0)[0:2, 0:MODC], cut, ALU.add))
                elif kind == "modv":
                    j = key[1]
                    n = chunk_at["mod", 0, j]
                    w = slot(n)
                    dve.wait_ge(w_full[n % WSLOTS], loaded(n))
                    if j:
                        read_by_pe(dve, ("mod", 0, j - 1))
                    for k in range(KT):
                        for c in range(2):
                            if k == 0:
                                ins_ = scaled(modacc[:, c], w[:, k], siluc[:, k, c:c + 1])
                            else:
                                ins_ = nc.vector.scalar_tensor_tensor(modacc[:, c], w[:, k], siluc[:, k, c:c + 1],
                                                                      modacc[:, c], ALU.mult, ALU.add)
                        if k < KT - 1:
                            chained(ins_)
                    ins_.then_inc(mod_sums, 1)
                elif kind == "memkv" and key[1] == 0:
                    for t in range(TT):
                        norm_scale("A", t)
                elif kind == "modT":
                    l = key[1]
                    b = full(dve, key, 0)[:, 0:6 * KT].rearrange("p (s k c) -> p s k c", s=3, c=2)
                    per_feature = lambda r: vec[:, r + l * KT:r + (l + 1) * KT].unsqueeze(2).to_broadcast([P, KT, 2])
                    nc.vector.scalar_tensor_tensor(modv[:, l, 0], b[:, 1], 1.0, per_feature(V_GPRE), ALU.add, ALU.mult)
                    if l == 1:
                        dve.wait_ge(gate_saved, 32)
                    mul(gatev.rearrange("p c k -> p k c"), b[:, 2], per_feature(V_GPOST)).then_inc(gate_row, 1)
                    free(nc.vector.tensor_copy(modv[:, l, 1], b[:, 0]))
                elif kind == "memT":
                    for i in (1, 3):
                        b = full(dve, key, i)
                        c = V_MEM + 2 * i
                        scaled(memT[:, 2 * i], b[:, 0:NMEM], vec[:, c:c + 1])
                        free(scaled(memT[:, 2 * i + 1], b[:, NMEM:], vec[:, c + 1:c + 2]))
                elif key == ("hT", "B"):
                    dve.wait_ge(x0_saved, 16 * TT)
                    for k in range(KT):
                        c = V_NORM + KT + k
                        dve.wait_ge(hi_ready, k + 1)
                        free(nc.vector.scalar_tensor_tensor(hT_lo[:, k], bank(key, k)[:, :], vec[:, c:c + 1],
                                                            hT_hi[:, k].bitcast(F32), ALU.mult, ALU.subtract))
                elif kind == "hT":
                    for k in range(1, KT, 2):
                        b = full(dve, key, k)
                        if key[1] == "A":
                            c = V_NORM + k
                            free(scaled(hT[:, k], b[:, :], vec[:, c:c + 1]))
                        else:
                            l = int(key[1][1])
                            free(nc.vector.tensor_scalar(hT[:, k], b[:, :], modv[:, l, 0, k, 0:1], modv[:, l, 1, k, 0:1],
                                                         ALU.mult, ALU.add))
                elif kind == "hcT":
                    l = key[1]
                    for i in (1, 3):
                        b = full(dve, key, i)
                        for k in (2 * i, 2 * i + 1):
                            ins_ = nc.vector.tensor_scalar(hcT[:, k], b[:, (k % 2) * NMEM:(k % 2 + 1) * NMEM],
                                                           modv[:, l, 0, k, 1:2], modv[:, l, 1, k, 1:2], ALU.mult, ALU.add)
                        free(ins_)
                elif kind == "Av":
                    for i in range(1, 8, 2):
                        half, t = divmod(i, TT)
                        free(nc.vector.tensor_copy(gv[:, t, half * 384:half * 384 + 384], full(dve, key, i)[:, 0:384]))
                elif kind == "Aproj":
                    h = key[1]
                    b = h % 2
                    t1, t2, t3, t4 = (gt[:, b, i] for i in range(4))
                    free(nc.vector.tensor_copy(gk[:, h], full(dve, key, 1)[0:GK, :]))
                    if h == 0:
                        dve.wait_ge(gla_in, 64)
                    if h >= 2:
                        dve.wait_ge(gla_keys, 2 * (h - 1))
                    dve.wait_ge(gla_abs, h + 1)
                    free(nc.vector.tensor_scalar(t2, full(dve, key, 2)[0:GK, :], bgate[:, h:h + 1], 0.0, ALU.add, ALU.min))
                    evacuated(dve, key, 2)
                    dve.wait_ge(gla_soft, h + 1)
                    chained(nc.vector.tensor_tensor(t2, t2, t1, ALU.subtract))
                    chained(nc.vector.tensor_tensor_scan(t3, greset, t2, 0.0, ALU.mult, ALU.add))
                    by_chunk = lambda v: v.rearrange("p (n c) -> p n c", c=GCHUNK)
                    last = by_chunk(t3)[:, :, GCHUNK - 1:GCHUNK].to_broadcast([GK, T // GCHUNK, GCHUNK])
                    nc.vector.tensor_tensor(by_chunk(t4), last, by_chunk(t3), ALU.subtract).then_inc(gla_cum, 1)
                    dve.wait_ge(gla_exps, 3 * h + 3)
                    nc.vector.tensor_copy(gdec[:, h], by_chunk(t1)[:, :, GCHUNK - 1])
                    evacuated(dve, key, 0)
                    mul(gq[:, h], gq[:, h], t1).then_inc(gla_qin, 1)
                elif kind == "AA":
                    h = key[1]
                    if h == 0:
                        dve.wait_ge(gla_zero, 6)
                    if h >= 2:
                        read_by_pe(dve, ("Ao", h - 2))
                    free(nc.vector.copy_predicated(gA[:, h % 2], gmask.unsqueeze(1).to_broadcast([P, TT, P]),
                                                   full(dve, key, 0)[:, :].rearrange("p (t q) -> p t q", q=P)))
                elif kind == "AdS":
                    h = key[1]
                    if h:
                        read_by_pe(dve, ("Ao", h - 1))
                    for n in range(T // GCHUNK - 1):
                        i, j = DS_BANK[n]
                        b = full(dve, key, i)[0:GK, j * GV:(j + 1) * GV]
                        if n == 0:
                            ins_ = nc.vector.tensor_copy(gS[:, 1], b)
                        else:
                            ins_ = nc.vector.scalar_tensor_tensor(gS[:, n + 1], gS[:, n], gdec[:, h, n:n + 1], b,
                                                                  ALU.mult, ALU.add)
                        if n in DS_LAST:
                            free(ins_)
                            evacuated(dve, key, i)
                        else:
                            chained(ins_)
                elif kind == "qm":
                    free(nc.vector.tensor_copy(qmem[key[1]][:, 1], full(dve, key, 1)[:, :]))
                elif kind == "mS":
                    ph = "AB".index(key[1])

                    def mem_normalise(i):
                        evacuated(dve, key, i)
                        chained(nc.vector.reciprocal(m_rec[:, ph, i], m_sum[:, ph, i]))
                        mul(mprob[:, i], mprob[:, i],
                            m_rec[:, ph, i].unsqueeze(2).to_broadcast([P, 2, NMEM])).then_inc(mem_probs, 1)

                    for i in range(8):
                        b = full(dve, key, i)
                        chained(nc.vector.reduce_max(m_max[:, ph, i], b[:, :].rearrange("p (h m) -> p h m", h=2), AX_X))
                        scaled(m_neg[:, ph, i], m_max[:, ph, i], -mem_scale).then_inc(mem_negmax, 1)
                        if i:
                            mem_normalise(i - 1)
                    mem_normalise(7)
                elif kind == "mT":
                    for i in range(1, 8, 2):
                        free(nc.vector.tensor_copy(mprobT[:, i % 2::2, :, (i // 2) * P:(i // 2 + 1) * P],
                                                   full(dve, key, i)[:, :].rearrange("p (h k q) -> p h k q", h=2, k=CT)))
                elif kind == "mPV":
                    for j in range(2):
                        evacuated(dve, ("gate", key[1], 6 + j))
                        free(mul(branch[:, 6 + j], full(dve, key, j)[:, :], branch[:, 6 + j]))
                elif kind == "AoT":
                    for f in range(6):
                        evacuated(dve, ("gate", "A", f))
                        free(nc.vector.scalar_tensor_tensor(branch[:, f], full(dve, key, f)[:, :],
                                                            vec[:, V_GLA + f % 3:V_GLA + f % 3 + 1], branch[:, f],
                                                            ALU.mult, ALU.mult))
                elif kind == "wout":
                    ph = key[1]
                    if ph == "B":
                        dve.wait_ge(x0_back, 16)
                    for i in range(8):
                        t, n = divmod(i, 2)
                        cut = x[:, t, n * BANK:(n + 1) * BANK]
                        free(nc.vector.tensor_tensor(cut, full(dve, key, i)[:, :], cut, ALU.add))
                    if ph == "A":
                        for t in range(TT):
                            norm_scale("B", t)
                    else:
                        read_by_pe(dve, ("BPV", BH - 1))
                        for pad in (u[:, :, 0:HALO], u[:, :, HALO + T:], uc[:, :, 0:HALO], uc[:, :, HALO + NMEM:],
                                    dstage[:, :, :, DD:]):
                            nc.vector.memset(pad, 0.0)
                        for t in range(CT):
                            norm_scale("c0", t)
                elif kind == "norms":
                    dve.wait_ge(fw_in, 16)
                    for t in range(TT):
                        dve.wait_ge(rstd_ready, norm_at["F"] + t + 1)
                        nc.vector.scalar_tensor_tensor(x[:, t], x[:, t], norms["F"][4][:, t:t + 1], fw,
                                                       ALU.mult, ALU.mult).then_inc(x_final, 1)
                    for t in range(TT):
                        norm_scale("C0", t)
                elif kind == "Bproj":
                    h, g = key[1:]
                    if h >= 2:
                        read_by_pe(dve, ("BS", h - 2))
                    if (h, g) == (0, 0):
                        dve.wait_ge(rope_in, 16)
                    b, dst = full(dve, key, 2), bvT[:, h % 2, g]
                    if g == 0:
                        free(nc.vector.tensor_copy(dst, b[:, :]))
                    else:
                        free(nc.vector.tensor_copy(dst.rearrange("p (b i) -> p b i", b=DIL),
                                                   b[:, :].rearrange("p (i b) -> p b i", b=DIL)))
                    evacuated(dve, key, 1)
                    rot = bqk[0:32, h % 2, g]
                    tab = lambda c: dil_rope[:, 2 * (g > 0) + c].unsqueeze(1).to_broadcast([32, 2, T])
                    chained(nc.vector.stream_shuffle(bswap, rot, [(i + 16) % 32 for i in range(32)]))
                    chained(mul(bswap, bswap, tab(1)))
                    chained(mul(rot, rot, tab(0)))
                    nc.vector.tensor_tensor(rot, rot, bswap, ALU.add).then_inc(rope_done, 1)
                    dve.wait_ge(rope_done, BG * h + g + 1)
                elif kind == "BS":
                    h = key[1]
                    p = h % 2
                    if h == 0:
                        dve.wait_ge(const_in, 48)
                    else:
                        read_by_pe(dve, ("BT", h - 1))
                    if h >= 2:
                        dve.wait_ge(st_saved, 48 * (h - 1))
                    for g in range(BG):
                        for n in range(TT):
                            i, lo, m_lo = dil_tile(g, n)
                            v = bprob_tile(g, n)
                            w = v.shape[1]
                            ins_ = nc.vector.tensor_tensor_reduce(
                                out=v, in0=full(dve, key, i)[:, lo:lo + w], in1=dil_mask[:, m_lo:m_lo + w],
                                scale=dil_scale, scalar=-3e38, op0=ALU.add, op1=ALU.max,
                                accum_out=b_stat[:, p, g, int(g > 0), 0, n:n + 1])
                            if n == 3 or (g == 0 and n == 1):
                                free(ins_)
                    evacuated(dve, key, 6)
                    scaled(b_neg[:, p, 0], b_stat[:, p, 0, 0, 0], -1.0)
                    scaled(b_neg[:, p, 1:3], b_stat[:, p, 1:3, 1, 0], -1.0).then_inc(dil_negmax, 1)
                elif kind == "Bw":
                    h = key[1]
                    p = h % 2
                    dve.wait_ge(dil_probs, h + 1)
                    dve.wait_ge(st_in, 48 * (h + 1))
                    top, bot = b_stat[:, p, :, :, 0], b_stat[:, p, :, :, 1]
                    chained(nc.vector.tensor_tensor(b_top, top[:, 0], top[:, 1], ALU.max))
                    chained(nc.vector.tensor_tensor(b_top, b_top, top[:, 2], ALU.max))
                    nc.vector.tensor_tensor(b_w, top, b_top.unsqueeze(1).to_broadcast([P, BG, 2, TT]),
                                            ALU.subtract).then_inc(dil_diff, 1)
                    dve.wait_ge(dil_exp, h + 1)
                    chained(mul(bot, bot, b_w))
                    chained(nc.vector.tensor_tensor(b_rec, bot[:, 0], bot[:, 1], ALU.add))
                    chained(nc.vector.tensor_tensor(b_rec, b_rec, bot[:, 2], ALU.add))
                    chained(nc.vector.reciprocal(b_rec, b_rec))
                    chained(mul(b_w, b_w, b_rec.unsqueeze(1).to_broadcast([P, BG, 2, TT])))
                    scaled(bprob[:, P:2 * P], bprob[:, P:2 * P], b_w[:, 0, 0, 0:1])
                    v = bprob[:, 2 * P:8 * P].rearrange("p (n k) -> p n k", n=3)
                    mul(v, v, b_w[:, 0, 0, 1:4].unsqueeze(2).to_broadcast([P, 3, 2 * P]))
                    v = bprob[:, 8 * P:].rearrange("p (g n k) -> p g n k", g=2, n=TT)
                    mul(v, v, b_w[:, 1:3, 1].unsqueeze(3).to_broadcast([P, 2, TT, P])).then_inc(dil_weighted, 1)
                elif kind == "BT":
                    h = key[1]
                    if h:
                        read_by_pe(dve, ("BPV", h - 1))
                    for i in (1, 3):
                        n0, n = PT_BANKS[i]
                        free(nc.vector.tensor_copy(bprobT[:, n0:n0 + n],
                                                   full(dve, key, i)[:, 0:n * P].rearrange("p (n q) -> p n q", q=P)))
                elif kind == "BPV":
                    h = key[1]
                    evacuated(dve, key, 1)
                    if h:
                        dve.wait_ge(dil_out, h)
                    free(nc.vector.tensor_tensor(bsum, full(dve, key, 0)[:, :], bo12, ALU.add))
                    evacuated(dve, key, 0)
                    evacuated(dve, ("gate", "B", h))
                    mul(branch[:, h], branch[:, h], bsum).then_inc(dil_out, 1)
                elif kind == "gate" and key[1][0] == "C":
                    conv_taps(int(key[1][1]), 0, 6)
                elif kind == "nkc":
                    taps.update(lat=0, ctx=0)
                    for j in range(3):
                        free(nc.vector.tensor_copy(nkcT[:, j], full(dve, key, j)[:, 0:NMEM]))
                elif kind == "nv":
                    for t in range(CT):
                        free(nc.vector.tensor_copy(vctx[:, t], full(dve, key, TT + t)[:, 0:NH * ND]))
                elif kind == "nq":
                    for j in range(3, njobs[key]):
                        free(scaled(nqcT[:, j - 3], full(dve, key, j)[:, 0:NMEM], ND ** -0.5))
                elif kind == "cv":
                    l = key[1]
                    for st in range(njobs[key] // 4):
                        n, dst = ((T, u), (NMEM, uc))[st]
                        for f in range(CF):
                            i = 4 * st + 2 * f
                            evacuated(dve, key, i)
                            free(mul(dst[:, f, HALO:HALO + n], full(dve, key, i + 1)[:, 0:n], csig[:, f, 0:n]))
                elif kind == "dP":
                    l, what, t = key[1:]
                    if t < TT:
                        n = stage_at(key)
                        if n >= 2:
                            read_by_pe(dve, stage_key(n - 2))
                        b = full(dve, key, 0)[:, 0:384]
                        st = dstage[:, n % 2, :, 0:DD]
                        cos = diff_rope[:, 0, t].unsqueeze(1).to_broadcast([P, 2 * DH, DD])
                        chained(mul(st, b.rearrange("p (h d) -> p h d", d=DD), cos))
                        pairs = b.rearrange("p (h a r d) -> p h a r d", h=2 * DH, a=2, r=2)
                        swap = dswap.rearrange("p h (a r d) -> p h a r d", a=2, r=2)
                        sin = diff_rope[:, 1, t].rearrange("p (a r d) -> p a r d", a=2, r=2)
                        for r in range(2):
                            ins_ = mul(swap[:, :, :, r], pairs[:, :, :, 1 - r],
                                       sin[:, :, r].unsqueeze(1).to_broadcast([P, 2 * DH, 2, DD // 4]))
                        free(ins_)
                        evacuated(dve, key)
                        nc.vector.tensor_tensor(st, st, dswap, ALU.add).then_inc(diff_staged, 1)
                        dve.wait_ge(diff_staged, roped_at(key) + 1)
                elif kind == "dv":
                    if key[2] % 2:
                        free(nc.vector.tensor_copy(dv[:, key[2]], full(dve, key, 0)[:, 0:384]))
                    conv_taps(key[1], 0, 4)
                elif kind == "nS":
                    l, h = key[1:]
                    dve.wait_ge(bias_ready, l * NH + h + 1)
                    if h:
                        read_by_pe(dve, ("nT", l, h - 1))
                    else:
                        dve.wait_ge(x_saved, 16 * (l + 1))
                    for n in range(NQB):
                        b = full(dve, key, n)
                        chained(nc.vector.reduce_max(n_ctx[:, n:n + 1], b[:, 256:512], AX_X))
                        ins_ = nc.vector.tensor_tensor_reduce(
                            out=nprob[:, n, 0:256], in0=b[:, 0:256], in1=bias[:, h % 2, BIAS_KIND[n]], scale=1.0,
                            scalar=n_ctx[:, n:n + 1], op0=ALU.add, op1=ALU.max, accum_out=n_max[:, n:n + 1])
                    chained(ins_)
                    scaled(n_neg, n_max, -1.0).then_inc(na_negmax, 1)
                elif kind == "nW":
                    l, h = key[1:]
                    evacuated(dve, ("nS", l, h))
                    chained(nc.vector.tensor_tensor(n_rec[:, 0], n_s[:, 0], n_s[:, 1], ALU.add))
                    chained(nc.vector.reciprocal(n_rec[:, 1], n_rec[:, 0]))
                    for n in range(NQB):
                        ins_ = scaled(nprob[:, n], nprob[:, n], n_rec[:, 1, n:n + 1])
                    ins_.then_inc(na_probs, 1)
                elif kind == "nT":
                    l, h = key[1:]
                    if h:
                        read_by_pe(dve, ("nPV", l, h - 1))
                    else:
                        dve.wait_ge(nv_saved, 16 * (l + 1))
                    for n in (1, 3):
                        free(nc.vector.tensor_copy(nprobT[:, n], full(dve, key, n)[:, :].rearrange("p (k q) -> p k q", q=P)))
                elif kind == "nPV":
                    l, h = key[1:]
                    lo = 64 * (h % 2)
                    evacuated(dve, ("gate", f"C{l}", h // 2), 0)
                    v = branch[lo:lo + 64, h // 2].rearrange("p (r n c) -> p n r c", r=GRID_H, n=NQB)
                    b = full(dve, key, 0)[lo:lo + 64, :].rearrange("p (n r c) -> p n r c", n=NQB, r=GRID_H)
                    free(mul(v, b, v))
                elif kind == "cS":
                    l, h = key[1:]
                    b = full(dve, key, 0)
                    if h >= 2:
                        evacuated(dve, ("cS", l, h - 2))
                    chained(nc.vector.reduce_max(c_max[:, h % 2], b[:, :].rearrange("p (t k) -> p t k", t=CT), AX_X))
                    scaled(c_neg[:, h % 2], c_max[:, h % 2], -1.0).then_inc(ctx_negmax, 1)
                elif kind == "cW":
                    l, h = key[1:]
                    evacuated(dve, ("cS", l, h))
                    chained(nc.vector.reciprocal(c_rec[:, h % 2], c_s[:, h % 2]))
                    v = cprob[:, h % 4]
                    mul(v, v, c_rec[:, h % 2].unsqueeze(2).to_broadcast([P, CT, NMEM])).then_inc(ctx_probs, 1)
                elif kind == "cPV":
                    l, h = key[1:]
                    lo = 64 * (h % 2)
                    evacuated(dve, ("gate", f"C{l}", h // 2), 1)
                    v = cbranch[lo:lo + 64, h // 2]
                    free(mul(v, full(dve, key, 0)[lo:lo + 64, 0:NMEM], v))
                elif kind == "dS":
                    l, t, h = key[1:]
                    n = diff_at(l, t, h)
                    p = n % 4
                    top = d_max[:, p]
                    if n >= 4 and (t, h) != (0, 0):
                        evacuated(dve, diff_step("dPV", n - 4))
                    for i in range(njobs[key]):
                        half, part, _, w = score_part(t, i)
                        c = 2 * part + half
                        ins_ = nc.vector.reduce_max(top[:, c:c + 1], full(dve, key, i)[:, 0:w], AX_X)
                        if part == 1:
                            chained(ins_)
                            if t < TT:
                                chained(nc.vector.tensor_tensor(top[:, c:c + 1], top[:, half:half + 1], top[:, c:c + 1], ALU.max))
                            scaled(d_neg[:, p, half:half + 1], top[:, c:c + 1], -diff_scale).then_inc(diff_negmax, 1)
                    if (t, h) != (0, 0):
                        diff_combine(n - 1)
                    if l == 0:
                        if (t, h) == (0, 0):
                            read_by_pe(dve, ("gate", "C0", KT - 1))
                        conv_taps(0, 1, 3)
                elif kind == "dT":
                    l, t, h = key[1:]
                    n = diff_at(l, t, h)
                    p = n % 2
                    if (t, h) == diff_items(l)[-2]:
                        diff_combine(n + 1)
                    if t < TT:
                        if n >= 2:
                            read_by_pe(dve, diff_step("dPV", n - 2))
                        free(nc.vector.tensor_copy(dwT[:, p, TT:], full(dve, key, 1)[:, 0:2 * P].rearrange("p (k q) -> p k q", q=P)))
                elif kind == "dPV":
                    l, t, h = key[1:]
                    if h == DH - 1:
                        n = diff_tile(l, t)
                        o = otok[t // TT][:, t % TT]
                        evacuated(dve, key)
                        sq = dswap.rearrange("p h d -> p (h d)")
                        chained(mul(sq, o, o))
                        nc.vector.tensor_reduce(o_ss[:, t], sq.rearrange("p (h d) -> p h d", d=DV), AX_X,
                                                ALU.add).then_inc(o_sq, 1)
                    elif h == 0 and t:
                        o_normalise(l, t - 1)
                elif kind == "doT":
                    l, st = key[1:]
                    if (l, st) != (0, 0):
                        o_normalise(l, TT + CT - 1 if st else TT - 1)
                    n, dst = ((T, branch), (NMEM, cbranch))[st]
                    for f in range(3):
                        evacuated(dve, ("gate", f"C{l}", 3 + f), st)
                        free(nc.vector.scalar_tensor_tensor(dst[:, 3 + f], full(dve, key, f)[:, 0:n], subw[:, l, f:f + 1],
                                                            dst[:, 3 + f], ALU.mult, ALU.mult))
                elif kind == "cvT":
                    l, st = key[1:]
                    conv_taps(l, st, CF * TAPS)
                    pairs = range((TT, CT)[st] // 2)
                    for i in pairs:
                        b = full(dve, key, i)
                        for j in range(2):
                            chained(nc.vector.bn_stats(ln_st, b[:, j * CW:(j + 1) * CW]))
                            ins_ = nc.vector.bn_aggr(ln_mv[:, i, j], ln_st)
                            if j == 0:
                                chained(ins_)
                        ins_.then_inc(ln_var, 1)
                        if i + 1 in pairs:
                            dve.wait_ge(ln_var, ln_pair(l, st, i) + 1)
                    for i in pairs:
                        b = bank(key, i)
                        dve.wait_ge(ln_rstd, ln_pair(l, st, i) + 1)
                        for j in range(2):
                            ins_ = nc.vector.tensor_scalar(czn[st][:, 2 * i + j], b[:, j * CW:(j + 1) * CW],
                                                           ln_mv[:, i, j, 0:1], ln_rs[:, i, j:j + 1], ALU.subtract, ALU.mult)
                        free(ins_)
                elif kind == "cvZ":
                    l, st = key[1:]
                    dst = (branch, cbranch)[st]
                    for f in range(CF):
                        evacuated(dve, key, f)
                        evacuated(dve, ("gate", f"C{l}", 6 + f), st)
                        mul(dst[:, 6 + f], dst[:, 6 + f], csilu[st][:, f]).then_inc(ln_done, 1)
                elif kind == "yo":
                    l, t = key[1:]
                    n = l * (TT + CT) + t
                    c = t // TT
                    row = x[:, t] if t < TT else xc[:, t - TT]
                    dve.wait_ge(y_rstd, n + 1)
                    dve.wait_ge(gmul_in, 32 * (l + 1))
                    if t < TT:
                        dve.wait_ge(x_back, 16 * (l + 1))
                    if n:
                        dve.wait_ge(x_new, n)
                    for i in range(2):
                        cut = slice(i * BANK, (i + 1) * BANK)
                        free(nc.vector.scalar_tensor_tensor(ytmp[:, cut], full(dve, key, i)[:, :], y_rs[:, n % 2, 1:2],
                                                            gmul[:, c, cut], ALU.mult, ALU.mult))
                    evacuated(dve, key)
                    nc.vector.tensor_tensor(row, row, ytmp, ALU.add).then_inc(x_new, 1)
                    if l == 0:
                        norm_scale("C1" if t < TT else "c1", t % TT)

        @block.tensor
        def _(pe):
            def done(ins_):
                ins_.then_inc(psum_full, 1)

            def product(out, pairs):
                pairs = list(pairs)
                for i, (lhsT, rhs) in enumerate(pairs):
                    ins_ = nc.tensor.matmul(out, lhsT, rhs, start=i == 0, stop=i == len(pairs) - 1)
                return ins_

            def features(out, w, c0, m, rhs):
                return product(out, ((w[:, k, c0:c0 + m], rhs[:, k]) for k in range(KT)))

            def split_features(key, i):
                n = split_at[key, i]
                _, _, hi, lo = split_weights(n)
                pe.wait_ge(split_lo, n + 1)
                b = claim(pe, key, i)
                done(product(b[:, :], (pair for k in range(KT) for pair in (
                    (hi[:, k], hT_hi[:, k]), (hi[:, k], hT_lo[:, k]), (lo[:, k], hT_hi[:, k])))))

            def tokens(out, lhs, t, w, c0, n):
                return product(out, ((lhs[:, k, t * P:(t + 1) * P], w[:, k, c0:c0 + n]) for k in range(KT)))

            def turn(out, in_):
                n = in_.shape[0]
                return nc.tensor.transpose(out, in_, ident[0:n, 0:n])

            def norm_in(ph):
                pe.wait_ge(xn_ready, norm_pe[ph])

            for key, _ in steps:
                kind = key[0]
                if kind == "vecT" and key[1] == 0:
                    pe.wait_ge(vecs_in, VECS_IN)
                    done(turn(claim(pe, key, 0)[:, 0:V_EARLY], vrows))
                elif kind == "vecT":
                    pe.wait_ge(vecs2_in, VECS2_IN)
                    late = V_ROWS - V_EARLY
                    b = claim(pe, key, 0)
                    turn(b[:, 0:late], vrows2)
                    for f in range(CF):
                        ins_ = turn(b[:, late + f * CW_ROWS:late + (f + 1) * CW_ROWS], crows[:, f * P:(f + 1) * P])
                    done(ins_)
                elif kind == "mod":
                    l, j = key[1:]
                    pe.wait_ge(silu_c, 1)
                    b = claim(pe, key, 0)
                    if l == 0:
                        pe.wait_ge(mod_sums, j + 1)
                        done(product(b[0:2, 0:MODC], ((pick[:, c], modacc[:, c]) for c in range(2))))
                    else:
                        w = chunk(pe, key)
                        done(product(b[0:2, 0:MODC], ((siluc[:, k], w[:, k]) for k in range(KT))))
                elif kind == "modT":
                    l = key[1]
                    evacuated(pe, ("mod", l, MODS - 1))
                    b = claim(pe, key, 0)
                    for c in range(3 * KT):
                        ins_ = turn(b[:, 2 * c:2 * c + 2], modrow[:, c * P:(c + 1) * P])
                    done(ins_)
                elif split_jobs(key):
                    for i in range(njobs[key]):
                        split_features(key, i)
                elif kind == "memT":
                    norm_in("m")
                    for i in range(4):
                        b = claim(pe, key, i)
                        for j in range(2):
                            k = 2 * i + j
                            for t in range(CT):
                                ins_ = turn(b[:, j * NMEM + t * P:j * NMEM + (t + 1) * P], memn[:, t, k * P:(k + 1) * P])
                        done(ins_)
                elif kind == "memkv":
                    l = key[1]
                    w = chunk(pe, key)
                    if l == 0:
                        evacuated(pe, ("memT",), 2)
                        evacuated(pe, ("memT",), 3)
                    b = claim(pe, key, 0)
                    for j in range(2):
                        ins_ = features(b[:, j * NMEM:(j + 1) * NMEM], w, j * P, P, memT)
                    done(ins_)
                    b = claim(pe, key, 1)
                    for t in range(CT):
                        ins_ = tokens(b[:, t * 256:(t + 1) * 256], memT, t, w, 256, 256)
                    done(ins_)
                elif kind == "hT":
                    norm_in(key[1])
                    src = norms[key[1]][1]
                    for k in range(KT):
                        b = claim(pe, key, k)
                        for t in range(TT):
                            ins_ = turn(b[:, t * P:(t + 1) * P], src[:, t, k * P:(k + 1) * P])
                        done(ins_)
                    evacuated(pe, key, 6)
                    evacuated(pe, key, 7)
                elif kind == "hcT":
                    norm_in(f"c{key[1]}")
                    for i in range(4):
                        b = claim(pe, key, i)
                        for j in range(2):
                            k = 2 * i + j
                            for t in range(CT):
                                ins_ = turn(b[:, j * NMEM + t * P:j * NMEM + (t + 1) * P], cxcn[:, t, k * P:(k + 1) * P])
                        done(ins_)
                    evacuated(pe, key, 2)
                    evacuated(pe, key, 3)
                elif kind == "Av":
                    for i in range(8):
                        half, t = divmod(i, TT)
                        w = chunk(pe, ("Av", half))
                        b = claim(pe, key, i)
                        done(tokens(b[:, 0:384], hT, t, w, 0, 384))
                elif kind == "Aglow":
                    w = chunk(pe, ("Av", 1))
                    done(features(claim(pe, key, 0)[0:GRANK, :], w, 384, GRANK, hT))
                elif kind == "Aproj":
                    h = key[1]
                    for i, name in enumerate(("Aq", "Ak")):
                        w = chunk(pe, (name,))
                        done(features(claim(pe, key, i)[0:GK, :], w, h * GK, GK, hT))
                    if h == 0:
                        pe.wait_ge(gla_in, 64)
                        evacuated(pe, ("Aglow",))
                    done(product(claim(pe, key, 2)[0:GK, :], [(wgu[:, h * GK:(h + 1) * GK], glow)]))
                elif kind == "AA":
                    h = key[1]
                    pe.wait_ge(gla_qin, h + 1)
                    pe.wait_ge(gla_keys, 2 * h + 2)
                    b = claim(pe, key, 0)
                    for t in range(TT):
                        cut = slice(t * P, (t + 1) * P)
                        ins_ = product(b[:, cut], [(gkin[:, h % 2, cut], gq[:, h, cut])])
                    done(ins_)
                    b = claim(pe, key, 1)
                    for t in range(TT):
                        ins_ = turn(b[:, t * GK:(t + 1) * GK], gkout[:, h % 2, t * P:(t + 1) * P])
                    done(ins_)
                elif kind == "AdS":
                    h = key[1]
                    evacuated(pe, ("AA", h), 1)
                    if h == 0:
                        evacuated(pe, ("Av",), 6)
                        evacuated(pe, ("Av",), 7)
                    for i in range(4):
                        b = claim(pe, key, i)
                        for n in range(T // GCHUNK - 1):
                            if DS_BANK[n][0] != i:
                                continue
                            t, half = divmod(n, 2)
                            lo = half * GCHUNK
                            ins_ = product(b[0:GK, DS_BANK[n][1] * GV:(DS_BANK[n][1] + 1) * GV],
                                           [(gkot[lo:lo + GCHUNK, h % 2, t], gv[lo:lo + GCHUNK, t, h * GV:(h + 1) * GV])])
                        done(ins_)
                elif kind == "Ao":
                    h = key[1]
                    evacuated(pe, ("AA", h), 0)
                    evacuated(pe, ("AdS", h), 3)
                    for i in range(2):
                        b = claim(pe, key, i)
                        for t in (2 * i, 2 * i + 1):
                            o = b[:, (t % 2) * GV:(t % 2 + 1) * GV]
                            ins_ = nc.tensor.matmul(o, gA[:, h % 2, t], gv[:, t, h * GV:(h + 1) * GV], start=True, stop=False)
                            for half in range(2):
                                lo = half * GCHUNK
                                ins_ = nc.tensor.matmul(o[lo:lo + GCHUNK], gq[:, h, t * P + lo:t * P + lo + GCHUNK],
                                                        gS[:, 2 * t + half], start=False, stop=True)
                        done(ins_)
                elif kind == "gate":
                    ph, i = key[1:]
                    name, c0 = gate_chunk(ph, i)
                    w = chunk(pe, name)
                    done(features(claim(pe, key, 0)[:, :], w, c0, P, hT))
                    if njobs[key] == 2:
                        done(features(claim(pe, key, 1)[:, 0:NMEM], w, c0, P, hcT))
                elif kind == "qm":
                    w = chunk(pe, key)
                    for j in range(2):
                        done(features(claim(pe, key, j)[:, :], w, j * P, P, hT))
                elif kind == "mS":
                    ph = key[1]
                    l = "AB".index(ph)
                    evacuated(pe, ("qm", ph), 0)
                    evacuated(pe, ("qm", ph), 1)
                    for i in range(8):
                        t, odd = divmod(i, 2)
                        lo = odd * MD
                        b = claim(pe, key, i)
                        for j in range(2):
                            ins_ = product(b[:, j * NMEM:(j + 1) * NMEM], [(qmem[ph][lo:lo + MD, j, t * P:(t + 1) * P],
                                                                            memk[lo:lo + MD, l, j])])
                        done(ins_)
                elif kind == "mT":
                    ph = key[1]
                    for i in range(8):
                        pe.wait_ge(mem_probs, 8 * "AB".index(ph) + i + 1)
                        b = claim(pe, key, i)
                        for j in range(2):
                            for k in range(CT):
                                ins_ = turn(b[:, (j * CT + k) * P:(j * CT + k + 1) * P], mprob[:, i, j, k * P:(k + 1) * P])
                        done(ins_)
                elif kind == "mPV":
                    ph = key[1]
                    l = "AB".index(ph)
                    evacuated(pe, ("mT", ph), 6)
                    evacuated(pe, ("mT", ph), 7)
                    for j in range(2):
                        b = claim(pe, key, j)
                        for h in (2 * j, 2 * j + 1):
                            lo = (h % 2) * MD
                            ins_ = product(b[lo:lo + MD, :], ((memv[:, l, k, h * MD:(h + 1) * MD], mprobT[:, h, k])
                                                              for k in range(CT)))
                        done(ins_)
                elif kind == "AoT":
                    evacuated(pe, ("Ao", GH - 1))
                    for f in range(6):
                        b = claim(pe, key, f)
                        for t in range(TT):
                            ins_ = turn(b[:, t * P:(t + 1) * P], go[:, t, f * P:(f + 1) * P])
                        done(ins_)
                elif kind == "wout":
                    ph = key[1]
                    evacuated(pe, ("mPV", ph), 1)
                    if ph == "A":
                        evacuated(pe, ("AoT",), 5)
                    else:
                        pe.wait_ge(dil_out, BH)
                    for i in range(8):
                        t, n = divmod(i, 2)
                        w = chunk(pe, ("wout", ph, n))
                        done(tokens(claim(pe, key, i)[:, :], branch, t, w, 0, WCOLS))
                elif kind == "BS":
                    h = key[1]
                    p = h % 2
                    for g in range(BG):
                        evacuated(pe, ("Bproj", h, g), 2)
                        b = claim(pe, key, g)
                        for n in range(TT):
                            ins_ = turn(b[:, n * P:(n + 1) * P], bvT[:, p, g, n * P:(n + 1) * P])
                        done(ins_)
                    pe.wait_ge(rope_done, BG * (h + 1))
                    for i in range(3, 7):
                        b = claim(pe, key, i)
                        for g in range(BG):
                            for n in range(TT):
                                at_, lo, _ = dil_tile(g, n)
                                if at_ == i:
                                    w = bprob_tile(g, n).shape[1]
                                    ins_ = product(b[:, lo:lo + w], [(bqk[:, p, g, 0, n * P:(n + 1) * P],
                                                                      bqk[:, p, g, 1, (n + 1) * P - w:(n + 1) * P])])
                        done(ins_)
                elif kind == "BT":
                    h = key[1]
                    pe.wait_ge(dil_weighted, h + 1)
                    for i, (n0, n) in enumerate(PT_BANKS):
                        b = claim(pe, key, i)
                        for j in range(n):
                            lo = PT_TILES[n0 + j] * P
                            ins_ = turn(b[:, j * P:(j + 1) * P], bprob[:, lo:lo + P])
                        done(ins_)
                elif kind == "BPV":
                    h = key[1]
                    for i in range(4):
                        evacuated(pe, ("BT", h), i)
                    evacuated(pe, ("BS", h), 2)
                    b = claim(pe, key, 0)
                    for n in range(TT):
                        pairs = [(bv[:, 0, n], bprobT[:, 2 * n])]
                        if n:
                            pairs.append((bv[:, 0, n - 1], bprobT[:, 2 * n - 1]))
                        ins_ = product(b[:, n * P:(n + 1) * P], pairs)
                    done(ins_)
                    b = claim(pe, key, 1)
                    for n in range(TT):
                        ins_ = product(b[:, n * P:(n + 1) * P], [(bv[:, 1, n], bprobT[:, 7 + n]), (bv[:, 2, n], bprobT[:, 11 + n])])
                    done(ins_)
                elif kind == "nkc":
                    w = chunk(pe, ("nk", key[1]))
                    for j in range(3):
                        done(features(claim(pe, key, j)[:, 0:NMEM], w, j * P, P, hcT))
                elif kind in ("nk", "nq"):
                    w = chunk(pe, key)
                    for j in range(njobs[key]):
                        b = claim(pe, key, j)
                        if j < 3:
                            done(features(b[:, :], w, j * P, P, hT))
                        else:
                            done(features(b[:, 0:NMEM], w, (j - 3) * P, P, hcT))
                elif kind == "dv":
                    l, t = key[1:]
                    src, tt = (hT, t) if t < TT else (hcT, t - TT)
                    done(tokens(claim(pe, key, 0)[:, 0:384], src, tt, chunk(pe, ("dv", l)), 0, 384))
                elif kind == "nv":
                    w = chunk(pe, key)
                    for t in range(TT + CT):
                        src, tt = (hT, t) if t < TT else (hcT, t - TT)
                        done(tokens(claim(pe, key, t)[:, 0:384], src, tt, w, 0, 384))
                elif kind == "cv":
                    w = chunk(pe, key)
                    for st in range(njobs[key] // 4):
                        n, src = ((T, hT), (NMEM, hcT))[st]
                        for f in range(CF):
                            done(features(claim(pe, key, 4 * st + 2 * f)[:, 0:n], w, CW + f * P, P, src))
                            done(features(claim(pe, key, 4 * st + 2 * f + 1)[:, 0:n], w, f * P, P, src))
                elif kind == "dP":
                    l, what, t = key[1:]
                    w = chunk(pe, ("d" + what, l))
                    src, tt = (hT, t) if t < TT else (hcT, t - TT)
                    done(tokens(claim(pe, key, 0)[:, 0:384], src, tt, w, 0, 384))
                elif kind == "dX":
                    l, what, t = key[1:]
                    key_p = ("dP", l, what, t)
                    if t < TT:
                        pe.wait_ge(diff_staged, roped_at(key_p) + 1)
                    else:
                        evacuated(pe, key_p)
                    b = claim(pe, key, 0)
                    n = stage_at(key_p)
                    for h in range(DH):
                        ins_ = turn(b[:, h * P:(h + 1) * P], dstage[:, n % 2, 2 * h:2 * h + 2].rearrange("p s d -> p (s d)"))
                    done(ins_)
                elif kind == "nS":
                    l, h = key[1:]
                    lo, j = 64 * (h % 2), h // 2
                    if h == 0:
                        evacuated(pe, ("nk", l))
                        evacuated(pe, ("nkc", l))
                        evacuated(pe, ("nq", l), 2)
                    k = nkT[lo:lo + ND, j].rearrange("p (r c) -> p r c", c=GRID_W)
                    for n in range(NQB):
                        b = claim(pe, key, n)
                        qn = nqT[lo:lo + ND, j, n * P:(n + 1) * P]
                        product(b[:, 0:256], [(qn, k[:, :, STRIP_START[n]:STRIP_START[n] + STRIP])])
                        done(product(b[:, 256:512], [(qn, nkcT[lo:lo + ND, j])]))
                elif kind == "nT":
                    l, h = key[1:]
                    pe.wait_ge(na_probs, l * NH + h + 1)
                    for n in range(NQB):
                        b = claim(pe, key, n)
                        for k in range(4):
                            ins_ = turn(b[:, k * P:(k + 1) * P], nprob[:, n, k * P:(k + 1) * P])
                        done(ins_)
                elif kind == "nPV":
                    l, h = key[1:]
                    lo = 64 * (h % 2)
                    if h == 0:
                        pe.wait_ge(strips_in, 512 * (l + 1))
                        evacuated(pe, ("nv", l), 5)
                    evacuated(pe, ("nT", l, h), 2)
                    evacuated(pe, ("nT", l, h), 3)
                    b = claim(pe, key, 0)
                    cut = slice(h * ND, (h + 1) * ND)
                    for n in range(NQB):
                        v = [vstrip[:, n, 0, cut], vstrip[:, n, 1, cut], vctx[:, 0, cut], vctx[:, 1, cut]]
                        ins_ = product(b[lo:lo + ND, n * P:(n + 1) * P], ((v[k], nprobT[:, n, k]) for k in range(4)))
                    done(ins_)
                elif kind == "cS":
                    l, h = key[1:]
                    lo, j = 64 * (h % 2), h // 2
                    if h == 0:
                        evacuated(pe, ("nq", l), 5)
                    b = claim(pe, key, 0)
                    for t in range(CT):
                        ins_ = product(b[:, t * NMEM:(t + 1) * NMEM], [(nqcT[lo:lo + ND, j, t * P:(t + 1) * P],
                                                                        nkcT[lo:lo + ND, j])])
                    done(ins_)
                elif kind == "cT":
                    l, h = key[1:]
                    pe.wait_ge(ctx_probs, h + 1)
                    b = claim(pe, key, 0)
                    for t in range(CT):
                        for k in range(CT):
                            ins_ = turn(b[:, (t * CT + k) * P:(t * CT + k + 1) * P], cprob[:, h % 4, t, k * P:(k + 1) * P])
                    done(ins_)
                elif kind == "cPV":
                    l, h = key[1:]
                    lo = 64 * (h % 2)
                    evacuated(pe, ("cT", l, h))
                    b = claim(pe, key, 0)
                    done(product(b[lo:lo + ND, 0:NMEM], ((vctx[:, k, h * ND:(h + 1) * ND], cprobT[:, h % 4, k]) for k in range(CT))))
                elif kind == "dS":
                    l, t, h = key[1:]
                    evacuated(pe, ("dX", l, "q", t))
                    if (t, h) == (0, 0):
                        evacuated(pe, ("dX", l, "k", TT + CT - 1))
                    for i in range(njobs[key]):
                        b = claim(pe, key, i)
                        half, _, k0, w = score_part(t, i)
                        lo = half * DPAD
                        q = dqT[t // TT][lo:lo + DD, h, (t % TT) * P:(t % TT + 1) * P]
                        done(product(b[:, 0:w], [(q, dkT[lo:lo + DD, h, k0:k0 + w])]))
                elif kind == "dT":
                    l, t, h = key[1:]
                    n = diff_at(l, t, h)
                    pe.wait_ge(diff_w, n + 1)
                    k0 = 0 if t < TT else TT
                    for i in range(njobs[key]):
                        b = claim(pe, key, i)
                        w = 4 if (t < TT and i == 0) else 2
                        for j in range(w):
                            k = k0 + 4 * i + j
                            ins_ = turn(b[:, j * P:(j + 1) * P], dprob[n % 3][:, 0, k * P:(k + 1) * P])
                        done(ins_)
                elif kind == "dPV":
                    l, t, h = key[1:]
                    n = diff_at(l, t, h)
                    if (t, h) == (0, 0):
                        evacuated(pe, ("dv", l, TT + CT - 2))
                        evacuated(pe, ("dv", l, TT + CT - 1))
                    for i in range(njobs[("dT", l, t, h)]):
                        evacuated(pe, ("dT", l, t, h), i)
                    b = claim(pe, key, 0)
                    tiles = range(TT + CT) if t < TT else range(TT, TT + CT)
                    done(product(b[:, 0:DV], ((dwT[:, n % 2, k], dv[:, k, h * DV:(h + 1) * DV]) for k in tiles)))
                elif kind == "doT":
                    l, st = key[1:]
                    nt = (TT, CT)[st]
                    pe.wait_ge(o_normed, diff_tile(l, (TT if st == 0 else TT + CT) - 1) + 1)
                    for f in range(3):
                        b = claim(pe, key, f)
                        for t in range(nt):
                            ins_ = turn(b[:, t * P:(t + 1) * P], otok[st][:, t, f * P:(f + 1) * P])
                        done(ins_)
                elif kind == "cvT":
                    l, st = key[1:]
                    pe.wait_ge(conv_done, 1 + st if l == 0 else 3)
                    src = (y, yc)[st]
                    for i in range((TT, CT)[st] // 2):
                        b = claim(pe, key, i)
                        for j in range(2):
                            t = 2 * i + j
                            for f in range(CF):
                                ins_ = turn(b[:, j * CW + f * P:j * CW + (f + 1) * P], src[:, f, t * P:(t + 1) * P])
                        done(ins_)
                elif kind == "cvZ":
                    l, st = key[1:]
                    nt = (TT, CT)[st]
                    evacuated(pe, ("cvT", l, st))
                    for f in range(CF):
                        b = claim(pe, key, f)
                        for t in range(nt):
                            ins_ = turn(b[:, t * P:(t + 1) * P], czn[st][:, t, f * P:(f + 1) * P])
                        done(ins_)
                elif kind == "yo":
                    l, t = key[1:]
                    st = t // TT
                    pe.wait_ge(ln_done, CF * (1 + st if l == 0 else 3))
                    evacuated(pe, ("doT", l, st))
                    src, tt = ((branch, t), (cbranch, t - TT))[st]
                    for n in range(2):
                        w = chunk(pe, ("yo", l, n))
                        done(tokens(claim(pe, key, n)[:, :], src, tt, w, 0, WCOLS))


_INS = ['x', 'mem', 'mem_norm_w', 'norm_w', 'w_memkv', 'w_out', 'w_in_a', 'w_gate_up', 'b_gate', 'gla_norm_w', 'w_in_b',
        'final_norm_w', 'c_2', 'ctx_2', 'c_ctx_2', 'w_mod_2', 'b_mod_2', 'g_pre_2', 'g_post_2', 'w_in_2', 'w_out_2',
        'na_rpb_2', 'diff_lq1_2', 'diff_lk1_2', 'diff_lq2_2', 'diff_lk2_2', 'diff_subln_g_2', 'conv_w_2', 'conv_b_2',
        'conv_ln_g_2', 'conv_ln_b_2']


def kernel(**inputs):
    import concourse.bacc as bacc
    from concourse.bass_utils import run_bass_kernel_spmd

    nc = bacc.Bacc("TRN2", target_bir_lowering=False, num_devices=1)
    arrays, ins, consts = {}, {}, {}
    for name in _INS:
        a = np.ascontiguousarray(inputs[name])
        arrays[f"in_{name}"] = a
        ins[name] = nc.dram_tensor(f"in_{name}", a.shape, mybir.dt.from_np(a.dtype), kind="ExternalInput").ap()
    for name, a in constants().items():
        arrays[f"const_{name}"] = a
        consts[name] = nc.dram_tensor(f"const_{name}", a.shape, mybir.dt.from_np(a.dtype), kind="ExternalInput").ap()
    out = nc.dram_tensor("out", (1, T, D), F32, kind="ExternalOutput").ap()
    hybrid_stack_kernel(nc, ins, consts, out)
    r = run_bass_kernel_spmd(nc, [arrays], core_ids=[0])
    return r.results[0]["out"]
```

```python
from contextlib import ExitStack
import math

import numpy as np

import concourse.bass as bass
from concourse import mybir

ALU = mybir.AluOpType
ACT = mybir.ActivationFunctionType
F32 = mybir.dt.float32
I32 = mybir.dt.int32
F32R = mybir.dt.float32r
AX_X = mybir.AxisListType.X

P = 128
D = 1024
KT = D // P
T = 512
TT = T // P
NMEM = 256
CT = NMEM // P
EPS = 1e-6
BANK = 512
BANKS = 8
WCOLS = 512
WSLOTS = 3
WNARROW = 384
MODC = 384
MODS = 3 * D // MODC
UNITS = 4

MH, MD = 4, 64
GH, GK, GV = 4, 96, 192
GCHUNK = 64
GRANK = 16
GTAU = 16.0
BH, BD = 6, 128
BG = 3
DIL = 4
NH, ND = 6, 64
GRID_W, GRID_H = 64, 8
NQB = 4
STRIP = 32
DH, DD, DV = 4, 48, 96
DPAD = 64
CW = 256
CF = CW // P
TAPS = 31
HALO = TAPS // 2
NEG = -1e30

C_NK, C_NV, C_DK, C_DV, C_NQ, C_NG, C_DQ, C_DG, C_CA, C_CB, C_CG = (
    0, 384, 768, 1152, 1536, 1920, 2304, 2688, 3072, 3328, 3584)
A_Q, A_K, A_V, A_G, A_M, A_GATE = 0, 384, 768, 1536, 1552, 1808

V_C, V_MEM, V_NORM, V_GPRE, V_GPOST, V_GLA, V_SUB, V_CB, V_LG, V_LB = 0, 16, 24, 40, 56, 72, 75, 81, 85, 89
V_EARLY = V_GLA
V_ROWS = 93
CW_ROWS = 2 * TAPS
STRIP_START = (0, 8, 24, 32)
BIAS_KIND = (0, 1, 1, 2)
BIAS_OFF = (0, -8, -16)
RPB = NH * 15 * 31
RPB_PAD = 16


def constants():
    f = np.float32
    out = {}
    out["ident"] = np.eye(P, dtype=f)
    j, i = np.arange(P)[:, None], np.arange(P)[None, :]
    out["gla_mask"] = ((j // GCHUNK == i // GCHUNK) & (j <= i)).astype(np.int32)
    t = np.arange(T)
    out["gla_reset"] = np.broadcast_to((t % GCHUNK != 0).astype(f), (GK, T)).copy()
    q, k = np.arange(P)[:, None], np.arange(P)[None, :]
    prev = np.where(k >= q, 0.0, NEG)
    own = np.where(k <= q, 0.0, NEG)
    phase = np.where((k <= q) & ((q - k) % 4 == 0), 0.0, NEG)
    out["dil_mask"] = np.concatenate([prev, own, phase], axis=1).astype(f)
    half = BD // 4 // 2
    inv = (f(500000.0) ** (-np.arange(half, dtype=f) / f(half))).astype(f)
    ang = (t.astype(f)[:, None] * inv[None, :]).astype(f).astype(np.float64)
    cos = np.concatenate([np.cos(ang), np.cos(ang)], axis=1).T
    sin = np.concatenate([-np.sin(ang), np.sin(ang)], axis=1).T
    perm = (np.arange(P)[None, :] * DIL + np.arange(DIL)[:, None]).ravel()
    out["dil_rope"] = np.stack([cos, sin, cos[:, perm], sin[:, perm]], axis=1).astype(f)
    d = DD // 2
    inv = (f(10000.0) ** (-np.arange(0, d, 2, dtype=f) / f(d))).astype(f)
    tab = np.zeros((2, T, 2, 2, d // 2))
    for a, pos in enumerate((t // GRID_W, t % GRID_W)):
        ang = (pos.astype(f)[:, None] * inv[None, :]).astype(f).astype(np.float64)
        tab[0, :, a, :, :] = np.cos(ang)[:, None, :]
        tab[1, :, a, 0, :] = -np.sin(ang)
        tab[1, :, a, 1, :] = np.sin(ang)
    out["diff_rope"] = tab.reshape(2, TT, P, DD).transpose(2, 0, 1, 3).astype(f).copy()
    neg = np.zeros((P, 3, GRID_H, STRIP))
    for kind, block in enumerate((0, 1, 3)):
        cq = block * 16 + np.arange(P) % 16
        start = np.clip(cq - 8, 0, GRID_W - 16)[:, None]
        ck = STRIP_START[block] + np.arange(STRIP)[None, :]
        neg[:, kind] = np.where((ck >= start) & (ck < start + 16), 0.0, NEG)[:, None, :]
    out["na_mask"] = neg.reshape(P, 3, GRID_H * STRIP).astype(f)
    return out


def schedule():
    s = []
    add = lambda readers, *key: s.append((key, readers))
    add("v", "vecT", 0)
    add("avav", "memT")
    add("aa", "memkv", 0)
    add("", "Aw", 0)
    add("aa", "memkv", 1)
    add("v", "vecT", 1)
    add("v" * 8, "hT", "A")
    add("", "Aw", 1)
    add("avavavav", "Av")
    add("a", "Aglow")
    add("avv", "Aproj", 0)
    add("avv", "Aproj", 1)
    add("va", "AA", 0)
    add("avv", "Aproj", 2)
    add("vvvv", "AdS", 0)
    add("va", "AA", 1)
    add("avv", "Aproj", 3)
    for i in (0, 1):
        add("a", "gate", "A", i)
    add("aa", "Ao", 0)
    add("vvvv", "AdS", 1)
    add("va", "AA", 2)
    add("aa", "Ao", 1)
    add("vvvv", "AdS", 2)
    add("va", "AA", 3)
    add("a", "gate", "A", 2)
    add("aa", "Ao", 2)
    add("vvvv", "AdS", 3)
    for i in (3, 4):
        add("a", "gate", "A", i)
    add("aa", "Ao", 3)
    add("av", "qm", "A")
    add("a", "gate", "A", 5)
    add("a" * 8, "mS", "A")
    for i in (6, 7):
        add("a", "gate", "A", i)
    add("av" * 4, "mT", "A")
    add("v" * 6, "AoT")
    add("", "wide", "wout", "A", 0)
    add("", "outs", "wout", "A", 0, (0, 1, 2, 3, 4, 5))
    add("vv", "mPV", "A")
    add("", "wide", "wout", "A", 1)
    add("", "outs", "wout", "A", 0, (6, 7))
    add("v" * 8, "wout", "A")
    add("v" * 8, "hT", "B")
    for i in range(8):
        add("a", "gate", "B", i)
    add("av", "qm", "B")
    add("a" * 8, "mS", "B")
    for g in range(2):
        add("aav", "Bproj", 0, g)
    add("av" * 4, "mT", "B")
    add("aav", "Bproj", 0, 2)
    add("vv", "mPV", "B")

    def modulation(j):
        if 0 < j <= MODS:
            add("v", "mod", 0, j - 1)
        if j < MODS:
            add("", "modv", j)

    for h in range(BH):
        add("aaavvvv", "BS", h)
        if h + 1 < BH:
            if h:
                modulation(2 * h - 1)
            add("aav", "Bproj", h + 1, 0)
            add("", "Bw", h)
            add("aav", "Bproj", h + 1, 1)
            add("avav", "BT", h)
            modulation(2 * h)
            add("aav", "Bproj", h + 1, 2)
            if 2 * h == MODS:
                add("v", "modT", 0)
        else:
            for j in range(MODS - 2):
                if j == MODS - 4:
                    add("", "Bw", h)
                add("v", "mod", 1, j)
            add("avav", "BT", h)
        add("va", "BPV", h)
    add("", "outs", "wout", "B", 0, (6, 7, 0, 1, 2, 3, 4))
    add("v", "mod", 1, MODS - 2)
    add("", "outs", "wout", "B", 0, (5,))
    add("", "wide", "wout", "B", 0)
    add("v", "mod", 1, MODS - 1)
    add("v", "modT", 1)
    add("", "wide", "wout", "B", 1)
    add("v" * 8, "wout", "B")
    for l in range(2):
        both = l == 0
        lat_ctx = "av" * both or "a"
        if both:
            add("v" * 8, "hT", "C0")
            add("vvvv", "hcT", l)
            add("aaa", "nk", l)
            add("vvv", "nkc", l)
        else:
            add("vvv", "nkc", l)
            add("v" * 8, "hT", "C1")
            add("aaa", "nk", l)
        add(lat_ctx * 3, "nq", l)
        add("av" * 3, "nvF", l)
        add("aaaavv", "nv", l)
        gates = [("a" + "a" * both, "gate", f"C{l}", i) for i in range(KT)]
        convs = [("av" + "av" * both, "cv", l, f) for f in range(CF)]
        fill = [gates[0:2], gates[2:4], gates[4:6], convs[0:1], convs[1:2], gates[6:8]]
        for h in range(NH):
            add("aaaa", "nS", l, h)
            if h:
                add("v", "nPV", l, h - 1)
            for i, step in enumerate(fill[h]):
                early = step[1] == "cv"
                if early:
                    add("", "nW", l, h)
                add(*step)
                if i == 0 and not early:
                    add("", "nW", l, h)
            add("avav", "nT", l, h)
        parts = [("av", "dF", l, "v", g) for g in range(3)] + [("av", "dF", l, "k", g) for g in range(3)]
        parts += [(lat_ctx, "dF", l, "q", g) for g in range(3)]

        def turned_keys(t):
            if t < TT + CT:
                add("v" if t < TT else "a", "dP", l, "k", t)
            if t:
                add("a", "dX", l, "k", t - 1)

        if both:
            for h in range(NH + 2):
                if h < NH:
                    add("a", "cS", l, h)
                if h == 0:
                    add("v", "nPV", l, NH - 1)
                if 0 <= h - 1 < NH:
                    add("", "cW", l, h - 1)
                if h < 6:
                    add(*parts[h])
                if 0 <= h - 1 < NH:
                    add("a", "cT", l, h - 1)
                if h >= 2:
                    add("v", "cPV", l, h - 2)
        else:
            add("v", "nPV", l, NH - 1)
            for step in parts[:6]:
                add(*step)
        for t in range(TT + CT):
            add("av"[t % 2], "dv", l, t)
        for g in range(3):
            add(*parts[6 + g])
            for t in range(2 * g, 2 * g + 2 + (g == 2)):
                turned_keys(t)
        queries = TT + CT * both
        add("v", "dP", l, "q", 0)
        add("a", "dX", l, "q", 0)
        items = diff_items(l)
        for n in range(len(items) + 3):
            if n < len(items):
                t, h = items[n]
                if h == 1 and t + 1 < queries:
                    add("v" if t + 1 < TT else "a", "dP", l, "q", t + 1)
                if h == 3 and t + 1 < queries:
                    add("a", "dX", l, "q", t + 1)
                add("aaaa" if t < TT else "aa", "dS", l, t, h)
            if 2 <= n < len(items) + 2:
                t, h = items[n - 2]
                add("aa" if t < TT else "a", "dT", l, t, h)
            if n >= 3:
                add("a", "dPV", l, *items[n - 3])
            for st in range(1 + both):
                at_ = 8 + 12 * st
                if n == at_:
                    add("v" * (2 if st == 0 else 1), "cvT", l, st)
                if n == at_ + 3:
                    add("aa", "cvZ", l, st)
            if both and n == TT * DH + 5:
                add("vvv", "doT", l, 0)
        add("", "last", l)
        add("", "wide", "yo", l, 0)
        early, late = (0, 1, 2, 6, 7), (3, 4, 5)
        add("", "outs", "yo", l, int(both), early)
        add("vvv", "doT", l, int(both))
        add("", "outs", "yo", l, int(both), late)
        add("", "wide", "yo", l, 1)
        if both:
            add("", "outs", "yo", l, 0, early + late)
        for t in (TT, TT + 1, 0, 1, 2, 3) if both else range(TT):
            add("vv", "yo", l, t)
            if both and t == 0:
                add("vvvv", "hcT", 1)
    out, n, split = [], 0, 0
    count = lambda part: sum(split_jobs(key) for key, _ in part)
    wide = [i for i, (key, _) in enumerate(s) if key in (("wout", "A"), ("wout", "B")) or key == ("yo", 0, TT - 1)]
    bounds = [count(s[:i]) for i in wide] + [count(s)]
    for key, readers in s:
        if key == ("Aw", 1):
            out.append((("split", 0), ""))
            split = 1
        if split_jobs(key) or key in (("hT", "B"), ("hT", "C0"), ("hcT", 1)) or (key[0] == "BS" and key[1] + 1 < BH):
            while split < min(n + UNITS - (key[0] in ("Bproj", "BS") or key == ("hcT", 1)), min(b for b in bounds if b > n)):
                out.append((("split", split), ""))
                split += 1
            n += split_jobs(key)
        out.append((key, readers))
        if key[0] == "Bproj" and key[1] > 0 and key[1:] != (BH - 1, BG - 1):
            while split < min(n + UNITS - 1, min(b for b in bounds if b > n)):
                out.append((("split", split), ""))
                split += 1
    return out


def split_jobs(key):
    if key[0] in ("nq", "nvF", "Bproj") or key == ("nk", 0) or key == ("nkc", 1):
        return 3
    return {"gate": 1, "dF": 1, "cv": 2, "qm": 2, "Aproj": 2}.get(key[0], 0)


def split_banks(key, n):
    if key[0] == "cv":
        return [(0, 0), (1, 0), (0, 1), (1, 1)][:n]
    groups = split_jobs(key)
    if key[0] == "nk":
        return [(g, 0) for g in range(n)]
    if key[0] == "nkc":
        return [(g, 1) for g in range(n)]
    if key[0] in ("nq", "nvF", "gate", "dF") and n == 2 * groups:
        return [(g, c) for g in range(groups) for c in range(2)]
    return [(g, 0) for g in range(groups)]


def diff_items(l):
    return [(t, h) for t in range(TT + (CT if l == 0 else 0)) for h in range(DH)]


def hybrid_stack_kernel(nc, ins, consts, out):
    steps = schedule()
    base, readers, order_of = {}, [], {}
    for n, (key, who) in enumerate(steps):
        base[key] = len(readers)
        order_of[key] = n
        readers += list(who)
    ordinal, seen = [], {"a": 0, "v": 0}
    for who in readers:
        seen[who] += 1
        ordinal.append(seen[who])
    njobs = {key: len(who) for key, who in steps}

    mem_scale = MD ** -0.5
    dil_scale = BD ** -0.5
    diff_scale = DD ** -0.5
    lam_init = [0.8 - 0.6 * math.exp(-0.3 * l) for l in range(2)]

    with ExitStack() as ctx:
        def sb(name, shape, dt=F32):
            return ctx.enter_context(nc.sbuf_tensor(name, shape, dt))

        def sem(name):
            return ctx.enter_context(nc.semaphore(name))

        def dram(name, shape):
            return nc.dram_tensor(name, shape, F32, kind="Internal").ap()

        arena_cols = 29696
        with (nc.sbuf_tensor("arena", [P, arena_cols], F32) as arena, nc.sbuf_tensor("hT", [P, KT, T], F32) as hT,
              nc.sbuf_tensor("wring", [P, WSLOTS, KT * WCOLS], F32) as wring,
              nc.sbuf_tensor("branch", [P, KT, T], F32) as branch):
            pass
        arena_r = sb("arena_r", [P, arena_cols], F32R)
        hT_r = sb("hT_r", [P, KT, T], F32R)
        wring_r = sb("wring_r", [P, WSLOTS, KT * WCOLS], F32R)
        branch_r = sb("branch_r", [P, KT, T], F32R)

        def at(off, *dims, parts=P):
            n = math.prod(dims)
            v = arena[0:parts, off:off + n]
            if len(dims) == 1:
                return v
            names = "abcde"[:len(dims)]
            sizes = {c: d for c, d in zip(names[1:], dims[1:])}
            return v.rearrange(f"p ({' '.join(names)}) -> p {' '.join(names)}", **sizes)

        ident = sb("ident", [P, P])
        vec = sb("vec", [P, V_ROWS + 2 * CW_ROWS])
        modv = sb("modv", [P, 2, 2, KT, 2])
        dil_mask = sb("dil_mask", [P, 3 * P])
        na_mask = sb("na_mask", [P, 3, GRID_H * STRIP])
        diff_rope = sb("diff_rope", [P, 2, TT, DD])
        siluc = sb("siluc", [P, KT, 2])
        subw = sb("subw", [P, 2, 3])
        lam = sb("lam", [P, 2])
        stat = sb("stat", [P, 600])
        cols = [0]

        def stats(*dims):
            n = math.prod(dims)
            v = stat[:, cols[0]:cols[0] + n]
            cols[0] += n
            if len(dims) == 1:
                return v
            names = "abcde"[:len(dims)]
            sizes = {c: d for c, d in zip(names[1:], dims[1:])}
            return v.rearrange(f"p ({' '.join(names)}) -> p {' '.join(names)}", **sizes)

        minus_half = stats(4)
        pick = stats(2, 2)
        gatev = stats(2, KT)
        conv_w = vec[:, V_ROWS:].rearrange("p (f r) -> p f r", f=CF)

        hT_hi = hT_r[:, :, :]
        hT_lo = arena_r[:, 0:KT * T].rearrange("p (k t) -> p k t", k=KT)
        x = at(0, TT, D)
        memk = at(4096, 2, 2, NMEM)
        memv = at(5120, 2, CT, MH * MD)
        xn = at(6144, TT, D)
        modrow = at(10240, 3 * D, parts=2)
        modacc = at(13312, 2, MODC)
        vrows = at(14336, P, parts=V_EARLY)
        vrows2 = at(27552, P, parts=V_ROWS - V_EARLY)
        crows = at(27680, CW, parts=CW_ROWS)
        memraw = at(14720, CT, D)
        memn = at(18816, CT, D)
        memT = at(16768, KT, NMEM)
        glow = at(18816, T, parts=GRANK)
        gv = at(19328, TT, GH * GV)
        wgu = at(22400, GH * GK, parts=GRANK)
        bgate = at(22784, 16, parts=GK)
        gmask = at(22800, P).bitcast(I32)
        greset = at(22928, T, parts=GK)
        gq = at(23440, GH, T, parts=GK)
        gk = at(25488, GH, T, parts=GK)
        gt = at(6144, 2, 4, T, parts=GK)
        gkin = at(10240, 2, T, parts=GK)
        gkout = at(11264, 2, T, parts=GK)
        gkot = at(12288, 2, TT, GK)
        gA = at(13056, 2, TT, P)
        gS = at(14080, T // GCHUNK, GV, parts=GK)
        go = at(15616, TT, GH * GV)
        gdec = sb("gdec", [GK, GH, T // GCHUNK])
        mprob = at(6144, 8, 2, NMEM)
        mprobT = at(10240, MH, CT, T)
        qmem = {"A": at(14336, 2, T), "B": at(25088, 2, T)}
        bqk = at(14336, 2, BG, 2, T)
        bvT = at(20480, 2, BG, T)
        bv = at(23552, BG, TT, BD)
        bswap = at(25088, 2, T, parts=32)
        bo12 = at(26112, T)
        bsum = at(26624, T)
        dil_rope = at(27136, 4, T, parts=32)
        bprob = at(6144, 2048)
        bprobT = at(8192, 15, P)
        hcT_hi = arena_r[:, 4096:6144].rearrange("p (k t) -> p k t", k=KT)
        hcT_lo = arena_r[:, 8192:10240].rearrange("p (k t) -> p k t", k=KT)
        hT_lo2 = arena_r[:, 20480:24576].rearrange("p (k t) -> p k t", k=KT)
        fullx = at(25856, 2, T)
        cbranch = at(6144, KT, NMEM)
        xc = at(8192, CT, D)
        cxn = at(10240, TT, D)
        cxcn = at(14336, CT, D)
        fw = at(16384, D)
        nkT = at(10240, 3, T)
        nqT = at(11776, 3, T)
        nqcT = at(13312, 3, NMEM)
        nkcT = at(14336, 3, NMEM)
        vstrip = at(15104, NQB, 2, NH * ND)
        vctx = at(18176, CT, NH * ND)
        bias = at(18944, 2, 3, GRID_H * STRIP)
        dkT = at(13312, DH, T + NMEM)
        dv = at(16384, TT + CT, DH * DV)
        dstage = at(25856, 2, 2 * DH, DPAD)
        dswap = dil_mask[:, :].rearrange("p (h d) -> p h d", d=DD)
        csig = at(25856, 2, T)
        u = at(27008, CF, T + 2 * HALO)
        uc = at(28092, CF, NMEM + 2 * HALO)
        y = at(28664, CF, T)
        yc = at(4096, CF, NMEM)
        nprob = at(0, NQB, BANK)
        nprobT = at(2048, NQB, 4, P)
        vnat = at(2304, TT, NH * ND)
        nvF = [at(0, 3, T), at(1536, 3, NMEM)]
        dF = {"v": [at(0, 3, T), at(3072, 3, NMEM)], "k": [at(1536, 3, T), at(18944, 3, NMEM)]}
        dF["q"] = dF["v"]
        cprob = at(15104, 2, CT, NMEM)
        cprobT = at(16128, 2, CT, NMEM)
        dqT = [at(10240, DH, T), at(12288, DH, NMEM)]
        hflat = hT[:, :, :].rearrange("p k t -> p (k t)")
        dprob = [hflat[:, i * 1536:(i + 1) * 1536].rearrange("p (s k) -> p s k", s=2) for i in range(2)]
        dprob.append(at(18688, 2, T + NMEM))
        dwT = at(20480, 2, TT + CT, P)
        otok = [at(23552, TT, DH * DV), at(25088, CT, DH * DV)]
        czn = [at(22016, TT, CW), at(23040, CT, CW)]
        csilu = [hflat[:, 3072:4096].rearrange("p (f t) -> p f t", f=CF), at(28664, CF, NMEM)]
        gmul = at(16384, 2, D)
        ytmp = at(25856, D)
        out_parts = [(hT_hi, branch_r[:, :, :]),
                     tuple(arena_r[:, i:i + KT * NMEM].rearrange("p (k t) -> p k t", k=KT) for i in (4096, 6144))]
        out_rows = [branch, cbranch]
        wide_room = {("wout", "A"): [18688 + 1024 * i for i in range(8)],
                     ("wout", "B"): [17408 + 1024 * i for i in range(6)] + [27136, 28160]}
        for l in range(2):
            wide_room["yo", l] = [18432 + 1024 * i for i in range(7)] + [28664]

        gate_dram = dram("gate_dram", [2, 2, D])
        x0_dram = dram("x0_dram", [T, D])
        st0_dram = dram("st0_dram", [BH, 2, T])
        st12_dram = dram("st12_dram", [BH, 4, T])
        x_dram = dram("x_dram", [2, T, D])
        nv_dram = dram("nv_dram", [2, T, NH * ND])
        rpb_dram = [dram(f"rpb_dram{l}", [RPB_PAD + RPB + 2 * RPB_PAD]) for l in range(2)]
        ebias_dram = [dram(f"ebias_dram{l}", [3, NH, 16, 15 * STRIP]) for l in range(2)]

        banks = [ctx.enter_context(nc.psum_tensor(f"bank{i}", [P, BANK], F32)) for i in range(BANKS)]

        psum_full = sem("psum_full")
        evac = {"a": sem("evac_scalar"), "v": sem("evac_vector")}
        w_full = [sem(f"w_full{i}") for i in range(WSLOTS)]
        vecs_in, vecs2_in, gla_in, const_in, mem_in, x_in = (sem(n) for n in (
            "vecs_in", "vecs2_in", "gla_in", "const_in", "mem_in", "x_in"))
        dve_chain, act_chain, pool_chain = sem("dve_chain"), sem("act_chain"), sem("pool_chain")
        silu_c, sq_done, rstd_ready, xn_ready = (sem(n) for n in ("silu_c", "sq_done", "rstd_ready", "xn_ready"))
        av_rounded, av_rest0, av_rest1 = sem("av_rounded"), sem("av_rest0"), sem("av_rest1")
        wide_hi, wide_lo_even, wide_lo_odd, out_hi, out_lo = (sem(n) for n in (
            "wide_hi", "wide_lo_even", "wide_lo_odd", "out_hi", "out_lo"))
        split_hi, split_lo, hi_ready, x0_saved, x0_back, xc_back = (sem(n) for n in (
            "split_hi", "split_lo", "hi_ready", "x0_saved", "x0_back", "xc_back"))
        bmod_in, mod_sums, gate_row, gate_saved = (sem(n) for n in ("bmod_in", "mod_sums", "gate_row", "gate_saved"))
        gla_abs, gla_soft, gla_cum, gla_exps, gla_qin, gla_keys, gla_sq, gla_rstd, gla_zero = (sem(n) for n in (
            "gla_abs", "gla_soft", "gla_cum", "gla_exps", "gla_qin", "gla_keys", "gla_sq", "gla_rstd", "gla_zero"))
        mem_negmax, mem_probs = sem("mem_negmax"), sem("mem_probs")
        rope_in, rope_done, dil_negmax, dil_probs, st_saved, st_in, dil_diff, dil_exp, dil_weighted, dil_out = (
            sem(n) for n in ("rope_in", "rope_done", "dil_negmax", "dil_probs", "st_saved", "st_in", "dil_diff",
                             "dil_exp", "dil_weighted", "dil_out"))
        fw_in, xc_in, x_final, x_saved, x_back, pads_zero, lam_in, lam_dots, lam_exps, lam_ready = (sem(n) for n in (
            "fw_in", "xc_in", "x_final", "x_saved", "x_back", "pads_zero", "lam_in", "lam_dots", "lam_exps",
            "lam_ready"))
        rpb_saved, ebias_saved, bias_ready = (sem(n) for n in ("rpb_saved", "ebias_saved", "bias_ready"))
        bias_in = [sem("bias_in_even"), sem("bias_in_odd")]
        nv_saved, strips_in, na_negmax, na_probs, ctx_negmax, ctx_probs = (sem(n) for n in (
            "nv_saved", "strips_in", "na_negmax", "na_probs", "ctx_negmax", "ctx_probs"))
        diff_staged, diff_negmax, diff_w, o_sq, o_rstd, o_normed = (sem(n) for n in (
            "diff_staged", "diff_negmax", "diff_w", "o_sq", "o_rstd", "o_normed"))
        conv_done, ln_var, ln_rstd, ln_done = (sem(n) for n in ("conv_done", "ln_var", "ln_rstd", "ln_done"))
        gmul_in, y_sq, y_rstd, x_new, out_saved = (sem(n) for n in ("gmul_in", "y_sq", "y_rstd", "x_new", "out_saved"))

        def bank(key, i):
            return banks[(base[key] + i) % BANKS]

        def claim(pe, key, i):
            n = base[key] + i
            if n >= BANKS:
                pe.wait_ge(evac[readers[n - BANKS]], ordinal[n - BANKS])
            return bank(key, i)

        def full(eng, key, i):
            eng.wait_ge(psum_full, base[key] + i + 1)
            return bank(key, i)

        def read_by_pe(eng, key):
            eng.wait_ge(psum_full, base[key] + njobs[key])

        def evacuated(eng, key, i=-1):
            n = base[key] + i % njobs[key]
            eng.wait_ge(evac[readers[n]], ordinal[n])

        def cols_of(w, c0, n):
            return w.rearrange("(k p) c -> p k c", p=P)[:, :, c0:c0 + n]

        wa, wb, wout, wmem = ins["w_in_a"][0], ins["w_in_b"][0], ins["w_out"], ins["w_memkv"]
        chunks = [(("memkv", l), cols_of(wmem[l], 0, 512), 512, ("memkv", l)) for l in range(2)]
        chunks += [
            (("Av", 0), cols_of(wa, A_V, 384), 384, ("Av",)),
            (("Av", 1), cols_of(wa, A_V + 384, 384 + GRANK), 384 + GRANK, ("Aglow",)),
            (("Aq",), cols_of(wa, A_Q, 384), 384, ("Aproj", 3)),
            (("Ak",), cols_of(wa, A_K, 384), 384, ("Aproj", 3)),
            (("gate", "A", 0), cols_of(wa, A_GATE, 384), 384, ("gate", "A", 2)),
            (("gate", "A", 1), cols_of(wa, A_GATE + 384, 384), 384, ("gate", "A", 5)),
            (("qm", "A"), cols_of(wa, A_M, 256), 256, ("qm", "A")),
            (("gate", "A", 2), cols_of(wa, A_GATE + 768, 256), 256, ("gate", "A", 7)),
        ]
        chunks += [(("wout", "A", n), cols_of(wout[0], n * 512, 512), 512, ("wout", "A")) for n in range(2)]
        rest = BG * 3 * BH * BD
        for n, c in ((0, 384), (1, 384), (2, 256)):
            chunks.append((("gate", "B", n), cols_of(wb, rest + 256 + n * WNARROW, c), c, ("gate", "B", min(3 * n + 2, 7))))
        chunks += [(("qm", "B"), cols_of(wb, rest, 256), 256, ("qm", "B"))]
        mods = [[(("mod", l, j), cols_of(ins["w_mod_2"][l], j * MODC, MODC), MODC, ("mod", l, j) if l else ("modv", j))
                 for j in range(MODS)] for l in range(2)]
        for h in range(BH):
            for g in range(BG):
                src = wb[:, g * 2304:(g + 1) * 2304].rearrange("(k p) (s c) -> p k s c", p=P, s=3)
                chunks.append((("Bproj", h, g), src[:, :, :, h * BD:(h + 1) * BD], 384, ("Bproj", h, g)))
                if h and g and 2 * (h - 1) + g - 1 < MODS:
                    chunks.append(mods[0][2 * (h - 1) + g - 1])
        chunks += mods[1]
        chunks += [(("wout", "B", n), cols_of(wout[1], n * 512, 512), 512, ("wout", "B")) for n in range(2)]
        for l in range(2):
            w2, wo2 = ins["w_in_2"][l], ins["w_out_2"][l]
            for name, c0, n, last in (
                    ("nk", C_NK, 384, ("nk", 1) if l else ("nkc", 0)), ("nq", C_NQ, 384, ("nq", l)), ("nv", C_NV, 384, ("nvF", l)),
                    ("g0", C_NG, 384, ("gate", f"C{l}", 2)), ("g1", C_DG, 384, ("gate", f"C{l}", 5)),
                    ("cb", C_CB, 256, ("cv", l, 1)), ("ca", C_CA, 256, ("cv", l, 1)),
                    ("g2", C_CG, 256, ("gate", f"C{l}", 7)), ("dv", C_DV, 384, ("dF", l, "v", 2)),
                    ("dk", C_DK, 384, ("dF", l, "k", 2)), ("dq", C_DQ, 384, ("dF", l, "q", 2))):
                chunks.append(((name, l), cols_of(w2, c0, n), n, last))
            chunks += [(("yo", l, n), cols_of(wo2, n * 512, 512), 512, ("yo", l, TT - 1))
                       for n in range(2)]
        chunk_at = {name: n for n, (name, *_) in enumerate(chunks)}

        def chunk(pe, name):
            n = chunk_at[name]
            pe.wait_ge(w_full[n % WSLOTS], loaded(n))
            return slot(n)

        def loads(n):
            return 3 if chunks[n][0][0] == "Bproj" else 1

        def slot(n):
            c = chunks[n][2]
            return wring[:, n % WSLOTS, 0:KT * c].rearrange("p (k c) -> p k c", c=c)

        def loaded(n):
            return 16 * sum(loads(m) for m in range(n % WSLOTS, n + 1, WSLOTS))

        def slot4(n):
            return wring[:, n % WSLOTS, 0:KT * 384].rearrange("p (k s c) -> p k s c", s=3, c=BD)

        def gate_chunk(ph, i):
            if ph in "AB":
                return ("gate", ph, i // 3), (i % 3) * P
            return (f"g{i // 3}", int(ph[1])), (i % 3) * P

        split_list = [(key, g) for key, _ in steps for g in range(split_jobs(key))]
        split_at = {job: n for n, job in enumerate(split_list)}
        before_mem = split_at[("Bproj", 1, 0), 0]
        split_starts = [("wout", "A"), ("wout", "B"), ("yo", 0, TT - 1)]
        split_bounds = [sum(split_jobs(key) for key, _ in steps[:order_of[start]]) for start in split_starts]

        def split_place(n):
            m = n - split_bounds[2]
            if n < split_bounds[0]:
                return (n + 1) % UNITS
            if m < 0:
                return n % UNITS
            wide = [chunk_at["yo", 0, i] % WSLOTS for i in range(2)]
            third = sum(range(WSLOTS)) - sum(wide)
            if m < UNITS:
                return (third, WSLOTS, WSLOTS + 1, wide[0])[m]
            return (third, WSLOTS, wide[1], wide[0])[m % UNITS]

        av_hi = [arena_r[:, off:off + n * c].rearrange("p (k c) -> p k c", c=c)
                 for off, n, c in ((23440, KT, 384), (10240, KT - 1, 384 + GRANK), (26512, 1, 384 + GRANK))]

        def av_parts(i):
            at_ = chunk_at["Av", min(i, 1)]
            c, k = chunks[at_][2], ((0, KT), (0, KT - 1), (KT - 1, KT))[i]
            rest = wring_r[:, at_ % WSLOTS, 0:KT * c].rearrange("p (k c) -> p k c", c=c)
            return at_, slot(at_)[:, k[0]:k[1]], av_hi[i], rest[:, k[0]:k[1]]

        def av_pair(half, k):
            i = 0 if half == 0 else 1 + k // (KT - 1)
            j = k - (KT - 1) * (i == 2)
            _, _, hi, rest = av_parts(i)
            return hi[:, j], rest[:, j]

        wide_keys = [key[1:] for key, _ in steps if key[0] == "wide"]
        out_list = [(*key[1:4], k) for key, _ in steps if key[0] == "outs" for k in key[4]]

        def wide_parts(name, l, n, q):
            at_ = chunk_at[name, l, n]
            room = wide_room[name, l][4 * n + q]
            part = lambda ring: ring[:, at_ % WSLOTS, 2 * q * WCOLS:(2 * q + 2) * WCOLS]
            return at_, part(wring), arena_r[:, room:room + 2 * WCOLS], part(wring_r)

        def wide_hi_count(name, l, n, q):
            return 4 * wide_keys.index((name, l, n)) + q + 1

        def wide_lo_count(name, l, n, q):
            return 2 * wide_keys.index((name, l, n)) + q // 2 + 1

        def out_count(name, l, st, k):
            return out_list.index((name, l, st, k)) + 1

        def last_use(n):
            key, g = split_list[n]
            if key == ("nk", 0) or key == ("nkc", 1):
                key = ("nkc", 0) if key[1] == 0 else ("nk", 1)
            last = max(i for i, (group, _) in enumerate(split_banks(key, njobs[key])) if group == g)
            return base[key] + last + 1

        def split_weights(n):
            key, g = split_list[n]
            kind, l = key[:2]
            if kind == "gate":
                name, c0 = gate_chunk(l, key[2])
            elif kind == "cv":
                name, c0 = ("cb" if g == 0 else "ca", l), key[2] * P
            elif kind == "dF":
                name, c0 = ("d" + key[2], l), key[3] * P
            elif kind == "Aproj":
                name, c0 = (("Aq", "Ak")[g],), l * GK
            else:
                name, c0 = ({"nvF": "nv", "nkc": "nk"}.get(kind, kind), *key[1:]), g * P
            at_, u = chunk_at[name], split_place(n)
            m = GK if kind == "Aproj" else P
            if u < WSLOTS:
                hi = wring_r[:, u, KT * WNARROW:KT * (WNARROW + m)]
            else:
                lo = (28672 if n < split_bounds[0] else 26112 if n < before_mem else 4096 if n < split_bounds[1] else 24576 if n < split_bounds[2] else
                      6144 + KT * P * (u - WSLOTS))
                hi = arena_r[:, lo:lo + KT * m]
            width = chunks[at_][2]
            rest = wring_r[:, at_ % WSLOTS, 0:KT * width].rearrange("p (k c) -> p k c", c=width)[:, :, c0:c0 + m]
            return at_, slot(at_)[:, :, c0:c0 + m], hi.rearrange("p (k c) -> p k c", c=m), rest

        def split_place_free(eng, n):
            if n < UNITS:
                read_by_pe(eng, ("memkv", 1) if n == 0 else ("Aglow",))
                return
            for start, bound in zip(split_starts, split_bounds):
                if bound <= n < bound + UNITS:
                    if start[0] == "yo" and n < bound + 3:
                        start = ("yo", 0, TT + CT - 1)
                    read_by_pe(eng, start)
                    return
            eng.wait_ge(psum_full, last_use(n - UNITS))
            if before_mem <= n < before_mem + UNITS:
                read_by_pe(eng, ("mPV", "B"))

        hi_keys = [key for key, _ in steps if key[0] in ("hT", "hcT")]

        def hi_at(key, k):
            return KT * hi_keys.index(key) + k + 1

        norms = {}
        for ph, src, dst, nt in (("m", memraw, memn, CT), ("A", x, xn, TT), ("B", x, xn, TT), ("c0", xc, cxcn, CT),
                                 ("F", x, cxn, TT), ("C0", x, cxn, TT), ("c1", xc, cxcn, CT), ("C1", x, cxn, TT)):
            norms[ph] = (src, dst, nt, stats(nt), stats(nt))

        gla_ss, gla_rs = stats(GH, TT), stats(GH, TT)
        m_max, m_neg, m_sum, m_rec = (stats(2, 8, 2) for _ in range(4))
        b_stat = stats(2, BG, 2, 2, TT)
        b_neg = stats(2, BG, TT)
        b_top, b_w, b_rec = stats(2, TT), stats(BG, 2, TT), stats(2, TT)
        n_ctx, n_max, n_neg, n_s, n_rec = stats(NQB), stats(NQB), stats(NQB), stats(2, NQB), stats(2, NQB)
        c_max, c_neg, c_s, c_rec = (stats(2, CT) for _ in range(4))
        d_max, d_neg, d_s, d_rec = (stats(4, 4) for _ in range(4))
        o_ss, o_rs = stats(TT + CT, DH), stats(TT + CT, DH)
        ln_st, ln_mv, ln_rs = stats(6), stats(2, 2, 2), stats(2, 2)
        y_ss, y_rs = stats(2, 2), stats(2, 2)
        lam_st = stats(2, 2)
        lam_v = sb("lam_v", [P, 2, 4, DD])
        lam_junk = at(28000, DD)
        assert cols[0] <= 600, cols[0]

        norm_no, n_tiles = {}, 0
        for ph in norms:
            if ph != "C0":
                for t in range(norms[ph][2]):
                    for name in ("F", "C0") if ph == "F" else (ph,):
                        n_tiles += 1
                        norm_no[name, t] = n_tiles
        norm_pe, n_tiles = {}, 0
        for ph in norms:
            if ph != "F":
                n_tiles += norms[ph][2]
            norm_pe[ph] = n_tiles
        stages = [key for key, _ in steps if key[0] == "dP"]
        roped = [key for key in stages if key[3] < TT]

        def stage_at(key):
            return stages.index(key)

        def stage_key(n):
            return ("dX", *stages[n][1:])

        def roped_at(key):
            return roped.index(key)

        all_diff = [(l, t, h) for l in range(2) for t, h in diff_items(l)]

        def diff_at(l, t, h):
            return all_diff.index((l, t, h))

        def diff_step(kind, n):
            return (kind, *all_diff[n])

        def diff_tile(l, t):
            return l * (TT + CT) + t

        def score_part(t, i):
            half, part = divmod(i, 2) if t < TT else (i, 1)
            return (half, part, 0, T) if part == 0 else (half, part, T, NMEM)

        def yo_at(l, t):
            return t - TT if t >= TT else CT + t if l == 0 else TT + CT + t

        def ln_pair(l, st, i):
            return 3 * l + 2 * st + i

        def bprob_tile(g, n):
            if g == 0:
                return bprob[:, P:2 * P] if n == 0 else bprob[:, 2 * n * P:(2 * n + 2) * P]
            return bprob[:, (4 + 4 * g + n) * P:(5 + 4 * g + n) * P]

        def dil_tile(g, n):
            if g == 0:
                return 3 + n // 2, (n % 2) * 2 * P, P if n == 0 else 0
            return 4 + g, n * P, P * g

        def self_bias(pool, l, h):
            if (l, h) == (0, 0):
                pool.wait_ge(const_in, 48)
            pool.wait_ge(bias_in[h % 2], 16 * GRID_H * ((l * NH + h) // 2 + 1))
            v = bias[:, h % 2]
            nc.gpsimd.tensor_tensor(v, v, na_mask[:, :, :], ALU.add).then_inc(bias_ready, 1)

        PT_BANKS = ((0, 4), (4, 3), (7, 4), (11, 4))
        PT_TILES = (1, 2, 3, 4, 5, 6, 7, 8, 9, 10, 11, 12, 13, 14, 15)
        DS_BANK = {0: (0, 0), 1: (1, 0), 2: (0, 1), 3: (1, 1), 4: (3, 0), 5: (2, 0), 6: (3, 1)}
        DS_LAST = (2, 3, 5, 6)
        VECS_IN = 16 * 7
        VECS2_IN = 16 * 20

        block = ctx.enter_context(nc.Block())

        def sync_items():
            items = []
            for n in range(len(chunks)):
                name = chunks[n][0]
                free = order_of[chunks[n - WSLOTS][3]] if n >= WSLOTS else -1
                if name[:2] == ("wout", "A"):
                    free = order_of[("gate", "A", 7)]
                if name[0] == "yo":
                    free = max(free, order_of[("dF", name[1], "q", 2)])
                items.append((free, "chunk", n))
            items.append((order_of[("gate", "A", 7)], "x_again", None))
            items.append((order_of[("Bproj", BH - 1, BG - 1)], "x0_back", None))
            for h in range(BH):
                items.append((order_of[("BS", h)], "stats", h))
            for l in range(2):
                items.append((order_of[("nv", l)], "strips", l))
                for kind in range(3):
                    n = 3 * l + kind
                    items.append((order_of[("BS", n - 1) if n else ("Bproj", 0, 0)], "ebias", (l, kind)))
                for h in range(NH):
                    free = ("wout", "B") if l == 0 else ("yo", 0, TT - 1)
                    items.append((order_of[free if h < 2 else ("nS", l, h - 2)], "bias", (l, h)))
                last_q = ("dP", l, "q", (TT + CT if l == 0 else TT) - 1)
                items.append((order_of[last_q], "x_back", (l, last_q)))
                last_pv = ("dPV", l, *diff_items(l)[-1])
                items.append((order_of[last_pv], "gmul", (l, last_pv)))
            return sorted(items, key=lambda i: i[0])

        @block.sync
        def _(sp):
            def late_vectors():
                n_vec = 0

                def piece(r, c, src):
                    sp.dma_start(vrows2[r - V_EARLY:r - V_EARLY + src.shape[0], c:c + src.shape[1]], src).then_inc(vecs2_in, 16)
                    return 1

                gla_w = ins["gla_norm_w"]
                n_vec += piece(V_GLA, 0, gla_w[:, 0:128])
                n_vec += piece(V_GLA + 1, 0, gla_w[:, 128:192])
                n_vec += piece(V_GLA + 1, 64, gla_w[:, 0:64])
                n_vec += piece(V_GLA + 2, 0, gla_w[:, 64:192])
                for l in range(2):
                    sw = ins["diff_subln_g_2"][l:l + 1]
                    for r in range(3):
                        f = r * P
                        while f < (r + 1) * P:
                            e = f % DV
                            n = min(DV - e, (r + 1) * P - f)
                            n_vec += piece(V_SUB + 3 * l + r, f - r * P, sw[:, e:e + n])
                            f += n
                for r, name in ((V_CB, "conv_b_2"), (V_LG, "conv_ln_g_2"), (V_LB, "conv_ln_b_2")):
                    n_vec += piece(r, 0, ins[name].rearrange("l (r c) -> (l r) c", c=P))
                sp.dma_start(crows, ins["conv_w_2"].rearrange("l k c -> (l k) c")).then_inc(vecs2_in, 16)
                assert 16 * (n_vec + 1) == VECS2_IN, n_vec
                for q, name in enumerate(("diff_lq1_2", "diff_lk1_2", "diff_lq2_2", "diff_lk2_2")):
                    sp.dma_start(lam_v[:, :, q, :], ins[name].partition_broadcast(P)).then_inc(lam_in, 16)
                sp.dma_start(wgu, ins["w_gate_up"][0]).then_inc(gla_in, 16)
                sp.dma_start(bgate[:, 0:GH], ins["b_gate"][0].rearrange("(h p) -> p h", p=GK),
                             allow_slow_non_contiguous=True).then_inc(gla_in, 16)
                sp.dma_start(gmask, consts["gla_mask"]).then_inc(gla_in, 16)
                sp.dma_start(greset, consts["gla_reset"]).then_inc(gla_in, 16)
                sp.dma_start(dil_mask[:, :], consts["dil_mask"]).then_inc(const_in, 16)
                sp.dma_start(na_mask[:, :, :], consts["na_mask"]).then_inc(const_in, 16)
                sp.dma_start(diff_rope[:, :, :, :], consts["diff_rope"]).then_inc(const_in, 16)

            sp.dma_start(memraw, ins["mem"][0].rearrange("(t p) d -> p t d", p=P)).then_inc(mem_in, 16)
            sp.wait_ge(vecs_in, VECS_IN)
            for _, what, arg in sync_items():
                if what == "chunk":
                    name, src, c, last = chunks[arg]
                    if arg >= WSLOTS:
                        last = chunks[arg - WSLOTS][3]
                        if name[:2] == ("wout", "A"):
                            read_by_pe(sp, ("gate", "A", 7))
                        if name[0] == "yo":
                            read_by_pe(sp, ("dF", name[1], "q", 2))
                        if last[0] == "modv":
                            sp.wait_ge(mod_sums, last[1] + 1)
                        else:
                            read_by_pe(sp, last)
                    for i in range(loads(arg)):
                        dst, part = (slot(arg), src) if loads(arg) == 1 else (slot4(arg)[:, :, i], src[:, :, i])
                        sp.dma_start(dst, part).then_inc(w_full[arg % WSLOTS], 16)
                    if arg == 0:
                        sp.dma_start(x, ins["x"][0].rearrange("(t p) d -> p t d", p=P)).then_inc(x_in, 16)
                    if arg == 2:
                        late_vectors()
                elif what == "ebias":
                    l, kind = arg
                    sp.wait_ge(rpb_saved, 48 * (l + 1))
                    for qq in range(16):
                        off = RPB_PAD + BIAS_OFF[kind] + 15 - qq
                        src = bass.AP(rpb_dram[l].tensor, off, [[465, NH], [31, 15], [1, STRIP]])
                        sp.dma_start(ebias_dram[l][kind, :, qq, :].rearrange("h (r c) -> h r c", c=STRIP),
                                     src).then_inc(ebias_saved, 16)
                elif what == "bias":
                    l, h = arg
                    if h < 2:
                        read_by_pe(sp, ("wout", "B") if l == 0 else ("yo", 0, TT - 1))
                    else:
                        sp.wait_ge(na_negmax, l * NH + h - 1)
                    sp.wait_ge(ebias_saved, 16 * 48 * 2)
                    for rq in range(GRID_H):
                        src = bass.AP(ebias_dram[l].tensor, h * 16 * 480 + (7 - rq) * STRIP,
                                      [[480, 16], [NH * 16 * 480, 3], [1, GRID_H * STRIP]])
                        sp.dma_start(bias[rq * 16:rq * 16 + 16, h % 2], src).then_inc(bias_in[h % 2], 16)
                elif what == "strips":
                    l = arg
                    sp.wait_ge(nv_saved, 16 * (l + 1))
                    grid = nv_dram[l].rearrange("(k r c) d -> r c k d", k=2, c=GRID_W)
                    for n in range(NQB):
                        for r in range(4):
                            sp.dma_start(vstrip[r * STRIP:(r + 1) * STRIP, n, :, :],
                                         grid[r, STRIP_START[n]:STRIP_START[n] + STRIP]).then_inc(strips_in, 16)
                elif what == "stats":
                    h = arg
                    b = h % 2
                    sp.wait_ge(dil_probs, h + 1)
                    stat_of = lambda g, order: b_stat[:, b, g, order].rearrange("p c n -> p (c n)")
                    natural = lambda d: d.rearrange("c (b i) -> i (c b)", b=TT)
                    strided = lambda d: d.rearrange("c (i b) -> i c b", b=DIL)
                    pairs = [(st0_dram[h], 0, natural, strided)]
                    pairs += [(st12_dram[h, 2 * g - 2:2 * g], g, strided, natural) for g in (1, 2)]
                    for d, g, save, _ in pairs:
                        sp.dma_start(save(d), b_stat[:, b, g, 1] if g else stat_of(g, 0),
                                     allow_slow_non_contiguous=True).then_inc(st_saved, 16)
                    sp.wait_ge(st_saved, 48 * (h + 1))
                    for d, g, _, load in pairs:
                        sp.dma_start(stat_of(g, 0) if g else b_stat[:, b, g, 1], load(d),
                                     allow_slow_non_contiguous=True).then_inc(st_in, 16)
                elif what == "x_again":
                    read_by_pe(sp, ("gate", "A", 7))
                    sp.dma_start(x, ins["x"][0].rearrange("(t p) d -> p t d", p=P)).then_inc(x_in, 16)
                elif what == "x0_back":
                    read_by_pe(sp, ("Bproj", BH - 1, BG - 1))
                    sp.wait_ge(x0_saved, 16 * TT)
                    sp.dma_start(x, x0_dram.rearrange("(t p) d -> p t d", p=P)).then_inc(x0_back, 16)
                elif what == "x_back":
                    l, last_q = arg
                    read_by_pe(sp, last_q)
                    sp.wait_ge(x_saved, 16 * (l + 1))
                    sp.dma_start(x, x_dram[l].rearrange("(t p) d -> p t d", p=P)).then_inc(x_back, 16)
                elif what == "gmul":
                    l, last_pv = arg
                    read_by_pe(sp, last_pv)
                    if l == 0:
                        read_by_pe(sp, ("dF", 0, "q", 2))
                        sp.dma_start(xc, ins["ctx_2"][0].rearrange("(t p) d -> p t d", p=P)).then_inc(xc_back, 16)
                    sp.wait_ge(gate_saved, 32 * (l + 1))
                    for c in range(2):
                        sp.dma_start(gmul[:, c], gate_dram[l, c].partition_broadcast(P)).then_inc(gmul_in, 16)
            for t in range(TT):
                sp.wait_ge(x_new, TT + CT + t + 1)
                sp.dma_start(out[0].rearrange("(t p) d -> p t d", p=P)[:, t], x[:, t]).then_inc(out_saved, 16)
            sp.wait_ge(out_saved, 16 * TT)

        @block.gpsimd
        def _(pool):
            count = {"chain": 0}

            def chained(ins):
                count["chain"] += 1
                ins.then_inc(pool_chain, 1)
                pool.wait_ge(pool_chain, count["chain"])

            def root(rs, ss, n, done):
                chained(nc.gpsimd.tensor_scalar(rs, ss, 1.0 / n, EPS, ALU.mult, ALU.add))
                width = rs.shape[1]
                nc.gpsimd.tensor_tensor(rs, rs, minus_half[:, 0:width], ALU.pow).then_inc(done, 1)

            def norm_roots(ph, t):
                _, _, _, ss, rs = norms[ph]
                pool.wait_ge(sq_done, norm_no[ph, t])
                root(rs[:, t:t + 1], ss[:, t:t + 1], D, rstd_ready)

            chained(nc.gpsimd.memset(minus_half, -0.5))
            zeros = lam_junk[0:1, 0:2 * RPB_PAD]
            nc.gpsimd.memset(lam_junk, 0.0).then_inc(pads_zero, 1)
            nc.gpsimd.wait_ge(pads_zero, 1)
            for l in range(2):
                pool.dma_start(rpb_dram[l][0:RPB_PAD].rearrange("(a n) -> a n", a=1),
                               zeros[:, 0:RPB_PAD]).then_inc(rpb_saved, 16)
                pool.dma_start(rpb_dram[l][RPB_PAD + RPB:].rearrange("(a n) -> a n", a=1), zeros).then_inc(rpb_saved, 16)
                pool.dma_start(rpb_dram[l][RPB_PAD:RPB_PAD + RPB],
                               ins["na_rpb_2"][l].rearrange("h r c -> (h r c)")).then_inc(rpb_saved, 16)

            def load_mod(l):
                pool.dma_start(modrow, ins["b_mod_2"][l].partition_broadcast(2)).then_inc(bmod_in, 16)

            for j in range(2):
                nc.gpsimd.memset(pick[:, j, j:j + 1], 1.0).then_inc(gla_zero, 1)
                nc.gpsimd.memset(pick[:, j, 1 - j:2 - j], 0.0).then_inc(gla_zero, 1)
            nc.gpsimd.memset(gA, 0.0).then_inc(gla_zero, 1)
            nc.gpsimd.memset(gS[:, 0], 0.0).then_inc(gla_zero, 1)
            for ph in "mA":
                for t in range(norms[ph][2]):
                    norm_roots(ph, t)

            for key, _ in steps:
                kind = key[0]
                if kind == "modT":
                    l = key[1]
                    pool.wait_ge(gate_row, l + 1)
                    for c in range(2):
                        pool.dma_start(gate_dram[l, c].rearrange("(k p) -> p k", p=P), gatev[:, c],
                                       allow_slow_non_contiguous=True).then_inc(gate_saved, 16)
                    if l == 0:
                        pool.wait_ge(gate_saved, 32)
                        load_mod(1)
                elif kind == "Aproj":
                    h = key[1]
                    b = h % 2
                    evacuated(pool, key, 1)
                    pool.wait_ge(gla_exps, 3 * h + 3)
                    if h >= 2:
                        read_by_pe(pool, ("AA", h - 2))
                    nc.gpsimd.tensor_tensor(gkin[:, b], gk[:, h], gt[:, b, 1], ALU.mult).then_inc(gla_keys, 1)
                    nc.gpsimd.tensor_tensor(gkout[:, b], gk[:, h], gt[:, b, 3], ALU.mult).then_inc(gla_keys, 1)
                elif kind == "split":
                    _, w, hi, rest = split_weights(key[1])
                    pool.wait_ge(split_hi, key[1] + 1)
                    nc.gpsimd.tensor_tensor(rest, w, hi.bitcast(F32), ALU.subtract).then_inc(split_lo, 1)
                elif key == ("Aw", 0):
                    _, w, hi, rest = av_parts(0)
                    pool.wait_ge(av_rounded, 1)
                    nc.gpsimd.tensor_tensor(rest, w, hi.bitcast(F32), ALU.subtract).then_inc(av_rest0, 1)
                elif kind == "wide":
                    for q in (0, 2):
                        _, w, hi, rest = wide_parts(*key[1:], q)
                        pool.wait_ge(wide_hi, wide_hi_count(*key[1:], q))
                        nc.gpsimd.tensor_tensor(rest, w, hi.bitcast(F32), ALU.subtract).then_inc(wide_lo_even, 1)
                elif key == ("mPV", "B"):
                    read_by_pe(pool, key)
                    load_mod(0)
                elif kind == "Ao":
                    h = key[1]
                    for i in range(2):
                        pool.wait_ge(gla_sq, 2 * h + i + 1)
                        root(gla_rs[:, h, 2 * i:2 * i + 2], gla_ss[:, h, 2 * i:2 * i + 2], GV, gla_rstd)
                elif kind == "wout":
                    ph = key[1]
                    if ph == "A":
                        read_by_pe(pool, ("mPV", "A"))
                        for t in range(TT):
                            evacuated(pool, key, 2 * t + 1)
                            pool.dma_start(x0_dram[t * P:(t + 1) * P], x[:, t]).then_inc(x0_saved, 16)
                        pool.dma_start(dil_rope, consts["dil_rope"]).then_inc(rope_in, 16)
                        for t in range(TT):
                            norm_roots("B", t)
                    else:
                        read_by_pe(pool, ("BPV", BH - 1))
                        pool.dma_start(xc, ins["ctx_2"][0].rearrange("(t p) d -> p t d", p=P)).then_inc(xc_in, 16)
                        pool.dma_start(fw, ins["final_norm_w"].partition_broadcast(P)).then_inc(fw_in, 16)
                        for t in range(CT):
                            norm_roots("c0", t)
                        for t in range(TT):
                            norm_roots("F", t)
                            norm_roots("C0", t)
                        pool.wait_ge(x_final, TT)
                        pool.dma_start(x_dram[0].rearrange("(t p) d -> p t d", p=P), x).then_inc(x_saved, 16)
                elif kind == "nv":
                    l = key[1]
                    evacuated(pool, key, 3)
                    evacuated(pool, key, 5)
                    pool.dma_start(nv_dram[l].rearrange("(t p) c -> p t c", p=P), vnat).then_inc(nv_saved, 16)
                elif kind == "nvF":
                    self_bias(pool, key[1], 0)
                elif kind == "nS" and key[2] + 1 < NH:
                    self_bias(pool, key[1], key[2] + 1)
                elif kind == "dPV":
                    l, t, h = key[1:]
                    if h == DH - 1:
                        n = diff_tile(l, t)
                        pool.wait_ge(o_sq, n + 1)
                        root(o_rs[:, t, :], o_ss[:, t, :], DV, o_rstd)
                elif kind == "cvT":
                    l, st = key[1:]
                    for i in range((TT, CT)[st] // 2):
                        n = ln_pair(l, st, i)
                        pool.wait_ge(ln_var, n + 1)
                        rs = ln_rs[:, i]
                        chained(nc.gpsimd.tensor_scalar(rs, ln_mv[:, i, :, 1], 1.0, EPS, ALU.mult, ALU.add))
                        nc.gpsimd.tensor_tensor(rs, rs, minus_half[:, 0:2], ALU.pow).then_inc(ln_rstd, 1)
                elif kind == "yo":
                    l, t = key[1:]
                    n = yo_at(l, t)
                    b = n % 2
                    pool.wait_ge(y_sq, 2 * n + 2)
                    if n >= 2:
                        pool.wait_ge(x_new, n - 1)
                    chained(nc.gpsimd.tensor_tensor(y_rs[:, b, 0:1], y_ss[:, b, 0:1], y_ss[:, b, 1:2], ALU.add))
                    root(y_rs[:, b, 1:2], y_rs[:, b, 0:1], D, y_rstd)
                    if l == 0:
                        norm_roots("C1" if t < TT else "c1", t % TT)
                    if l == 0 and t == TT - 1:
                        pool.wait_ge(x_new, TT + CT)
                        pool.dma_start(x_dram[1].rearrange("(t p) d -> p t d", p=P), x).then_inc(x_saved, 16)

        @block.scalar
        def _(act):
            count = {"chain": 0}

            def chained(ins):
                count["chain"] += 1
                ins.then_inc(act_chain, 1)
                act.wait_ge(act_chain, count["chain"])

            def free(ins):
                ins.then_inc(evac["a"], 1)

            def move(out, in_, scale=1.0):
                return nc.scalar.activation(out, in_, ACT.Copy, scale=scale)

            def square(ph, t):
                src, dst, _, ss, _ = norms[ph]
                nc.scalar.activation(dst[:, t], src[:, t], ACT.Square, accum_out=ss[:, t:t + 1]).then_inc(sq_done, 1)

            def rows(r, src, n):
                act.dma_start(vrows[r:r + n, :], src).then_inc(vecs_in, 16)

            act.dma_start(ident[:, :], consts["ident"]).then_inc(vecs_in, 16)
            rows(V_C, ins["c_2"][0].rearrange("(r c) -> r c", c=P), KT)
            rows(V_C + KT, ins["c_ctx_2"].rearrange("(r c) -> r c", c=P), KT)
            rows(V_MEM, ins["mem_norm_w"].rearrange("(r c) -> r c", c=P), KT)
            rows(V_NORM, ins["norm_w"].rearrange("l (r c) -> (l r) c", c=P), 2 * KT)
            rows(V_GPRE, ins["g_pre_2"].rearrange("l (r c) -> (l r) c", c=P), 2 * KT)
            rows(V_GPOST, ins["g_post_2"].rearrange("l (r c) -> (l r) c", c=P), 2 * KT)

            for key, _ in steps:
                kind = key[0]
                if kind == "vecT" and key[1] == 0:
                    evacuated(act, key)
                    nc.scalar.activation(siluc[:, :, :].rearrange("p k c -> p c k"),
                                         vec[:, V_C:V_C + 2 * KT].rearrange("p (c k) -> p c k", c=2),
                                         ACT.Silu).then_inc(silu_c, 1)
                    act.wait_ge(mem_in, 16)
                    for t in range(CT):
                        square("m", t)
                elif kind == "vecT":
                    act.wait_ge(lam_dots, 1)
                    nc.scalar.activation(lam_st, lam_st, ACT.Exp).then_inc(lam_exps, 1)
                elif kind == "split":
                    n = key[1]
                    at_, w, hi, _ = split_weights(n)
                    act.wait_ge(w_full[at_ % WSLOTS], loaded(at_))
                    split_place_free(act, n)
                    move(hi, w).then_inc(split_hi, 1)
                elif kind == "Aw":
                    for i in ((0,), (1, 2))[key[1]]:
                        at_, w, hi, _ = av_parts(i)
                        act.wait_ge(w_full[at_ % WSLOTS], loaded(at_))
                        move(hi, w).then_inc(av_rounded, 1)
                elif kind == "wide":
                    name, l, n = key[1:]
                    if name == "yo":
                        read_by_pe(act, ("doT", l, 1 - l) if n else ("dPV", l, *diff_items(l)[-1]))
                        if n:
                            act.wait_ge(ln_done, CF * (2 + l))
                    else:
                        read_by_pe(act, ("Ao", GH - 1) if l == "A" else ("BS", BH - 1))
                    for q in range(4):
                        at_, w, hi, _ = wide_parts(name, l, n, q)
                        if q == 0:
                            act.wait_ge(w_full[at_ % WSLOTS], loaded(at_))
                        move(hi, w).then_inc(wide_hi, 1)
                elif kind == "outs":
                    name, l, st, rows = key[1:]
                    if name == "yo":
                        read_by_pe(act, ("dT", l, *diff_items(l)[-1]))
                        act.wait_ge(ln_done, CF * (2 + l))
                        evacuated(act, ("nPV", l, NH - 1) if st == 0 else ("cPV", l, NH - 1))
                    elif l == "A":
                        read_by_pe(act, ("gate", "A", 7))
                        evacuated(act, ("mPV", "A") if 6 in rows else ("AoT",))
                    else:
                        read_by_pe(act, ("Bproj", BH - 1, BG - 1))
                        evacuated(act, ("mPV", "B"))
                        act.wait_ge(dil_out, max(k for k in rows if k < BH) + 1)
                    for k in rows:
                        if name == "yo" and 3 <= k < 6:
                            evacuated(act, ("doT", l, st), k - 3)
                        move(out_parts[st][0][:, k], out_rows[st][:, k]).then_inc(out_hi, 1)
                elif kind == "memT":
                    for i in (0, 2):
                        b = full(act, key, i)
                        move(memT[:, 2 * i], b[:, 0:NMEM], vec[:, V_MEM + 2 * i:V_MEM + 2 * i + 1])
                        free(move(memT[:, 2 * i + 1], b[:, NMEM:], vec[:, V_MEM + 2 * i + 1:V_MEM + 2 * i + 2]))
                elif kind == "memkv":
                    if key[1] == 0:
                        act.wait_ge(x_in, 16)
                        for t in range(TT):
                            square("A", t)
                    for i, dst in enumerate((memk, memv)):
                        free(move(dst[:, key[1]], full(act, key, i)[:, :].rearrange("p (a b) -> p a b", a=2)))
                elif kind == "hT" and key[1] in "AB":
                    for k in range(KT):
                        c = V_NORM + KT * (key[1] == "B") + k
                        move(hT_hi[:, k], full(act, key, k)[:, :], vec[:, c:c + 1]).then_inc(hi_ready, 1)
                elif kind in ("hT", "hcT"):
                    l, c, dst, n = (int(key[1][1]), 0, hT_hi, T) if kind == "hT" else (key[1], 1, hcT_hi, NMEM)
                    for k in range(KT):
                        b = full(act, key, k * n // T)
                        lo = (k * n) % T
                        nc.scalar.activation(dst[:, k], b[:, lo:lo + n], ACT.Identity, bias=modv[:, l, 1, k, c:c + 1],
                                             scale=modv[:, l, 0, k, c:c + 1]).then_inc(hi_ready, 1)
                elif kind == "Av":
                    for i in range(0, 8, 2):
                        half, t = divmod(i, TT)
                        free(move(gv[:, t, half * 384:half * 384 + 384], full(act, key, i)[:, 0:384]))
                elif kind == "Aglow":
                    free(move(glow, full(act, key, 0)[0:GRANK, :]))
                elif kind == "Aproj":
                    h = key[1]
                    b = h % 2
                    t1, t2, t3, t4 = (gt[:, b, i] for i in range(4))
                    free(move(gq[:, h], full(act, key, 0)[0:GK, :], GK ** -0.5))
                    z = full(act, key, 2)[0:GK, :]
                    if h == 0:
                        act.wait_ge(gla_in, 64)
                    if h >= 2:
                        act.wait_ge(gla_qin, h - 1)
                    nc.scalar.activation(t1, z, ACT.Abs, bias=bgate[:, h:h + 1]).then_inc(gla_abs, 1)
                    act.wait_ge(gla_abs, h + 1)
                    chained(nc.scalar.activation(t1, t1, ACT.Exp, scale=-1.0))
                    nc.scalar.activation(t1, t1, ACT.Ln, bias=1.0).then_inc(gla_soft, 1)
                    act.wait_ge(gla_cum, h + 1)
                    nc.scalar.activation(t1, t3, ACT.Exp, scale=1.0 / GTAU).then_inc(gla_exps, 1)
                    nc.scalar.activation(t2, t3, ACT.Exp, scale=-1.0 / GTAU).then_inc(gla_exps, 1)
                    nc.scalar.activation(t4, t4, ACT.Exp, scale=1.0 / GTAU).then_inc(gla_exps, 1)
                elif kind == "AA":
                    h = key[1]
                    if h >= 2:
                        read_by_pe(act, ("AdS", h - 2))
                    free(move(gkot[:, h % 2], full(act, key, 1)[:, 0:TT * GK].rearrange("p (t d) -> p t d", d=GK)))
                elif kind == "Ao":
                    h = key[1]
                    for i in range(2):
                        b = full(act, key, i)
                        for j in range(2):
                            t = 2 * i + j
                            ins_ = nc.scalar.activation(go[:, t, h * GV:(h + 1) * GV], b[:, j * GV:(j + 1) * GV],
                                                        ACT.Square, accum_out=gla_ss[:, h, t:t + 1])
                        ins_.then_inc(gla_sq, 1)
                        act.wait_ge(gla_rstd, 2 * h + i + 1)
                        for j in range(2):
                            t = 2 * i + j
                            ins_ = move(go[:, t, h * GV:(h + 1) * GV], b[:, j * GV:(j + 1) * GV], gla_rs[:, h, t:t + 1])
                        free(ins_)
                elif kind == "gate":
                    ph, i = key[1:]
                    free(nc.scalar.activation(branch[:, i], full(act, key, 0)[:, :], ACT.Silu))
                    if njobs[key] == 2:
                        free(nc.scalar.activation(cbranch[:, i], full(act, key, 1)[:, 0:NMEM], ACT.Silu))
                elif kind == "qm":
                    free(move(qmem[key[1]][:, 0], full(act, key, 0)[:, :]))
                elif kind == "mS":
                    ph = "AB".index(key[1])
                    for i in range(8):
                        b = bank(key, i)
                        act.wait_ge(mem_negmax, 8 * ph + i + 1)
                        for j in range(2):
                            ins_ = nc.scalar.activation(mprob[:, i, j], b[:, j * NMEM:(j + 1) * NMEM], ACT.Exp,
                                                        bias=m_neg[:, ph, i, j:j + 1], scale=mem_scale,
                                                        accum_out=m_sum[:, ph, i, j:j + 1])
                        free(ins_)
                elif kind == "mT":
                    for i in range(0, 8, 2):
                        free(move(mprobT[:, i % 2::2, :, (i // 2) * P:(i // 2 + 1) * P],
                                  full(act, key, i)[:, :].rearrange("p (h k q) -> p h k q", h=2, k=CT)))
                elif kind == "wout":
                    ph = key[1]
                    if ph == "A":
                        for t in range(TT):
                            evacuated(act, key, 2 * t + 1)
                            square("B", t)
                    else:
                        act.wait_ge(xc_in, 16)
                        act.wait_ge(gate_saved, 64)
                        read_by_pe(act, ("BPV", BH - 1))
                        for t in range(CT):
                            square("c0", t)
                        for t in range(TT):
                            evacuated(act, key, 2 * t + 1)
                            square("F", t)
                            act.wait_ge(x_final, t + 1)
                            square("C0", t)
                elif kind == "Bproj":
                    h, g = key[1:]
                    if h >= 2:
                        read_by_pe(act, ("BS", h - 2))
                    for i in range(2):
                        b, dst = full(act, key, i), bqk[:, h % 2, g, i]
                        if g == 0:
                            free(move(dst, b[:, :]))
                        else:
                            free(move(dst.rearrange("p (b i) -> p b i", b=DIL), b[:, :].rearrange("p (i b) -> p b i", b=DIL)))
                elif kind == "BS":
                    h = key[1]
                    if h:
                        read_by_pe(act, ("BPV", h - 1))
                    for g in range(BG):
                        free(move(bv[:, g], full(act, key, g)[:, :].rearrange("p (b d) -> p b d", d=BD)))
                    act.wait_ge(dil_negmax, h + 1)
                    for g in range(BG):
                        for n in range(TT):
                            v = bprob_tile(g, n)
                            ins_ = nc.scalar.activation(v, v, ACT.Exp, bias=b_neg[:, h % 2, g, n:n + 1],
                                                        accum_out=b_stat[:, h % 2, g, int(g > 0), 1, n:n + 1])
                    ins_.then_inc(dil_probs, 1)
                elif kind == "Bw":
                    h = key[1]
                    act.wait_ge(dil_diff, h + 1)
                    nc.scalar.activation(b_w, b_w, ACT.Exp).then_inc(dil_exp, 1)
                elif kind == "BT":
                    h = key[1]
                    if h:
                        read_by_pe(act, ("BPV", h - 1))
                    for i in (0, 2):
                        n0, n = PT_BANKS[i]
                        free(move(bprobT[:, n0:n0 + n], full(act, key, i)[:, 0:n * P].rearrange("p (n q) -> p n q", q=P)))
                elif kind == "BPV":
                    h = key[1]
                    if h:
                        act.wait_ge(dil_out, h)
                    free(move(bo12.rearrange("p (i b) -> p b i", b=DIL), full(act, key, 1)[:, :].rearrange("p (b i) -> p b i", b=DIL)))
                elif kind == "nk":
                    for j in range(3):
                        free(move(nkT[:, j], full(act, key, j)[:, :]))
                elif kind == "nvF":
                    act.wait_ge(x_saved, 16 * (key[1] + 1))
                    for j in range(3):
                        free(move(nvF[0][:, j], full(act, key, 2 * j)[:, :]))
                elif kind == "dF":
                    l, what, g = key[1:]
                    if what == "q":
                        read_by_pe(act, ("dv", l, TT + CT - 1))
                    free(move(dF[what][0][:, g], full(act, key, 0)[:, :]))
                elif kind == "nv":
                    for t in range(TT):
                        free(move(vnat[:, t], full(act, key, t)[:, 0:NH * ND]))
                elif kind == "nq":
                    for j in range(3):
                        free(move(nqT[:, j].rearrange("p (n r c) -> p n r c", n=NQB, r=GRID_H),
                                  full(act, key, j * njobs[key] // 3)[:, :].rearrange("p (r n c) -> p n r c", r=GRID_H, n=NQB),
                                  ND ** -0.5))
                elif kind == "cv":
                    f = key[2]
                    for st, n in ((0, T), (1, NMEM))[0:njobs[key] // 2]:
                        if st:
                            evacuated(act, key, 1)
                        free(nc.scalar.activation(csig[:, f, 0:n], full(act, key, 2 * st)[:, 0:n], ACT.Sigmoid))
                elif kind == "dP":
                    l, what, t = key[1:]
                    if t >= TT:
                        n = stage_at(key)
                        if n >= 2:
                            read_by_pe(act, stage_key(n - 2))
                        free(move(dstage[:, n % 2, :, 0:DD], full(act, key, 0)[:, 0:384].rearrange("p (h d) -> p h d", d=DD)))
                elif kind == "dX":
                    l, what, t = key[1:]
                    dst = dkT[:, :, t * P:(t + 1) * P] if what == "k" else dqT[t // TT][:, :, (t % TT) * P:(t % TT + 1) * P]
                    free(move(dst, full(act, key, 0)[:, :].rearrange("p (h q) -> p h q", q=P)))
                elif kind == "dv" and key[2] % 2 == 0:
                    free(move(dv[:, key[2]], full(act, key, 0)[:, 0:384]))
                elif kind == "nS":
                    l, h = key[1:]
                    act.wait_ge(na_negmax, l * NH + h + 1)
                    for n in range(NQB):
                        nc.scalar.activation(nprob[:, n, 0:256], nprob[:, n, 0:256], ACT.Exp, bias=n_neg[:, n:n + 1],
                                             accum_out=n_s[:, 0, n:n + 1])
                        free(nc.scalar.activation(nprob[:, n, 256:512], bank(key, n)[:, 256:512], ACT.Exp,
                                                  bias=n_neg[:, n:n + 1], accum_out=n_s[:, 1, n:n + 1]))
                elif kind == "nT":
                    l, h = key[1:]
                    if h:
                        read_by_pe(act, ("nPV", l, h - 1))
                    else:
                        act.wait_ge(nv_saved, 16 * (l + 1))
                    for n in (0, 2):
                        free(move(nprobT[:, n], full(act, key, n)[:, :].rearrange("p (k q) -> p k q", q=P)))
                elif kind == "cS":
                    l, h = key[1:]
                    if h >= 2:
                        read_by_pe(act, ("cT", l, h - 2))
                    elif h == 0:
                        read_by_pe(act, ("nPV", l, NH - 1))
                    act.wait_ge(ctx_negmax, h + 1)
                    for t in range(CT):
                        ins_ = nc.scalar.activation(cprob[:, h % 2, t], bank(key, 0)[:, t * NMEM:(t + 1) * NMEM], ACT.Exp,
                                                    bias=c_neg[:, h % 2, t:t + 1], accum_out=c_s[:, h % 2, t:t + 1])
                    free(ins_)
                elif kind == "cT":
                    l, h = key[1:]
                    if h >= 2:
                        read_by_pe(act, ("cPV", l, h - 2))
                    free(move(cprobT[:, h % 2].rearrange("p k (t q) -> p t k q", t=CT),
                              full(act, key, 0)[:, :].rearrange("p (t k q) -> p t k q", t=CT, k=CT)))
                elif kind == "dS":
                    l, t, h = key[1:]
                    n = diff_at(l, t, h)
                    if (t, h) == (0, 0):
                        read_by_pe(act, ("dF", l, "q", 2))
                    elif n >= 3:
                        read_by_pe(act, diff_step("dT", n - 3))
                    for i in range(njobs[key]):
                        half, part, k0, w = score_part(t, i)
                        act.wait_ge(diff_negmax, 2 * n + half + 1)
                        free(nc.scalar.activation(dprob[n % 3][:, half, k0:k0 + w], bank(key, i)[:, 0:w], ACT.Exp,
                                                  bias=d_neg[:, n % 4, half:half + 1], scale=diff_scale,
                                                  accum_out=d_s[:, n % 4, 2 * part + half:2 * part + half + 1]))
                elif kind == "dT":
                    l, t, h = key[1:]
                    n = diff_at(l, t, h)
                    if n >= 2:
                        read_by_pe(act, diff_step("dPV", n - 2))
                    for i in range(njobs[key]):
                        k0, w = (0, 4) if t < TT and i == 0 else (TT, 2)
                        free(move(dwT[:, n % 2, k0:k0 + w], full(act, key, i)[:, 0:w * P].rearrange("p (k q) -> p k q", q=P)))
                elif kind == "dPV":
                    l, t, h = key[1:]
                    n = diff_at(l, t, h)
                    free(move(otok[t // TT][:, t % TT, h * DV:(h + 1) * DV], full(act, key, 0)[:, 0:DV], d_rec[:, n % 4, 0:1]))
                elif kind == "cvZ":
                    l, st = key[1:]
                    n = (T, NMEM)[st]
                    for f in range(CF):
                        c = 2 * l + f
                        free(nc.scalar.activation(csilu[st][:, f], full(act, key, f)[:, 0:n], ACT.Silu,
                                                  bias=vec[:, V_LB + c:V_LB + c + 1], scale=vec[:, V_LG + c:V_LG + c + 1]))
                elif kind == "yo":
                    l, t = key[1:]
                    n = yo_at(l, t)
                    if n >= 2:
                        act.wait_ge(y_rstd, n - 1)
                    for i in range(2):
                        b = full(act, key, i)
                        if n:
                            act.wait_ge(y_sq, 2 * n - 2 + i + 1)
                        yjunk = cxn[:, t] if t < TT else cxcn[:, t - TT]
                        nc.scalar.activation(yjunk[:, i * BANK:(i + 1) * BANK], b[:, :], ACT.Square,
                                             accum_out=y_ss[:, n % 2, i:i + 1]).then_inc(y_sq, 1)
                    if l == 0:
                        act.wait_ge(x_new, n + 1)
                        square("C1" if t < TT else "c1", t % TT)

        @block.vector
        def _(dve):
            count = {"chain": 0}
            taps = {"lat": 0, "ctx": 0}

            def chained(ins_):
                count["chain"] += 1
                ins_.then_inc(dve_chain, 1)
                dve.wait_ge(dve_chain, count["chain"])

            def free(ins_):
                return ins_.then_inc(evac["v"], 1)

            def mul(out, a, b):
                return nc.vector.tensor_tensor(out, a, b, ALU.mult)

            def scaled(out, a, s):
                return nc.vector.tensor_scalar(out, a, s, None, ALU.mult)

            def norm_scale(ph, t):
                src, dst, _, _, rs = norms[ph]
                dve.wait_ge(rstd_ready, norm_no[ph, t])
                scaled(dst[:, t], src[:, t], rs[:, t:t + 1]).then_inc(xn_ready, 1)

            def conv_taps(l, st, n):
                name = ("lat", "ctx")[st]
                total = CF * TAPS
                src, dst, width = ((u, y, T), (uc, yc, NMEM))[st]
                for _ in range(n):
                    if taps[name] == total:
                        return
                    tap, f = divmod(taps[name], CF)
                    if tap == 0:
                        if st == 1:
                            read_by_pe(dve, ("dF", 0, "q", 2))
                        evacuated(dve, ("cv", l, f), 2 * st + 1)
                    w = conv_w[:, f, l * TAPS + tap:l * TAPS + tap + 1]
                    cut = src[:, f, tap:tap + width]
                    if tap == 0:
                        c = V_CB + 2 * l + f
                        ins_ = nc.vector.tensor_scalar(dst[:, f], cut, w, vec[:, c:c + 1], ALU.mult, ALU.add)
                    else:
                        ins_ = nc.vector.scalar_tensor_tensor(dst[:, f], cut, w, dst[:, f], ALU.mult, ALU.add)
                    taps[name] += 1
                    if taps[name] == total:
                        ins_.then_inc(conv_done, 1)
                    else:
                        chained(ins_)

            def o_normalise(l, t):
                dve.wait_ge(o_rstd, diff_tile(l, t) + 1)
                v = otok[t // TT][:, t % TT].rearrange("p (h d) -> p h d", d=DV)
                mul(v, v, o_rs[:, t].unsqueeze(2).to_broadcast([P, DH, DV])).then_inc(o_normed, 1)

            def diff_combine(n):
                l, t, h = all_diff[n]
                evacuated(dve, ("dS", l, t, h))
                rec, s = d_rec[:, n % 4], d_s[:, n % 4]
                if t < TT:
                    chained(nc.vector.tensor_tensor(s[:, 2:4], s[:, 0:2], s[:, 2:4], ALU.add))
                chained(nc.vector.reciprocal(rec[:, 0:2], s[:, 2:4]))
                chained(nc.vector.scalar_tensor_tensor(rec[:, 2:3], s[:, 2:3], lam[:, l:l + 1], rec[:, 1:2], ALU.mult, ALU.mult))
                k0 = 0 if t < TT else T
                p1, p2 = dprob[n % 3][:, 0, k0:], dprob[n % 3][:, 1, k0:]
                nc.vector.scalar_tensor_tensor(p1, p2, rec[:, 2:3], p1, ALU.mult, ALU.add).then_inc(diff_w, 1)

            for key, _ in steps:
                kind = key[0]
                if kind == "vecT" and key[1] == 0:
                    free(nc.vector.tensor_copy(vec[:, 0:V_EARLY], full(dve, key, 0)[:, 0:V_EARLY]))
                    evacuated(dve, key)
                    for t in range(CT):
                        norm_scale("m", t)
                elif kind == "vecT":
                    free(nc.vector.tensor_copy(vec[:, V_EARLY:], full(dve, key, 0)[:, 0:V_ROWS - V_EARLY + 2 * CW_ROWS]))
                    evacuated(dve, key)
                    for l in range(2):
                        chained(scaled(subw[:, l], vec[:, V_SUB + 3 * l:V_SUB + 3 * l + 3], 1.0 - lam_init[l]))
                    dve.wait_ge(lam_in, 64)
                    dve.wait_ge(rpb_saved, 96)
                    for l in range(2):
                        for q in range(2):
                            ins_ = nc.vector.tensor_tensor_reduce(
                                out=lam_junk, in0=lam_v[:, l, 2 * q], in1=lam_v[:, l, 2 * q + 1], scale=1.0,
                                scalar=0.0, op0=ALU.mult, op1=ALU.add, accum_out=lam_st[:, l, q:q + 1])
                            if (l, q) != (1, 1):
                                chained(ins_)
                    ins_.then_inc(lam_dots, 1)
                    dve.wait_ge(lam_exps, 1)
                    for l in range(2):
                        chained(nc.vector.tensor_tensor(lam[:, l:l + 1], lam_st[:, l, 1:2], lam_st[:, l, 0:1], ALU.subtract))
                        chained(nc.vector.tensor_scalar(lam[:, l:l + 1], lam[:, l:l + 1], lam_init[l], None, ALU.subtract))
                elif kind == "mod":
                    l, j = key[1:]
                    cut = modrow[:, j * MODC:(j + 1) * MODC]
                    dve.wait_ge(bmod_in, 16 * (l + 1))
                    free(nc.vector.tensor_tensor(cut, full(dve, key, 0)[0:2, 0:MODC], cut, ALU.add))
                elif kind == "modv":
                    j = key[1]
                    n = chunk_at["mod", 0, j]
                    w = slot(n)
                    dve.wait_ge(w_full[n % WSLOTS], loaded(n))
                    if j:
                        read_by_pe(dve, ("mod", 0, j - 1))
                    for k in range(KT):
                        for c in range(2):
                            if k == 0:
                                ins_ = scaled(modacc[:, c], w[:, k], siluc[:, k, c:c + 1])
                            else:
                                ins_ = nc.vector.scalar_tensor_tensor(modacc[:, c], w[:, k], siluc[:, k, c:c + 1],
                                                                      modacc[:, c], ALU.mult, ALU.add)
                        if k < KT - 1:
                            chained(ins_)
                    ins_.then_inc(mod_sums, 1)
                elif kind == "memkv" and key[1] == 0:
                    for t in range(TT):
                        norm_scale("A", t)
                elif kind == "modT":
                    l = key[1]
                    b = full(dve, key, 0)[:, 0:6 * KT].rearrange("p (s k c) -> p s k c", s=3, c=2)
                    per_feature = lambda r: vec[:, r + l * KT:r + (l + 1) * KT].unsqueeze(2).to_broadcast([P, KT, 2])
                    nc.vector.scalar_tensor_tensor(modv[:, l, 0], b[:, 1], 1.0, per_feature(V_GPRE), ALU.add, ALU.mult)
                    if l == 1:
                        dve.wait_ge(gate_saved, 32)
                    mul(gatev.rearrange("p c k -> p k c"), b[:, 2], per_feature(V_GPOST)).then_inc(gate_row, 1)
                    free(nc.vector.tensor_copy(modv[:, l, 1], b[:, 0]))
                elif kind == "memT":
                    for i in (1, 3):
                        b = full(dve, key, i)
                        c = V_MEM + 2 * i
                        scaled(memT[:, 2 * i], b[:, 0:NMEM], vec[:, c:c + 1])
                        free(scaled(memT[:, 2 * i + 1], b[:, NMEM:], vec[:, c + 1:c + 2]))
                elif kind == "wide":
                    for q in (1, 3):
                        _, w, hi, rest = wide_parts(*key[1:], q)
                        dve.wait_ge(wide_hi, wide_hi_count(*key[1:], q))
                        nc.vector.scalar_tensor_tensor(rest, w, 1.0, hi.bitcast(F32), ALU.mult,
                                                       ALU.subtract).then_inc(wide_lo_odd, 1)
                elif kind == "outs":
                    name, l, st, rows = key[1:]
                    hi, lo = out_parts[st]
                    for k in rows:
                        dve.wait_ge(out_hi, out_count(name, l, st, k))
                        nc.vector.scalar_tensor_tensor(lo[:, k], out_rows[st][:, k], 1.0, hi[:, k].bitcast(F32), ALU.mult,
                                                       ALU.subtract).then_inc(out_lo, 1)
                elif key == ("Aw", 1):
                    for i in (1, 2):
                        _, w, hi, rest = av_parts(i)
                        dve.wait_ge(av_rounded, i + 1)
                        nc.vector.scalar_tensor_tensor(rest, w, 1.0, hi.bitcast(F32), ALU.mult,
                                                       ALU.subtract).then_inc(av_rest1, 1)
                elif kind == "hT" and key[1] in "AB":
                    if key[1] == "B":
                        dve.wait_ge(x0_saved, 16 * TT)
                    for k in range(KT):
                        c = V_NORM + KT * (key[1] == "B") + k
                        dve.wait_ge(hi_ready, hi_at(key, k))
                        free(nc.vector.scalar_tensor_tensor(hT_lo[:, k], bank(key, k)[:, :], vec[:, c:c + 1],
                                                            hT_hi[:, k].bitcast(F32), ALU.mult, ALU.subtract))
                elif kind in ("hT", "hcT"):
                    l, c, hi, lo, n = ((int(key[1][1]), 0, hT_hi, hT_lo2, T) if kind == "hT" else
                                       (key[1], 1, hcT_hi, hcT_lo, NMEM))
                    if l == 1:
                        dve.wait_ge(x_new, TT + CT if kind == "hT" else CT + 1)
                    for k in range(KT):
                        i, c0 = divmod(k * n, T)
                        v = fullx[:, k % 2, 0:n]
                        if c0 == 0:
                            dve.wait_ge(hi_ready, hi_at(key, (i + 1) * T // n - 1))
                        chained(nc.vector.tensor_scalar(v, bank(key, i)[:, c0:c0 + n], modv[:, l, 0, k, c:c + 1],
                                                        modv[:, l, 1, k, c:c + 1], ALU.mult, ALU.add))
                        ins_ = nc.vector.scalar_tensor_tensor(lo[:, k], v, 1.0, hi[:, k].bitcast(F32), ALU.mult, ALU.subtract)
                        if c0 + n == T:
                            free(ins_)
                elif kind == "Av":
                    for i in range(1, 8, 2):
                        half, t = divmod(i, TT)
                        free(nc.vector.tensor_copy(gv[:, t, half * 384:half * 384 + 384], full(dve, key, i)[:, 0:384]))
                elif kind == "Aproj":
                    h = key[1]
                    b = h % 2
                    t1, t2, t3, t4 = (gt[:, b, i] for i in range(4))
                    free(nc.vector.tensor_copy(gk[:, h], full(dve, key, 1)[0:GK, :]))
                    if h == 0:
                        dve.wait_ge(gla_in, 64)
                    if h >= 2:
                        dve.wait_ge(gla_keys, 2 * (h - 1))
                    dve.wait_ge(gla_abs, h + 1)
                    free(nc.vector.tensor_scalar(t2, full(dve, key, 2)[0:GK, :], bgate[:, h:h + 1], 0.0, ALU.add, ALU.min))
                    evacuated(dve, key, 2)
                    dve.wait_ge(gla_soft, h + 1)
                    chained(nc.vector.tensor_tensor(t2, t2, t1, ALU.subtract))
                    chained(nc.vector.tensor_tensor_scan(t3, greset, t2, 0.0, ALU.mult, ALU.add))
                    by_chunk = lambda v: v.rearrange("p (n c) -> p n c", c=GCHUNK)
                    last = by_chunk(t3)[:, :, GCHUNK - 1:GCHUNK].to_broadcast([GK, T // GCHUNK, GCHUNK])
                    nc.vector.tensor_tensor(by_chunk(t4), last, by_chunk(t3), ALU.subtract).then_inc(gla_cum, 1)
                    dve.wait_ge(gla_exps, 3 * h + 3)
                    nc.vector.tensor_copy(gdec[:, h], by_chunk(t1)[:, :, GCHUNK - 1])
                    evacuated(dve, key, 0)
                    mul(gq[:, h], gq[:, h], t1).then_inc(gla_qin, 1)
                elif kind == "AA":
                    h = key[1]
                    if h == 0:
                        dve.wait_ge(gla_zero, 6)
                    if h >= 2:
                        read_by_pe(dve, ("Ao", h - 2))
                    free(nc.vector.copy_predicated(gA[:, h % 2], gmask.unsqueeze(1).to_broadcast([P, TT, P]),
                                                   full(dve, key, 0)[:, :].rearrange("p (t q) -> p t q", q=P)))
                elif kind == "AdS":
                    h = key[1]
                    if h:
                        read_by_pe(dve, ("Ao", h - 1))
                    for n in range(T // GCHUNK - 1):
                        i, j = DS_BANK[n]
                        b = full(dve, key, i)[0:GK, j * GV:(j + 1) * GV]
                        if n == 0:
                            ins_ = nc.vector.tensor_copy(gS[:, 1], b)
                        else:
                            ins_ = nc.vector.scalar_tensor_tensor(gS[:, n + 1], gS[:, n], gdec[:, h, n:n + 1], b,
                                                                  ALU.mult, ALU.add)
                        if n in DS_LAST:
                            free(ins_)
                            evacuated(dve, key, i)
                        else:
                            chained(ins_)
                elif kind == "qm":
                    free(nc.vector.tensor_copy(qmem[key[1]][:, 1], full(dve, key, 1)[:, :]))
                elif kind == "mS":
                    ph = "AB".index(key[1])

                    def mem_normalise(i):
                        evacuated(dve, key, i)
                        chained(nc.vector.reciprocal(m_rec[:, ph, i], m_sum[:, ph, i]))
                        mul(mprob[:, i], mprob[:, i],
                            m_rec[:, ph, i].unsqueeze(2).to_broadcast([P, 2, NMEM])).then_inc(mem_probs, 1)

                    for i in range(8):
                        b = full(dve, key, i)
                        chained(nc.vector.reduce_max(m_max[:, ph, i], b[:, :].rearrange("p (h m) -> p h m", h=2), AX_X))
                        scaled(m_neg[:, ph, i], m_max[:, ph, i], -mem_scale).then_inc(mem_negmax, 1)
                        if i:
                            mem_normalise(i - 1)
                    mem_normalise(7)
                elif kind == "mT":
                    for i in range(1, 8, 2):
                        free(nc.vector.tensor_copy(mprobT[:, i % 2::2, :, (i // 2) * P:(i // 2 + 1) * P],
                                                   full(dve, key, i)[:, :].rearrange("p (h k q) -> p h k q", h=2, k=CT)))
                elif kind == "mPV":
                    for j in range(2):
                        evacuated(dve, ("gate", key[1], 6 + j))
                        free(mul(branch[:, 6 + j], full(dve, key, j)[:, :], branch[:, 6 + j]))
                elif kind == "AoT":
                    for f in range(6):
                        evacuated(dve, ("gate", "A", f))
                        free(nc.vector.scalar_tensor_tensor(branch[:, f], full(dve, key, f)[:, :],
                                                            vec[:, V_GLA + f % 3:V_GLA + f % 3 + 1], branch[:, f],
                                                            ALU.mult, ALU.mult))
                elif kind == "wout":
                    ph = key[1]
                    if ph == "A":
                        dve.wait_ge(x_in, 32)
                    if ph == "B":
                        dve.wait_ge(x0_back, 16)
                    if ph == "B":
                        read_by_pe(dve, ("BPV", BH - 1))
                        dve.wait_ge(dil_out, BH)
                        nc.vector.memset(dstage[:, :, :, DD:], 0.0)
                        for t in range(CT):
                            norm_scale("c0", t)
                        dve.wait_ge(fw_in, 16)
                    for t in range(TT):
                        for n in range(2):
                            cut = x[:, t, n * BANK:(n + 1) * BANK]
                            free(nc.vector.tensor_tensor(cut, full(dve, key, 2 * t + n)[:, :], cut, ALU.add))
                        if ph == "B":
                            dve.wait_ge(rstd_ready, norm_no["F", t])
                            nc.vector.scalar_tensor_tensor(x[:, t], x[:, t], norms["F"][4][:, t:t + 1], fw,
                                                           ALU.mult, ALU.mult).then_inc(x_final, 1)
                            norm_scale("C0", t)
                    if ph == "A":
                        for t in range(TT):
                            norm_scale("B", t)
                elif kind == "Bproj":
                    h, g = key[1:]
                    if h >= 2:
                        read_by_pe(dve, ("BS", h - 2))
                    if (h, g) == (0, 0):
                        dve.wait_ge(rope_in, 16)
                    b, dst = full(dve, key, 2), bvT[:, h % 2, g]
                    if g == 0:
                        free(nc.vector.tensor_copy(dst, b[:, :]))
                    else:
                        free(nc.vector.tensor_copy(dst.rearrange("p (b i) -> p b i", b=DIL),
                                                   b[:, :].rearrange("p (i b) -> p b i", b=DIL)))
                    evacuated(dve, key, 1)
                    rot = bqk[0:32, h % 2, g]
                    tab = lambda c: dil_rope[:, 2 * (g > 0) + c].unsqueeze(1).to_broadcast([32, 2, T])
                    chained(nc.vector.stream_shuffle(bswap, rot, [(i + 16) % 32 for i in range(32)]))
                    chained(mul(bswap, bswap, tab(1)))
                    chained(mul(rot, rot, tab(0)))
                    nc.vector.tensor_tensor(rot, rot, bswap, ALU.add).then_inc(rope_done, 1)
                    dve.wait_ge(rope_done, BG * h + g + 1)
                elif kind == "BS":
                    h = key[1]
                    p = h % 2
                    if h == 0:
                        dve.wait_ge(const_in, 48)
                    else:
                        read_by_pe(dve, ("BT", h - 1))
                    if h >= 2:
                        dve.wait_ge(st_saved, 48 * (h - 1))
                    for g in range(BG):
                        for n in range(TT):
                            i, lo, m_lo = dil_tile(g, n)
                            v = bprob_tile(g, n)
                            w = v.shape[1]
                            ins_ = nc.vector.tensor_tensor_reduce(
                                out=v, in0=full(dve, key, i)[:, lo:lo + w], in1=dil_mask[:, m_lo:m_lo + w],
                                scale=dil_scale, scalar=-3e38, op0=ALU.add, op1=ALU.max,
                                accum_out=b_stat[:, p, g, int(g > 0), 0, n:n + 1])
                            if n == 3 or (g == 0 and n == 1):
                                free(ins_)
                    evacuated(dve, key, 6)
                    scaled(b_neg[:, p, 0], b_stat[:, p, 0, 0, 0], -1.0)
                    scaled(b_neg[:, p, 1:3], b_stat[:, p, 1:3, 1, 0], -1.0).then_inc(dil_negmax, 1)
                elif kind == "Bw":
                    h = key[1]
                    p = h % 2
                    dve.wait_ge(dil_probs, h + 1)
                    dve.wait_ge(st_in, 48 * (h + 1))
                    top, bot = b_stat[:, p, :, :, 0], b_stat[:, p, :, :, 1]
                    chained(nc.vector.tensor_tensor(b_top, top[:, 0], top[:, 1], ALU.max))
                    chained(nc.vector.tensor_tensor(b_top, b_top, top[:, 2], ALU.max))
                    nc.vector.tensor_tensor(b_w, top, b_top.unsqueeze(1).to_broadcast([P, BG, 2, TT]),
                                            ALU.subtract).then_inc(dil_diff, 1)
                    dve.wait_ge(dil_exp, h + 1)
                    chained(mul(bot, bot, b_w))
                    chained(nc.vector.tensor_tensor(b_rec, bot[:, 0], bot[:, 1], ALU.add))
                    chained(nc.vector.tensor_tensor(b_rec, b_rec, bot[:, 2], ALU.add))
                    chained(nc.vector.reciprocal(b_rec, b_rec))
                    chained(mul(b_w, b_w, b_rec.unsqueeze(1).to_broadcast([P, BG, 2, TT])))
                    scaled(bprob[:, P:2 * P], bprob[:, P:2 * P], b_w[:, 0, 0, 0:1])
                    v = bprob[:, 2 * P:8 * P].rearrange("p (n k) -> p n k", n=3)
                    mul(v, v, b_w[:, 0, 0, 1:4].unsqueeze(2).to_broadcast([P, 3, 2 * P]))
                    v = bprob[:, 8 * P:].rearrange("p (g n k) -> p g n k", g=2, n=TT)
                    mul(v, v, b_w[:, 1:3, 1].unsqueeze(3).to_broadcast([P, 2, TT, P])).then_inc(dil_weighted, 1)
                elif kind == "BT":
                    h = key[1]
                    if h:
                        read_by_pe(dve, ("BPV", h - 1))
                    for i in (1, 3):
                        n0, n = PT_BANKS[i]
                        free(nc.vector.tensor_copy(bprobT[:, n0:n0 + n],
                                                   full(dve, key, i)[:, 0:n * P].rearrange("p (n q) -> p n q", q=P)))
                elif kind == "BPV":
                    h = key[1]
                    evacuated(dve, key, 1)
                    if h:
                        dve.wait_ge(dil_out, h)
                    free(nc.vector.tensor_tensor(bsum, full(dve, key, 0)[:, :], bo12, ALU.add))
                    evacuated(dve, key, 0)
                    evacuated(dve, ("gate", "B", h))
                    mul(branch[:, h], branch[:, h], bsum).then_inc(dil_out, 1)
                elif kind == "gate" and key[1][0] == "C":
                    if key[2] >= 6:
                        conv_taps(int(key[1][1]), 0, 7)
                elif kind == "nkc":
                    taps.update(lat=0, ctx=0)
                    if key[1] == 0:
                        read_by_pe(dve, ("wout", "B"))
                        for pad in (u[:, :, 0:HALO], u[:, :, HALO + T:], uc[:, :, 0:HALO], uc[:, :, HALO + NMEM:]):
                            nc.vector.memset(pad, 0.0)
                    for j in range(3):
                        free(nc.vector.tensor_copy(nkcT[:, j], full(dve, key, j)[:, 0:NMEM]))
                elif kind == "nvF":
                    dve.wait_ge(x_saved, 16 * (key[1] + 1))
                    for j in range(3):
                        free(nc.vector.tensor_copy(nvF[1][:, j], full(dve, key, 2 * j + 1)[:, 0:NMEM]))
                elif kind == "dF":
                    l, what, g = key[1:]
                    if what == "q":
                        read_by_pe(dve, ("dv", l, TT + CT - 1))
                    if njobs[key] == 2:
                        free(nc.vector.tensor_copy(dF[what][1][:, g], full(dve, key, 1)[:, 0:NMEM]))
                    if what != "q":
                        conv_taps(l, 0, 8)
                elif kind == "nv":
                    for t in range(CT):
                        free(nc.vector.tensor_copy(vctx[:, t], full(dve, key, TT + t)[:, 0:NH * ND]))
                elif kind == "nq" and key[1] == 0:
                    for j in range(3):
                        free(scaled(nqcT[:, j], full(dve, key, 2 * j + 1)[:, 0:NMEM], ND ** -0.5))
                elif kind == "cv":
                    f = key[2]
                    for st in range(njobs[key] // 2):
                        n, dst = ((T, u), (NMEM, uc))[st]
                        evacuated(dve, key, 2 * st)
                        free(mul(dst[:, f, HALO:HALO + n], full(dve, key, 2 * st + 1)[:, 0:n], csig[:, f, 0:n]))
                elif kind == "dP":
                    l, what, t = key[1:]
                    if t < TT:
                        n = stage_at(key)
                        if n >= 2:
                            read_by_pe(dve, stage_key(n - 2))
                        b = full(dve, key, 0)[:, 0:384]
                        st = dstage[:, n % 2, :, 0:DD]
                        cos = diff_rope[:, 0, t].unsqueeze(1).to_broadcast([P, 2 * DH, DD])
                        chained(mul(st, b.rearrange("p (h d) -> p h d", d=DD), cos))
                        pairs = b.rearrange("p (h a r d) -> p h a r d", h=2 * DH, a=2, r=2)
                        swap = dswap.rearrange("p h (a r d) -> p h a r d", a=2, r=2)
                        sin = diff_rope[:, 1, t].rearrange("p (a r d) -> p a r d", a=2, r=2)
                        for r in range(2):
                            ins_ = mul(swap[:, :, :, r], pairs[:, :, :, 1 - r],
                                       sin[:, :, r].unsqueeze(1).to_broadcast([P, 2 * DH, 2, DD // 4]))
                        free(ins_)
                        evacuated(dve, key)
                        nc.vector.tensor_tensor(st, st, dswap, ALU.add).then_inc(diff_staged, 1)
                        dve.wait_ge(diff_staged, roped_at(key) + 1)
                elif kind == "dv":
                    if key[2] % 2:
                        free(nc.vector.tensor_copy(dv[:, key[2]], full(dve, key, 0)[:, 0:384]))
                elif kind == "nS":
                    l, h = key[1:]
                    dve.wait_ge(bias_ready, l * NH + h + 1)
                    if h:
                        read_by_pe(dve, ("nT", l, h - 1))
                    else:
                        dve.wait_ge(x_saved, 16 * (l + 1))
                    for n in range(NQB):
                        b = full(dve, key, n)
                        chained(nc.vector.reduce_max(n_ctx[:, n:n + 1], b[:, 256:512], AX_X))
                        ins_ = nc.vector.tensor_tensor_reduce(
                            out=nprob[:, n, 0:256], in0=b[:, 0:256], in1=bias[:, h % 2, BIAS_KIND[n]], scale=1.0,
                            scalar=n_ctx[:, n:n + 1], op0=ALU.add, op1=ALU.max, accum_out=n_max[:, n:n + 1])
                    chained(ins_)
                    scaled(n_neg, n_max, -1.0).then_inc(na_negmax, 1)
                elif kind == "nW":
                    l, h = key[1:]
                    evacuated(dve, ("nS", l, h))
                    chained(nc.vector.tensor_tensor(n_rec[:, 0], n_s[:, 0], n_s[:, 1], ALU.add))
                    chained(nc.vector.reciprocal(n_rec[:, 1], n_rec[:, 0]))
                    for n in range(NQB):
                        ins_ = scaled(nprob[:, n], nprob[:, n], n_rec[:, 1, n:n + 1])
                    ins_.then_inc(na_probs, 1)
                elif kind == "nT":
                    l, h = key[1:]
                    if h:
                        read_by_pe(dve, ("nPV", l, h - 1))
                    else:
                        dve.wait_ge(nv_saved, 16 * (l + 1))
                    for n in (1, 3):
                        free(nc.vector.tensor_copy(nprobT[:, n], full(dve, key, n)[:, :].rearrange("p (k q) -> p k q", q=P)))
                elif kind == "nPV":
                    l, h = key[1:]
                    lo = 64 * (h % 2)
                    evacuated(dve, ("gate", f"C{l}", h // 2), 0)
                    v = branch[lo:lo + 64, h // 2].rearrange("p (r n c) -> p n r c", r=GRID_H, n=NQB)
                    b = full(dve, key, 0)[lo:lo + 64, :].rearrange("p (n r c) -> p n r c", n=NQB, r=GRID_H)
                    free(mul(v, b, v))
                elif kind == "cS":
                    l, h = key[1:]
                    b = full(dve, key, 0)
                    if h >= 2:
                        evacuated(dve, ("cS", l, h - 2))
                    chained(nc.vector.reduce_max(c_max[:, h % 2], b[:, :].rearrange("p (t k) -> p t k", t=CT), AX_X))
                    scaled(c_neg[:, h % 2], c_max[:, h % 2], -1.0).then_inc(ctx_negmax, 1)
                elif kind == "cW":
                    l, h = key[1:]
                    evacuated(dve, ("cS", l, h))
                    chained(nc.vector.reciprocal(c_rec[:, h % 2], c_s[:, h % 2]))
                    v = cprob[:, h % 2]
                    mul(v, v, c_rec[:, h % 2].unsqueeze(2).to_broadcast([P, CT, NMEM])).then_inc(ctx_probs, 1)
                elif kind == "cPV":
                    l, h = key[1:]
                    lo = 64 * (h % 2)
                    evacuated(dve, ("gate", f"C{l}", h // 2), 1)
                    v = cbranch[lo:lo + 64, h // 2]
                    free(mul(v, full(dve, key, 0)[lo:lo + 64, 0:NMEM], v))
                elif kind == "dS":
                    l, t, h = key[1:]
                    n = diff_at(l, t, h)
                    p = n % 4
                    top = d_max[:, p]
                    if n >= 4 and (t, h) != (0, 0):
                        evacuated(dve, diff_step("dPV", n - 4))
                    for i in range(njobs[key]):
                        half, part, _, w = score_part(t, i)
                        c = 2 * part + half
                        ins_ = nc.vector.reduce_max(top[:, c:c + 1], full(dve, key, i)[:, 0:w], AX_X)
                        if part == 1:
                            chained(ins_)
                            if t < TT:
                                chained(nc.vector.tensor_tensor(top[:, c:c + 1], top[:, half:half + 1], top[:, c:c + 1], ALU.max))
                            scaled(d_neg[:, p, half:half + 1], top[:, c:c + 1], -diff_scale).then_inc(diff_negmax, 1)
                    if (t, h) != (0, 0):
                        diff_combine(n - 1)
                    if l == 0:
                        conv_taps(0, 1, 4)
                elif kind == "dT":
                    l, t, h = key[1:]
                    n = diff_at(l, t, h)
                    p = n % 2
                    if (t, h) == diff_items(l)[-2]:
                        diff_combine(n + 1)
                elif kind == "dPV":
                    l, t, h = key[1:]
                    if h == DH - 1:
                        n = diff_tile(l, t)
                        o = otok[t // TT][:, t % TT]
                        evacuated(dve, key)
                        sq = dswap.rearrange("p h d -> p (h d)")
                        chained(mul(sq, o, o))
                        nc.vector.tensor_reduce(o_ss[:, t], sq.rearrange("p (h d) -> p h d", d=DV), AX_X,
                                                ALU.add).then_inc(o_sq, 1)
                    elif h == 0 and t:
                        o_normalise(l, t - 1)
                elif kind == "last":
                    l = key[1]
                    o_normalise(l, TT + CT - 1 if l == 0 else TT - 1)
                elif kind == "doT":
                    l, st = key[1:]
                    n, dst = ((T, branch), (NMEM, cbranch))[st]
                    for f in range(3):
                        evacuated(dve, ("gate", f"C{l}", 3 + f), st)
                        free(nc.vector.scalar_tensor_tensor(dst[:, 3 + f], full(dve, key, f)[:, 0:n], subw[:, l, f:f + 1],
                                                            dst[:, 3 + f], ALU.mult, ALU.mult))
                elif kind == "cvT":
                    l, st = key[1:]
                    conv_taps(l, st, CF * TAPS)
                    pairs = range((TT, CT)[st] // 2)
                    for i in pairs:
                        b = full(dve, key, i)
                        for j in range(2):
                            chained(nc.vector.bn_stats(ln_st, b[:, j * CW:(j + 1) * CW]))
                            ins_ = nc.vector.bn_aggr(ln_mv[:, i, j], ln_st)
                            if j == 0:
                                chained(ins_)
                        ins_.then_inc(ln_var, 1)
                        if i + 1 in pairs:
                            dve.wait_ge(ln_var, ln_pair(l, st, i) + 1)
                    for i in pairs:
                        b = bank(key, i)
                        dve.wait_ge(ln_rstd, ln_pair(l, st, i) + 1)
                        for j in range(2):
                            ins_ = nc.vector.tensor_scalar(czn[st][:, 2 * i + j], b[:, j * CW:(j + 1) * CW],
                                                           ln_mv[:, i, j, 0:1], ln_rs[:, i, j:j + 1], ALU.subtract, ALU.mult)
                        free(ins_)
                elif kind == "cvZ":
                    l, st = key[1:]
                    dst = (branch, cbranch)[st]
                    for f in range(CF):
                        evacuated(dve, key, f)
                        evacuated(dve, ("gate", f"C{l}", 6 + f), st)
                        mul(dst[:, 6 + f], dst[:, 6 + f], csilu[st][:, f]).then_inc(ln_done, 1)
                elif kind == "yo":
                    l, t = key[1:]
                    n = yo_at(l, t)
                    c = t // TT
                    row = x[:, t] if t < TT else xc[:, t - TT]
                    dve.wait_ge(y_rstd, n + 1)
                    dve.wait_ge(gmul_in, 32 * (l + 1))
                    if t < TT:
                        dve.wait_ge(x_back, 16 * (l + 1))
                    else:
                        dve.wait_ge(xc_back, 16)
                    if n:
                        dve.wait_ge(x_new, n)
                    if (l, t) == (0, 1):
                        evacuated(dve, ("hcT", 1))
                    for i in range(2):
                        cut = slice(i * BANK, (i + 1) * BANK)
                        free(nc.vector.scalar_tensor_tensor(ytmp[:, cut], full(dve, key, i)[:, :], y_rs[:, n % 2, 1:2],
                                                            gmul[:, c, cut], ALU.mult, ALU.mult))
                    evacuated(dve, key)
                    nc.vector.tensor_tensor(row, row, ytmp, ALU.add).then_inc(x_new, 1)
                    if l == 0:
                        norm_scale("C1" if t < TT else "c1", t % TT)

        @block.tensor
        def _(pe):
            def done(ins_):
                ins_.then_inc(psum_full, 1)

            def product(out, pairs):
                pairs = list(pairs)
                for i, (lhsT, rhs) in enumerate(pairs):
                    ins_ = nc.tensor.matmul(out, lhsT, rhs, start=i == 0, stop=i == len(pairs) - 1)
                return ins_

            def features(out, w, c0, m, rhs):
                return product(out, ((w[:, k, c0:c0 + m], rhs[:, k]) for k in range(KT)))

            def split_features(key, i, g, context):
                n = split_at[{("nk", 1): ("nkc", 1), ("nkc", 0): ("nk", 0)}.get(key, key), g]
                _, _, hi, lo = split_weights(n)
                pe.wait_ge(split_lo, n + 1)
                first = key[0] in ("Aproj", "Bproj") or key[1] in ("A", "B")
                x_hi, x_lo, width = (hcT_hi, hcT_lo, NMEM) if context else (hT_hi, hT_lo if first else hT_lo2, T)
                b = claim(pe, key, i)
                new = {("gate", "B", 0): ("hT", "B"), ("nk", 0): ("hT", "C0"), ("nk", 1): ("hT", "C1")}.get(key)
                if key[0] == "nkc" and i == 0:
                    evacuated(pe, ("hcT", key[1]), 3)
                for k in range(KT):
                    if new and i == 0:
                        evacuated(pe, new, k)
                    for p, (w, v) in enumerate(((hi, x_hi), (hi, x_lo), (lo, x_hi))):
                        ins_ = nc.tensor.matmul(b[0:hi.shape[2], 0:width], w[:, k], v[:, k], start=k + p == 0, stop=(k, p) == (KT - 1, 2))
                done(ins_)

            def split_tokens(out, name, l, t, n, first):
                st, tt = divmod(t, TT)
                hi, lo = out_parts[st]
                order = (0, 1, 2, 6, 7, 3, 4, 5) if name == "yo" else range(KT) if l == "A" else (6, 7, 0, 1, 2, 3, 4, 5)
                at_ = chunk_at[name, l, n]
                rest = wring_r[:, at_ % WSLOTS].rearrange("p (k c) -> p k c", c=WCOLS)
                for i, k in enumerate(order):
                    q = k // 2
                    room = wide_room[name, l][4 * n + q] + k % 2 * WCOLS
                    rounded = arena_r[:, room:room + WCOLS]
                    x_hi, x_lo = (v[:, k, tt * P:(tt + 1) * P] for v in (hi, lo))
                    if first:
                        pe.wait_ge(out_lo, out_count(name, l, st, k))
                        pe.wait_ge(wide_lo_odd if q % 2 else wide_lo_even, wide_lo_count(name, l, n, q))
                    for p, (v, w) in enumerate(((x_hi, rounded), (x_lo, rounded), (x_hi, rest[:, k]))):
                        ins_ = nc.tensor.matmul(out, v, w, start=i + p == 0, stop=(i, p) == (KT - 1, 2))
                return ins_

            def tokens(out, lhs, t, w, c0, n):
                return product(out, ((lhs[:, k, t * P:(t + 1) * P], w[:, k, c0:c0 + n]) for k in range(KT)))

            def turn(out, in_):
                n = in_.shape[0]
                return nc.tensor.transpose(out, in_, ident[0:n, 0:n])

            def norm_in(ph):
                pe.wait_ge(xn_ready, norm_pe[ph])

            for key, _ in steps:
                kind = key[0]
                if kind == "vecT" and key[1] == 0:
                    pe.wait_ge(vecs_in, VECS_IN)
                    done(turn(claim(pe, key, 0)[:, 0:V_EARLY], vrows))
                elif kind == "vecT":
                    pe.wait_ge(vecs2_in, VECS2_IN)
                    late = V_ROWS - V_EARLY
                    b = claim(pe, key, 0)
                    turn(b[:, 0:late], vrows2)
                    for f in range(CF):
                        ins_ = turn(b[:, late + f * CW_ROWS:late + (f + 1) * CW_ROWS], crows[:, f * P:(f + 1) * P])
                    done(ins_)
                elif kind == "mod":
                    l, j = key[1:]
                    pe.wait_ge(silu_c, 1)
                    b = claim(pe, key, 0)
                    if l == 0:
                        pe.wait_ge(mod_sums, j + 1)
                        done(product(b[0:2, 0:MODC], ((pick[:, c], modacc[:, c]) for c in range(2))))
                    else:
                        w = chunk(pe, key)
                        done(product(b[0:2, 0:MODC], ((siluc[:, k], w[:, k]) for k in range(KT))))
                elif kind == "modT":
                    l = key[1]
                    evacuated(pe, ("mod", l, MODS - 1))
                    b = claim(pe, key, 0)
                    for c in range(3 * KT):
                        ins_ = turn(b[:, 2 * c:2 * c + 2], modrow[:, c * P:(c + 1) * P])
                    done(ins_)
                elif (split_jobs(key) and kind != "Aproj") or kind in ("nk", "nkc"):
                    for i, (g, context) in enumerate(split_banks(key, njobs[key])):
                        split_features(key, i, g, context)
                elif kind == "memT":
                    norm_in("m")
                    for i in range(4):
                        b = claim(pe, key, i)
                        for j in range(2):
                            k = 2 * i + j
                            for t in range(CT):
                                ins_ = turn(b[:, j * NMEM + t * P:j * NMEM + (t + 1) * P], memn[:, t, k * P:(k + 1) * P])
                        done(ins_)
                elif kind == "memkv":
                    l = key[1]
                    w = chunk(pe, key)
                    if l == 0:
                        evacuated(pe, ("memT",), 2)
                        evacuated(pe, ("memT",), 3)
                    b = claim(pe, key, 0)
                    for j in range(2):
                        ins_ = features(b[:, j * NMEM:(j + 1) * NMEM], w, j * P, P, memT)
                    done(ins_)
                    b = claim(pe, key, 1)
                    for t in range(CT):
                        ins_ = tokens(b[:, t * 256:(t + 1) * 256], memT, t, w, 256, 256)
                    done(ins_)
                elif kind == "hT":
                    norm_in(key[1])
                    src = norms[key[1]][1]
                    for k in range(KT):
                        b = claim(pe, key, k)
                        for t in range(TT):
                            ins_ = turn(b[:, t * P:(t + 1) * P], src[:, t, k * P:(k + 1) * P])
                        done(ins_)
                elif kind == "hcT":
                    norm_in(f"c{key[1]}")
                    for i in range(4):
                        b = claim(pe, key, i)
                        for j in range(2):
                            k = 2 * i + j
                            for t in range(CT):
                                ins_ = turn(b[:, j * NMEM + t * P:j * NMEM + (t + 1) * P], cxcn[:, t, k * P:(k + 1) * P])
                        done(ins_)
                elif kind == "Av":
                    for i in range(8):
                        half, t = divmod(i, TT)
                        if t == 0:
                            pe.wait_ge(av_rest1 if half else av_rest0, 1 + half)
                        b = claim(pe, key, i)
                        for k in range(KT):
                            if i == 0:
                                evacuated(pe, ("hT", "A"), k)
                            hi, lo = av_pair(half, k)
                            x_hi, x_lo = (v[:, k, t * P:(t + 1) * P] for v in (hT_hi, hT_lo))
                            for p, (v, w) in enumerate(((x_hi, hi), (x_lo, hi), (x_hi, lo))):
                                ins_ = nc.tensor.matmul(b[:, 0:384], v, w[:, 0:384], start=k + p == 0, stop=(k, p) == (KT - 1, 2))
                        done(ins_)
                elif kind == "Aglow":
                    b = claim(pe, key, 0)
                    for k in range(KT):
                        hi, lo = (w[:, 384:384 + GRANK] for w in av_pair(1, k))
                        for p, (w, v) in enumerate(((hi, hT_hi), (hi, hT_lo), (lo, hT_hi))):
                            ins_ = nc.tensor.matmul(b[0:GRANK, :], w, v[:, k], start=k + p == 0, stop=(k, p) == (KT - 1, 2))
                    done(ins_)
                elif kind == "Aproj":
                    h = key[1]
                    for i in range(2):
                        split_features(key, i, i, 0)
                    if h == 0:
                        pe.wait_ge(gla_in, 64)
                        evacuated(pe, ("Aglow",))
                    done(product(claim(pe, key, 2)[0:GK, :], [(wgu[:, h * GK:(h + 1) * GK], glow)]))
                elif kind == "AA":
                    h = key[1]
                    pe.wait_ge(gla_qin, h + 1)
                    pe.wait_ge(gla_keys, 2 * h + 2)
                    b = claim(pe, key, 0)
                    for t in range(TT):
                        cut = slice(t * P, (t + 1) * P)
                        ins_ = product(b[:, cut], [(gkin[:, h % 2, cut], gq[:, h, cut])])
                    done(ins_)
                    b = claim(pe, key, 1)
                    for t in range(TT):
                        ins_ = turn(b[:, t * GK:(t + 1) * GK], gkout[:, h % 2, t * P:(t + 1) * P])
                    done(ins_)
                elif kind == "AdS":
                    h = key[1]
                    evacuated(pe, ("AA", h), 1)
                    if h == 0:
                        evacuated(pe, ("Av",), 6)
                        evacuated(pe, ("Av",), 7)
                    for i in range(4):
                        b = claim(pe, key, i)
                        for n in range(T // GCHUNK - 1):
                            if DS_BANK[n][0] != i:
                                continue
                            t, half = divmod(n, 2)
                            lo = half * GCHUNK
                            ins_ = product(b[0:GK, DS_BANK[n][1] * GV:(DS_BANK[n][1] + 1) * GV],
                                           [(gkot[lo:lo + GCHUNK, h % 2, t], gv[lo:lo + GCHUNK, t, h * GV:(h + 1) * GV])])
                        done(ins_)
                elif kind == "Ao":
                    h = key[1]
                    evacuated(pe, ("AA", h), 0)
                    evacuated(pe, ("AdS", h), 3)
                    for i in range(2):
                        b = claim(pe, key, i)
                        for t in (2 * i, 2 * i + 1):
                            o = b[:, (t % 2) * GV:(t % 2 + 1) * GV]
                            ins_ = nc.tensor.matmul(o, gA[:, h % 2, t], gv[:, t, h * GV:(h + 1) * GV], start=True, stop=False)
                            for half in range(2):
                                lo = half * GCHUNK
                                ins_ = nc.tensor.matmul(o[lo:lo + GCHUNK], gq[:, h, t * P + lo:t * P + lo + GCHUNK],
                                                        gS[:, 2 * t + half], start=False, stop=True)
                        done(ins_)
                elif kind == "mS":
                    ph = key[1]
                    l = "AB".index(ph)
                    evacuated(pe, ("qm", ph), 0)
                    evacuated(pe, ("qm", ph), 1)
                    for i in range(8):
                        t, odd = divmod(i, 2)
                        lo = odd * MD
                        b = claim(pe, key, i)
                        for j in range(2):
                            ins_ = product(b[:, j * NMEM:(j + 1) * NMEM], [(qmem[ph][lo:lo + MD, j, t * P:(t + 1) * P],
                                                                            memk[lo:lo + MD, l, j])])
                        done(ins_)
                elif kind == "mT":
                    ph = key[1]
                    for i in range(8):
                        pe.wait_ge(mem_probs, 8 * "AB".index(ph) + i + 1)
                        b = claim(pe, key, i)
                        for j in range(2):
                            for k in range(CT):
                                ins_ = turn(b[:, (j * CT + k) * P:(j * CT + k + 1) * P], mprob[:, i, j, k * P:(k + 1) * P])
                        done(ins_)
                elif kind == "mPV":
                    ph = key[1]
                    l = "AB".index(ph)
                    evacuated(pe, ("mT", ph), 6)
                    evacuated(pe, ("mT", ph), 7)
                    for j in range(2):
                        b = claim(pe, key, j)
                        for h in (2 * j, 2 * j + 1):
                            lo = (h % 2) * MD
                            ins_ = product(b[lo:lo + MD, :], ((memv[:, l, k, h * MD:(h + 1) * MD], mprobT[:, h, k])
                                                              for k in range(CT)))
                        done(ins_)
                elif kind == "AoT":
                    evacuated(pe, ("Ao", GH - 1))
                    for f in range(6):
                        b = claim(pe, key, f)
                        for t in range(TT):
                            ins_ = turn(b[:, t * P:(t + 1) * P], go[:, t, f * P:(f + 1) * P])
                        done(ins_)
                elif kind == "wout":
                    ph = key[1]
                    for i in range(8):
                        t, n = divmod(i, 2)
                        done(split_tokens(claim(pe, key, i)[:, :], "wout", ph, t, n, t == 0))
                elif kind == "BS":
                    h = key[1]
                    p = h % 2
                    for g in range(BG):
                        evacuated(pe, ("Bproj", h, g), 2)
                        b = claim(pe, key, g)
                        for n in range(TT):
                            ins_ = turn(b[:, n * P:(n + 1) * P], bvT[:, p, g, n * P:(n + 1) * P])
                        done(ins_)
                    pe.wait_ge(rope_done, BG * (h + 1))
                    for i in range(3, 7):
                        b = claim(pe, key, i)
                        for g in range(BG):
                            for n in range(TT):
                                at_, lo, _ = dil_tile(g, n)
                                if at_ == i:
                                    w = bprob_tile(g, n).shape[1]
                                    ins_ = product(b[:, lo:lo + w], [(bqk[:, p, g, 0, n * P:(n + 1) * P],
                                                                      bqk[:, p, g, 1, (n + 1) * P - w:(n + 1) * P])])
                        done(ins_)
                elif kind == "BT":
                    h = key[1]
                    pe.wait_ge(dil_weighted, h + 1)
                    for i, (n0, n) in enumerate(PT_BANKS):
                        b = claim(pe, key, i)
                        for j in range(n):
                            lo = PT_TILES[n0 + j] * P
                            ins_ = turn(b[:, j * P:(j + 1) * P], bprob[:, lo:lo + P])
                        done(ins_)
                elif kind == "BPV":
                    h = key[1]
                    for i in range(4):
                        evacuated(pe, ("BT", h), i)
                    evacuated(pe, ("BS", h), 2)
                    b = claim(pe, key, 0)
                    for n in range(TT):
                        pairs = [(bv[:, 0, n], bprobT[:, 2 * n])]
                        if n:
                            pairs.append((bv[:, 0, n - 1], bprobT[:, 2 * n - 1]))
                        ins_ = product(b[:, n * P:(n + 1) * P], pairs)
                    done(ins_)
                    b = claim(pe, key, 1)
                    for n in range(TT):
                        ins_ = product(b[:, n * P:(n + 1) * P], [(bv[:, 1, n], bprobT[:, 7 + n]), (bv[:, 2, n], bprobT[:, 11 + n])])
                    done(ins_)
                elif kind in ("nv", "dv", "dP"):
                    l = key[1]
                    if kind == "nv":
                        src, tiles = nvF, [(t, t) for t in range(TT + CT)]
                        evacuated(pe, ("nvF", l), 4)
                        evacuated(pe, ("nvF", l), 5)
                    else:
                        what, t = ("v", key[2]) if kind == "dv" else key[2:]
                        src, tiles = dF[what], [(0, t)]
                        for i in range(njobs["dF", l, what, 2]):
                            evacuated(pe, ("dF", l, what, 2), i)
                    for i, t in tiles:
                        b = claim(pe, key, i)
                        rows, tt = (src[0], t) if t < TT else (src[1], t - TT)
                        for g in range(3):
                            ins_ = turn(b[:, g * P:(g + 1) * P], rows[:, g, tt * P:(tt + 1) * P])
                        done(ins_)
                elif kind == "dX":
                    l, what, t = key[1:]
                    key_p = ("dP", l, what, t)
                    if t < TT:
                        pe.wait_ge(diff_staged, roped_at(key_p) + 1)
                    else:
                        evacuated(pe, key_p)
                    b = claim(pe, key, 0)
                    n = stage_at(key_p)
                    for h in range(DH):
                        ins_ = turn(b[:, h * P:(h + 1) * P], dstage[:, n % 2, 2 * h:2 * h + 2].rearrange("p s d -> p (s d)"))
                    done(ins_)
                elif kind == "nS":
                    l, h = key[1:]
                    lo, j = 64 * (h % 2), h // 2
                    if h == 0:
                        evacuated(pe, ("nk", l))
                        evacuated(pe, ("nkc", l))
                        evacuated(pe, ("nq", l), 4 if l == 0 else 2)
                    k = nkT[lo:lo + ND, j].rearrange("p (r c) -> p r c", c=GRID_W)
                    for n in range(NQB):
                        b = claim(pe, key, n)
                        qn = nqT[lo:lo + ND, j, n * P:(n + 1) * P]
                        product(b[:, 0:256], [(qn, k[:, :, STRIP_START[n]:STRIP_START[n] + STRIP])])
                        done(product(b[:, 256:512], [(qn, nkcT[lo:lo + ND, j])]))
                elif kind == "nT":
                    l, h = key[1:]
                    pe.wait_ge(na_probs, l * NH + h + 1)
                    for n in range(NQB):
                        b = claim(pe, key, n)
                        for k in range(4):
                            ins_ = turn(b[:, k * P:(k + 1) * P], nprob[:, n, k * P:(k + 1) * P])
                        done(ins_)
                elif kind == "nPV":
                    l, h = key[1:]
                    lo = 64 * (h % 2)
                    if h == 0:
                        pe.wait_ge(strips_in, 16 * 4 * NQB * (l + 1))
                        evacuated(pe, ("nv", l), 5)
                    evacuated(pe, ("nT", l, h), 2)
                    evacuated(pe, ("nT", l, h), 3)
                    b = claim(pe, key, 0)
                    cut = slice(h * ND, (h + 1) * ND)
                    for n in range(NQB):
                        v = [vstrip[:, n, 0, cut], vstrip[:, n, 1, cut], vctx[:, 0, cut], vctx[:, 1, cut]]
                        ins_ = product(b[lo:lo + ND, n * P:(n + 1) * P], ((v[k], nprobT[:, n, k]) for k in range(4)))
                    done(ins_)
                elif kind == "cS":
                    l, h = key[1:]
                    lo, j = 64 * (h % 2), h // 2
                    if h == 0:
                        evacuated(pe, ("nq", l), 5)
                    b = claim(pe, key, 0)
                    for t in range(CT):
                        ins_ = product(b[:, t * NMEM:(t + 1) * NMEM], [(nqcT[lo:lo + ND, j, t * P:(t + 1) * P],
                                                                        nkcT[lo:lo + ND, j])])
                    done(ins_)
                elif kind == "cT":
                    l, h = key[1:]
                    pe.wait_ge(ctx_probs, h + 1)
                    b = claim(pe, key, 0)
                    for t in range(CT):
                        for k in range(CT):
                            ins_ = turn(b[:, (t * CT + k) * P:(t * CT + k + 1) * P], cprob[:, h % 2, t, k * P:(k + 1) * P])
                    done(ins_)
                elif kind == "cPV":
                    l, h = key[1:]
                    lo = 64 * (h % 2)
                    evacuated(pe, ("cT", l, h))
                    b = claim(pe, key, 0)
                    done(product(b[lo:lo + ND, 0:NMEM], ((vctx[:, k, h * ND:(h + 1) * ND], cprobT[:, h % 2, k]) for k in range(CT))))
                elif kind == "dS":
                    l, t, h = key[1:]
                    evacuated(pe, ("dX", l, "q", t))
                    if (t, h) == (0, 0):
                        evacuated(pe, ("dX", l, "k", TT + CT - 1))
                    for i in range(njobs[key]):
                        b = claim(pe, key, i)
                        half, _, k0, w = score_part(t, i)
                        lo = half * DPAD
                        q = dqT[t // TT][lo:lo + DD, h, (t % TT) * P:(t % TT + 1) * P]
                        done(product(b[:, 0:w], [(q, dkT[lo:lo + DD, h, k0:k0 + w])]))
                elif kind == "dT":
                    l, t, h = key[1:]
                    n = diff_at(l, t, h)
                    pe.wait_ge(diff_w, n + 1)
                    k0 = 0 if t < TT else TT
                    for i in range(njobs[key]):
                        b = claim(pe, key, i)
                        w = 4 if (t < TT and i == 0) else 2
                        for j in range(w):
                            k = k0 + 4 * i + j
                            ins_ = turn(b[:, j * P:(j + 1) * P], dprob[n % 3][:, 0, k * P:(k + 1) * P])
                        done(ins_)
                elif kind == "dPV":
                    l, t, h = key[1:]
                    n = diff_at(l, t, h)
                    if (t, h) == (0, 0):
                        evacuated(pe, ("dv", l, TT + CT - 2))
                        evacuated(pe, ("dv", l, TT + CT - 1))
                    for i in range(njobs[("dT", l, t, h)]):
                        evacuated(pe, ("dT", l, t, h), i)
                    b = claim(pe, key, 0)
                    tiles = range(TT + CT) if t < TT else range(TT, TT + CT)
                    done(product(b[:, 0:DV], ((dwT[:, n % 2, k], dv[:, k, h * DV:(h + 1) * DV]) for k in tiles)))
                elif kind == "doT":
                    l, st = key[1:]
                    nt = (TT, CT)[st]
                    pe.wait_ge(o_normed, diff_tile(l, (TT if st == 0 else TT + CT) - 1) + 1)
                    for f in range(3):
                        b = claim(pe, key, f)
                        for t in range(nt):
                            ins_ = turn(b[:, t * P:(t + 1) * P], otok[st][:, t, f * P:(f + 1) * P])
                        done(ins_)
                elif kind == "cvT":
                    l, st = key[1:]
                    pe.wait_ge(conv_done, 1 + st if l == 0 else 3)
                    src = (y, yc)[st]
                    for i in range((TT, CT)[st] // 2):
                        b = claim(pe, key, i)
                        for j in range(2):
                            t = 2 * i + j
                            for f in range(CF):
                                ins_ = turn(b[:, j * CW + f * P:j * CW + (f + 1) * P], src[:, f, t * P:(t + 1) * P])
                        done(ins_)
                elif kind == "cvZ":
                    l, st = key[1:]
                    nt = (TT, CT)[st]
                    evacuated(pe, ("cvT", l, st))
                    for f in range(CF):
                        b = claim(pe, key, f)
                        for t in range(nt):
                            ins_ = turn(b[:, t * P:(t + 1) * P], czn[st][:, t, f * P:(f + 1) * P])
                        done(ins_)
                elif kind == "yo":
                    l, t = key[1:]
                    for n in range(2):
                        done(split_tokens(claim(pe, key, n)[:, :], "yo", l, t, n, t % TT == 0))


_INS = ['x', 'mem', 'mem_norm_w', 'norm_w', 'w_memkv', 'w_out', 'w_in_a', 'w_gate_up', 'b_gate', 'gla_norm_w', 'w_in_b',
        'final_norm_w', 'c_2', 'ctx_2', 'c_ctx_2', 'w_mod_2', 'b_mod_2', 'g_pre_2', 'g_post_2', 'w_in_2', 'w_out_2',
        'na_rpb_2', 'diff_lq1_2', 'diff_lk1_2', 'diff_lq2_2', 'diff_lk2_2', 'diff_subln_g_2', 'conv_w_2', 'conv_b_2',
        'conv_ln_g_2', 'conv_ln_b_2']


def kernel(**inputs):
    import concourse.bacc as bacc
    from concourse.bass_utils import run_bass_kernel_spmd

    nc = bacc.Bacc("TRN2", target_bir_lowering=False, num_devices=1)
    arrays, ins, consts = {}, {}, {}
    for name in _INS:
        a = np.ascontiguousarray(inputs[name])
        arrays[f"in_{name}"] = a
        ins[name] = nc.dram_tensor(f"in_{name}", a.shape, mybir.dt.from_np(a.dtype), kind="ExternalInput").ap()
    for name, a in constants().items():
        arrays[f"const_{name}"] = a
        consts[name] = nc.dram_tensor(f"const_{name}", a.shape, mybir.dt.from_np(a.dtype), kind="ExternalInput").ap()
    out = nc.dram_tensor("out", (1, T, D), F32, kind="ExternalOutput").ap()
    hybrid_stack_kernel(nc, ins, consts, out)
    r = run_bass_kernel_spmd(nc, [arrays], core_ids=[0])
    return r.results[0]["out"]
```
